# Optimizing a Trainium2 kernel written in Bass

```python
import jax, jax.numpy as jnp
from jax import lax
import numpy as np
import math

D_MODEL = 1024
BATCH = 1
SEQ = 512
DEPTH = 1

CHUNK = 64
N_LEFT_CHUNKS = 8
BAND = (N_LEFT_CHUNKS + 1) * CHUNK
D_MIX = D_MODEL
D_ATTN = D_MIX // 2
HEAD_DIM = 64
N_HEADS = D_ATTN // HEAD_DIM
D_POOL = D_MIX - D_ATTN
POOL_WINDOWS = (2, 4, 8, 16)
N_POOL_GROUPS = len(POOL_WINDOWS)
POOL_GROUP_DIM = D_POOL // N_POOL_GROUPS
REL_CLIP = 128
N_REL = 2 * REL_CLIP + 1
D_FF = 2816
D_IN = 3 * D_ATTN + D_POOL
EPS = 1e-6
NEG_INF = -1e30


def rmsnorm(x, g):
    xf = x.astype(jnp.float32)
    y = xf * lax.rsqrt(jnp.mean(xf * xf, axis=-1, keepdims=True) + EPS)
    return (y * g.astype(jnp.float32)).astype(x.dtype)

def swiglu_ffn(x, w_gate, w_up, w_down):
    return (jax.nn.silu(x @ w_gate) * (x @ w_up)) @ w_down

def multiscale_pool(u, pool_w, pool_scale):
    B, S, _ = u.shape
    uf = u.astype(jnp.float32)
    cs = jnp.cumsum(uf, axis=1)
    cs = jnp.concatenate([jnp.zeros_like(cs[:, :1]), cs], axis=1)
    t = jnp.arange(S)
    outs = []
    for g, w in enumerate(POOL_WINDOWS):
        lo, hi = g * POOL_GROUP_DIM, (g + 1) * POOL_GROUP_DIM
        c = cs[:, :, lo:hi]
        start = jnp.maximum(t + 1 - w, 0)
        win_sum = c[:, 1:] - c[:, start]
        count = (t + 1 - start).astype(jnp.float32)
        outs.append(win_sum / count[None, :, None] - uf[:, :, lo:hi])
    d = jnp.stack(outs, axis=2)
    y = jnp.einsum('bsgc,gcd->bsgd', d, pool_w.astype(jnp.float32)).reshape(B, S, D_POOL)
    return (y * pool_scale.astype(jnp.float32)).astype(u.dtype)

def chunked_attention(q, k, v, q_gain, k_gain, rel_bias):
    B, S, _ = q.shape
    nc = S // CHUNK
    q = rmsnorm(q.reshape(B, S, N_HEADS, HEAD_DIM), q_gain)
    k = rmsnorm(k.reshape(B, S, N_HEADS, HEAD_DIM), k_gain)
    v = v.reshape(B, S, N_HEADS, HEAD_DIM)
    pad = N_LEFT_CHUNKS * CHUNK
    kp = jnp.pad(k, ((0, 0), (pad, 0), (0, 0), (0, 0)))
    vp = jnp.pad(v, ((0, 0), (pad, 0), (0, 0), (0, 0)))
    qc = q.reshape(B, nc, CHUNK, N_HEADS, HEAD_DIM)
    qpos = jnp.arange(CHUNK)[:, None] + pad
    kpos = jnp.arange(BAND)[None, :]
    rel_idx = jnp.clip(qpos - kpos, -REL_CLIP, REL_CLIP) + REL_CLIP
    bias = rel_bias.astype(jnp.float32)[:, rel_idx]
    scale = HEAD_DIM ** -0.5

    def one_chunk(c):
        qb = lax.dynamic_index_in_dim(qc, c, axis=1, keepdims=False)
        kb = lax.dynamic_slice_in_dim(kp, c * CHUNK, BAND, axis=1)
        vb = lax.dynamic_slice_in_dim(vp, c * CHUNK, BAND, axis=1)
        s = jnp.einsum('bqhd,bkhd->bhqk', qb, kb).astype(jnp.float32) * scale + bias
        valid = (c * CHUNK + kpos - pad) >= 0
        s = jnp.where(valid[None, None], s, NEG_INF)
        p = jax.nn.softmax(s, axis=-1)
        return jnp.einsum('bhqk,bkhd->bqhd', p.astype(vb.dtype), vb)

    o = lax.map(one_chunk, jnp.arange(nc))
    return o.transpose(1, 0, 2, 3, 4).reshape(B, S, D_ATTN)

def hybrid_mixer(h, w_in, q_gain, k_gain, rel_bias, pool_w, pool_scale, w_out):
    proj = h @ w_in
    q = proj[..., :D_ATTN]
    k = proj[..., D_ATTN:2 * D_ATTN]
    v = proj[..., 2 * D_ATTN:3 * D_ATTN]
    u = proj[..., 3 * D_ATTN:]
    a = chunked_attention(q, k, v, q_gain, k_gain, rel_bias)
    p = multiscale_pool(u, pool_w, pool_scale)
    return jnp.concatenate([a, p], axis=-1) @ w_out

def first_inputs(seed: int = 0) -> dict:
    key = jax.random.key(seed)
    ks = jax.random.split(key, 20)
    f32 = jnp.float32
    L = DEPTH

    def nrm(k, shape, fan_in):
        return jax.random.normal(k, shape, f32) * fan_in ** -0.5

    def gain(k, shape):
        return 1.0 + 0.1 * jax.random.normal(k, shape, f32)

    return {
        "x": jax.random.normal(ks[0], (BATCH, SEQ, D_MODEL), f32),
        "ffn1_norm": gain(ks[1], (L, D_MODEL)),
        "ffn1_w_gate": nrm(ks[2], (L, D_MODEL, D_FF), D_MODEL),
        "ffn1_w_up": nrm(ks[3], (L, D_MODEL, D_FF), D_MODEL),
        "ffn1_w_down": nrm(ks[4], (L, D_FF, D_MODEL), D_FF),
        "mix_norm": gain(ks[5], (L, D_MODEL)),
        "w_in": nrm(ks[6], (L, D_MODEL, D_IN), D_MODEL),
        "q_norm": gain(ks[7], (L, HEAD_DIM)),
        "k_norm": gain(ks[8], (L, HEAD_DIM)),
        "rel_bias": 0.5 * jax.random.normal(ks[9], (L, N_HEADS, N_REL), f32),
        "pool_w": nrm(ks[10], (L, N_POOL_GROUPS, POOL_GROUP_DIM, POOL_GROUP_DIM), POOL_GROUP_DIM),
        "pool_scale": gain(ks[11], (L, D_POOL)),
        "w_out": nrm(ks[12], (L, D_MIX, D_MODEL), D_MIX),
        "ffn2_norm": gain(ks[13], (L, D_MODEL)),
        "ffn2_w_gate": nrm(ks[14], (L, D_MODEL, D_FF), D_MODEL),
        "ffn2_w_up": nrm(ks[15], (L, D_MODEL, D_FF), D_MODEL),
        "ffn2_w_down": nrm(ks[16], (L, D_FF, D_MODEL), D_FF),
        "final_norm": gain(ks[17], (L, D_MODEL)),
    }

def first_block(x, ffn1_norm, ffn1_w_gate, ffn1_w_up, ffn1_w_down, mix_norm, w_in,
              q_norm, k_norm, rel_bias, pool_w, pool_scale, w_out,
              ffn2_norm, ffn2_w_gate, ffn2_w_up, ffn2_w_down, final_norm):
    for l in range(DEPTH):
        x = x + 0.5 * swiglu_ffn(rmsnorm(x, ffn1_norm[l]), ffn1_w_gate[l], ffn1_w_up[l], ffn1_w_down[l])
        x = x + hybrid_mixer(rmsnorm(x, mix_norm[l]), w_in[l], q_norm[l], k_norm[l], rel_bias[l],
                             pool_w[l], pool_scale[l], w_out[l])
        x = x + 0.5 * swiglu_ffn(rmsnorm(x, ffn2_norm[l]), ffn2_w_gate[l], ffn2_w_up[l], ffn2_w_down[l])
        x = rmsnorm(x, final_norm[l])
    return x


N_DIFF_HEADS = 4
DIFF_HEAD_DIM = 64
DIFF_V_DIM = 2 * DIFF_HEAD_DIM
DIFF_WIDTH = N_DIFF_HEADS * DIFF_V_DIM
N_MLSTM_HEADS = 4
MLSTM_QK_DIM = 64
MLSTM_V_DIM = 128
MLSTM_WIDTH = N_MLSTM_HEADS * MLSTM_V_DIM
MIX_WIDTH = DIFF_WIDTH + MLSTM_WIDTH
CONV_WIDTH = 4
Q_BLOCK = 128
D_FF_2 = 4 * D_MODEL
ROPE_THETA = 10000.0

IN_SIZES = (
    N_DIFF_HEADS * 2 * DIFF_HEAD_DIM,
    N_DIFF_HEADS * 2 * DIFF_HEAD_DIM,
    DIFF_WIDTH,
    N_MLSTM_HEADS * MLSTM_QK_DIM,
    N_MLSTM_HEADS * MLSTM_QK_DIM,
    MLSTM_WIDTH,
    MLSTM_WIDTH,
    N_MLSTM_HEADS,
    N_MLSTM_HEADS,
)
IN_WIDTH = sum(IN_SIZES)
IN_OFFSETS = tuple(int(o) for o in np.cumsum(IN_SIZES)[:-1])
CONV_CH = 2 * N_MLSTM_HEADS * MLSTM_QK_DIM


def lambda_init(layer):
    return 0.8 - 0.6 * math.exp(-0.3 * layer)

def rmsnorm_2(x, g):
    xf = x.astype(jnp.float32)
    y = xf * lax.rsqrt(jnp.mean(xf * xf, axis=-1, keepdims=True) + EPS)
    return (y * g.astype(jnp.float32)).astype(x.dtype)

def rope(x, pos):
    d = x.shape[-1]
    inv = ROPE_THETA ** (-jnp.arange(0, d, 2, dtype=jnp.float32) / d)
    ang = pos.astype(jnp.float32)[:, None] * inv[None, :]
    cos = jnp.cos(ang)[None, :, None, :]
    sin = jnp.sin(ang)[None, :, None, :]
    xf = x.astype(jnp.float32)
    x1, x2 = xf[..., : d // 2], xf[..., d // 2:]
    out = jnp.concatenate([x1 * cos - x2 * sin, x2 * cos + x1 * sin], axis=-1)
    return out.astype(x.dtype)

def diff_attention(q, k, v, lam):
    S = q.shape[3]
    scale = DIFF_HEAD_DIM ** -0.5
    outs = []
    for blk in range(S // Q_BLOCK):
        lo, hi = blk * Q_BLOCK, (blk + 1) * Q_BLOCK
        qb = q[:, :, :, lo:hi]
        kb = k[:, :, :, :hi]
        s = jnp.einsum('bhcqd,bhckd->bhcqk', qb, kb).astype(jnp.float32) * scale
        mask = (lo + jnp.arange(Q_BLOCK))[:, None] >= jnp.arange(hi)[None, :]
        s = jnp.where(mask, s, -jnp.inf)
        p = jax.nn.softmax(s, axis=-1)
        p_diff = p[:, :, 0] - lam * p[:, :, 1]
        outs.append(jnp.einsum('bhqk,bhkv->bhqv', p_diff.astype(v.dtype), v[:, :, :hi]))
    return jnp.concatenate(outs, axis=2)

def mlstm_chunkwise(q, k, v, i_pre, logf):
    B, H, S, dqk = q.shape
    dv = v.shape[-1]
    nc = S // CHUNK
    q = q * (dqk ** -0.5)

    def chunked(t):
        t = t.reshape(t.shape[:2] + (nc, CHUNK) + t.shape[3:])
        return jnp.moveaxis(t, 2, 0)

    xs = (chunked(q), chunked(k), chunked(v), chunked(i_pre), chunked(logf))
    causal = jnp.tril(jnp.ones((CHUNK, CHUNK), dtype=bool))

    def step(carry, inp):
        C, n, m = carry
        qc, kc, vc, ic, fc = inp
        b = jnp.cumsum(fc, axis=-1)
        g = b[..., -1]
        logD = b[..., :, None] - b[..., None, :] + ic[..., None, :]
        logD = jnp.where(causal, logD, -jnp.inf)
        inter = b + m[..., None]
        m_comb = jnp.maximum(inter, jnp.max(logD, axis=-1))
        scores = jnp.einsum('bhjd,bhsd->bhjs', qc, kc) * jnp.exp(logD - m_comb[..., None])
        w_inter = jnp.exp(inter - m_comb)
        num = (w_inter[..., None] * jnp.einsum('bhjd,bhdv->bhjv', qc, C)
               + jnp.einsum('bhjs,bhsv->bhjv', scores, vc))
        den = w_inter * jnp.einsum('bhjd,bhd->bhj', qc, n) + jnp.sum(scores, axis=-1)
        h = num / jnp.maximum(jnp.abs(den), jnp.exp(-m_comb))[..., None]
        log_w = g[..., None] - b + ic
        m_new = jnp.maximum(g + m, jnp.max(log_w, axis=-1))
        decay = jnp.exp(g + m - m_new)
        w = jnp.exp(log_w - m_new[..., None])
        C_new = decay[..., None, None] * C + jnp.einsum('bhs,bhsd,bhsv->bhdv', w, kc, vc)
        n_new = decay[..., None] * n + jnp.einsum('bhs,bhsd->bhd', w, kc)
        return (C_new, n_new, m_new), h

    init = (jnp.zeros((B, H, dqk, dv), jnp.float32),
            jnp.zeros((B, H, dqk), jnp.float32),
            jnp.zeros((B, H), jnp.float32))
    _, hs = lax.scan(step, init, xs)
    return jnp.moveaxis(hs, 0, 2).reshape(B, H, S, dv)

def causal_dwconv(x, w, b):
    S = x.shape[1]
    xp = jnp.pad(x, ((0, 0), (CONV_WIDTH - 1, 0), (0, 0)))
    y = b
    for j in range(CONV_WIDTH):
        y = y + w[j] * xp[:, j:j + S]
    return y

def second_inputs(seed: int = 0) -> dict:
    key = jax.random.key(seed)
    ks = jax.random.split(key, 20)
    f32 = jnp.float32
    nrm = lambda k, shape, s: jax.random.normal(k, shape, f32) * s
    gain = lambda k, shape: 1.0 + 0.05 * jax.random.normal(k, shape, f32)
    return {
        "x": jax.random.normal(ks[0], (BATCH, SEQ, D_MODEL), f32),
        "norm_mix_pre": gain(ks[1], (DEPTH, D_MODEL)),
        "w_in": nrm(ks[2], (DEPTH, D_MODEL, IN_WIDTH), D_MODEL ** -0.5),
        "conv_w": nrm(ks[3], (DEPTH, CONV_WIDTH, CONV_CH), CONV_WIDTH ** -0.5),
        "conv_b": nrm(ks[4], (DEPTH, CONV_CH), 0.01),
        "b_igate": nrm(ks[5], (DEPTH, N_MLSTM_HEADS), 0.1),
        "b_fgate": 3.0 + nrm(ks[6], (DEPTH, N_MLSTM_HEADS), 0.5),
        "lambda_q1": nrm(ks[7], (DEPTH, DIFF_HEAD_DIM), 0.1),
        "lambda_k1": nrm(ks[8], (DEPTH, DIFF_HEAD_DIM), 0.1),
        "lambda_q2": nrm(ks[9], (DEPTH, DIFF_HEAD_DIM), 0.1),
        "lambda_k2": nrm(ks[10], (DEPTH, DIFF_HEAD_DIM), 0.1),
        "diff_norm": gain(ks[11], (DEPTH, DIFF_V_DIM)),
        "mlstm_norm": gain(ks[12], (DEPTH, N_MLSTM_HEADS, MLSTM_V_DIM)),
        "w_out": nrm(ks[13], (DEPTH, MIX_WIDTH, D_MODEL), MIX_WIDTH ** -0.5),
        "norm_mix_post": gain(ks[14], (DEPTH, D_MODEL)),
        "norm_mlp_pre": gain(ks[15], (DEPTH, D_MODEL)),
        "w_up": nrm(ks[16], (DEPTH, D_MODEL, D_FF_2), D_MODEL ** -0.5),
        "w_down": nrm(ks[17], (DEPTH, D_FF_2, D_MODEL), D_FF_2 ** -0.5),
        "norm_mlp_post": gain(ks[18], (DEPTH, D_MODEL)),
    }

def second_block(x, norm_mix_pre, w_in, conv_w, conv_b, b_igate, b_fgate,
              lambda_q1, lambda_k1, lambda_q2, lambda_k2, diff_norm, mlstm_norm,
              w_out, norm_mix_post, norm_mlp_pre, w_up, w_down, norm_mlp_post):
    B, S, _ = x.shape
    pos = jnp.arange(S, dtype=jnp.int32)
    for l in range(DEPTH):
        lam_init = lambda_init(l)
        h = rmsnorm_2(x, norm_mix_pre[l])
        proj = h @ w_in[l]
        dq, dk, dvv, mq, mk, mv, mo, mi, mf = jnp.split(proj, IN_OFFSETS, axis=-1)

        dq = rope(dq.reshape(B, S, 2 * N_DIFF_HEADS, DIFF_HEAD_DIM), pos)
        dk = rope(dk.reshape(B, S, 2 * N_DIFF_HEADS, DIFF_HEAD_DIM), pos)
        dq = dq.reshape(B, S, N_DIFF_HEADS, 2, DIFF_HEAD_DIM).transpose(0, 2, 3, 1, 4)
        dk = dk.reshape(B, S, N_DIFF_HEADS, 2, DIFF_HEAD_DIM).transpose(0, 2, 3, 1, 4)
        dvv = dvv.reshape(B, S, N_DIFF_HEADS, DIFF_V_DIM).transpose(0, 2, 1, 3)
        lam = (jnp.exp(jnp.sum(lambda_q1[l].astype(jnp.float32) * lambda_k1[l].astype(jnp.float32)))
               - jnp.exp(jnp.sum(lambda_q2[l].astype(jnp.float32) * lambda_k2[l].astype(jnp.float32)))
               + lam_init)
        o_diff = diff_attention(dq, dk, dvv, lam)
        o_diff = rmsnorm_2(o_diff, diff_norm[l]) * (1.0 - lam_init)
        o_diff = o_diff.transpose(0, 2, 1, 3).reshape(B, S, DIFF_WIDTH)

        qk = causal_dwconv(jnp.concatenate([mq, mk], axis=-1), conv_w[l], conv_b[l])
        qk = jax.nn.silu(qk)
        mq, mk = qk[..., :CONV_CH // 2], qk[..., CONV_CH // 2:]
        to_heads = lambda t, d: t.reshape(B, S, N_MLSTM_HEADS, d).transpose(0, 2, 1, 3).astype(jnp.float32)
        i_pre = (mi + b_igate[l]).astype(jnp.float32).transpose(0, 2, 1)
        logf = jax.nn.log_sigmoid((mf + b_fgate[l]).astype(jnp.float32)).transpose(0, 2, 1)
        hm = mlstm_chunkwise(to_heads(mq, MLSTM_QK_DIM), to_heads(mk, MLSTM_QK_DIM),
                             to_heads(mv, MLSTM_V_DIM), i_pre, logf)
        hm = rmsnorm_2(hm.transpose(0, 2, 1, 3), mlstm_norm[l]).astype(x.dtype)
        o_mlstm = hm.reshape(B, S, MLSTM_WIDTH) * jax.nn.sigmoid(mo)

        mixed = jnp.concatenate([o_diff.astype(x.dtype), o_mlstm], axis=-1) @ w_out[l]
        x = x + rmsnorm_2(mixed, norm_mix_post[l])

        h = rmsnorm_2(x, norm_mlp_pre[l])
        u = jnp.square(jax.nn.relu(h @ w_up[l]))
        x = x + rmsnorm_2(u @ w_down[l], norm_mlp_post[l])
    return x


def setup_inputs(seed=0):
    out = dict(first_inputs(seed))
    for name, value in second_inputs(seed + 1).items():
        if name != "x":
            out[name + "_2"] = value
    return out


def reference(
    x, ffn1_norm, ffn1_w_gate, ffn1_w_up, ffn1_w_down, mix_norm, w_in, q_norm, k_norm, rel_bias,
    pool_w, pool_scale, w_out, ffn2_norm, ffn2_w_gate, ffn2_w_up, ffn2_w_down, final_norm,
    norm_mix_pre_2, w_in_2, conv_w_2, conv_b_2, b_igate_2, b_fgate_2, lambda_q1_2, lambda_k1_2,
    lambda_q2_2, lambda_k2_2, diff_norm_2, mlstm_norm_2, w_out_2, norm_mix_post_2,
    norm_mlp_pre_2, w_up_2, w_down_2, norm_mlp_post_2,
):
    x = first_block(
        x, ffn1_norm, ffn1_w_gate, ffn1_w_up, ffn1_w_down, mix_norm, w_in, q_norm, k_norm,
        rel_bias, pool_w, pool_scale, w_out, ffn2_norm, ffn2_w_gate, ffn2_w_up, ffn2_w_down,
        final_norm,
    )
    return second_block(
        x, norm_mix_pre_2, w_in_2, conv_w_2, conv_b_2, b_igate_2, b_fgate_2, lambda_q1_2,
        lambda_k1_2, lambda_q2_2, lambda_k2_2, diff_norm_2, mlstm_norm_2, w_out_2,
        norm_mix_post_2, norm_mlp_pre_2, w_up_2, w_down_2, norm_mlp_post_2,
    )


_drawn_inputs = setup_inputs


def setup_inputs(seed=0):
    import zlib

    import numpy as np

    out = dict(_drawn_inputs(seed))
    spreads = {}
    factors = {'q_norm': 4.405, 'k_norm': 4.821, 'conv_b_2': 8.0, 'b_igate_2': 8.0, 'lambda_k2_2': 6.17}
    for name, (base, spread) in spreads.items():
        noise = np.random.default_rng([zlib.crc32(name.encode()), seed]).standard_normal(out[name].shape)
        drawn = base * np.exp(spread * noise) if base else spread * noise
        out[name] = __import__('jax').numpy.asarray(drawn.astype(out[name].dtype))
    for name, factor in factors.items():
        out[name] = (out[name] * factor).astype(out[name].dtype)
    return out
```

```python
from contextlib import ExitStack

import numpy as np
import concourse.bass as bass
from concourse import mybir

ALU = mybir.AluOpType
ACT = mybir.ActivationFunctionType
F32 = mybir.dt.float32
F32R = mybir.dt.float32r

P = 128
S = 512
TT = S // P
D = 1024
DT = D // P
EPS = 1e-6
BIG = 1e30
FF = 2816
FF2 = 4096
HALF = 16
HEADS = 8
DH = 4
MH = 4
LAM_INIT = 0.2
PAD = 16
CONV = 4
SCAN_PAD = S // 2
RING = 4
BANKS = 4
AHEAD = 2

C_IDENT, C_FLIP, C_SWAP, C_HSUM, C_ONES, C_MASKT, C_CAUSAL = (128 * i for i in range(7))
C_HROW = 7 * 128
C_SEL4 = C_HROW + 1024
C_HOT = C_SEL4 + 512
C_COS = C_HOT + 16
C_SIN = C_COS + 512
C_POOL = C_SIN + 512
C_ALL = C_POOL + 64


def shape_constants():
    c = np.zeros((P, C_ALL), np.float32)
    p = np.arange(P)
    c[:, C_IDENT:C_IDENT + P] = np.eye(P)
    c[p, C_FLIP + P - 1 - p] = -1.0
    partner = np.where(p % 64 < 32, p + 32, p - 32)
    c[partner, C_SWAP + p] = 1.0
    for t in range(8):
        c[p, C_HSUM + 16 * t + 2 * t + p // 64] = 1.0
        c[2 * t + p // 64, C_HROW + P * t + p] = 1.0
    c[:, C_ONES:C_ONES + P] = 1.0
    c[:, C_MASKT:C_MASKT + P] = np.where(p[:, None] > p[None, :], -BIG, 0.0)
    c[:, C_CAUSAL:C_CAUSAL + P] = np.where(p[None, :] > p[:, None], BIG, 0.0)
    for h in range(4):
        c[h, C_SEL4 + P * h:C_SEL4 + P * (h + 1)] = 1.0
        c[32 + h, C_SEL4 + P * h:C_SEL4 + P * (h + 1)] = 1.0
        c[:, C_HOT + 4 * h + h] = 1.0
    inv = np.float32(10000.0) ** (-np.arange(0, 64, 2, dtype=np.float32) / np.float32(64))
    ang = np.arange(S, dtype=np.float32)[None, :] * inv[p % 32][:, None]
    c[:, C_COS:C_COS + S] = np.cos(ang)
    c[:, C_SIN:C_SIN + S] = np.sin(ang) * np.where(p % 64 < 32, -1.0, 1.0)[:, None]
    for g in range(4):
        w = 2 ** (g + 1)
        c[:, C_POOL + 16 * g:C_POOL + 16 * (g + 1)] = w / np.minimum(np.arange(16) + 1, w)
    return c


def numbered(sizes):
    first, n = {}, 0
    for name, size in sizes:
        first[name] = n
        n += size
    return first, n


FT = FF // P
FT2 = FF2 // P
BLK, NBLK = numbered([
    ("f1_up0", 2 * HALF), ("f1_dn0", 2 * DT), ("f1_up1", 2 * (FT - HALF)), ("f1_dn1", DT),
    ("qk", 8), ("v", 4), ("u", 4), ("poolw", 1), ("out1", 8),
    ("f2_up0", 2 * HALF), ("f2_dn0", 2 * DT), ("f2_up1", 2 * (FT - HALF)), ("f2_dn1", DT),
    ("gate", 1), ("dqk", 8), ("dv", 4), ("mqk", 4), ("mv", 4), ("mo", 4), ("out2", 8),
    ("f3_up0", HALF), ("f3_dn0", 2 * DT), ("f3_up1", HALF), ("f3_dn1", 2 * DT)])
RES, NRES = numbered([
    ("input", 8),
    ("f1_up0", 2 * HALF), ("f1_dn0", DT), ("f1_up1", 2 * (FT - HALF)), ("f1_dn1", DT),
    ("qk", 8), ("v", 4), ("u", 4), ("poolw", 4), ("out1", 8),
    ("f2_up0", 2 * HALF), ("f2_dn0", DT), ("f2_up1", 2 * (FT - HALF)), ("f2_dn1", DT),
    ("gate", 1), ("dqk", 8), ("dv", 4), ("mqk", 4), ("mv", 4), ("mo", 4), ("out2", 8),
    ("f3_up0", HALF), ("f3_dn0", DT), ("f3_up1", HALF), ("f3_dn1", DT), ("final", 8)])
HID, NHID = numbered([("f1_up0", HALF), ("f1_up1", FT - HALF), ("f2_up0", HALF), ("f2_up1", FT - HALF),
                      ("f3_up0", HALF), ("f3_up1", HALF)])
GEN, _ = numbered([("f1", 8), ("m1", 8), ("f2", 8), ("m2", 8), ("f3", 8)])
SQ, _ = numbered([("f1", 8), ("m1", 8), ("f2", 8), ("m2", 16), ("post1", 8), ("f3", 8), ("post2", 8)])
SPREAD, _ = numbered([("f1", 1), ("m1", 1), ("f2", 1), ("m2", 2), ("post1", 1), ("f3", 1), ("post2", 1)])
NORM = {n: i for i, n in enumerate(["f1", "m1", "f2", "m2", "post1", "f3", "post2"])}
GAINS = ["ffn1_norm", "mix_norm", "ffn2_norm", "final_norm", "norm_mix_pre_2", "norm_mix_post_2",
         "norm_mlp_pre_2", "norm_mlp_post_2"]


def build(nc, t):
    with ExitStack() as ctx:
        def sb(name, shape, dt=F32, stack=ctx):
            return stack.enter_context(nc.sbuf_tensor(name, shape, dt))

        def sem(name):
            return ctx.enter_context(nc.semaphore(name))

        x = sb("x", [P, DT, S])
        part = []
        over = []
        for r in range(3):
            with ExitStack() as s:
                over.append(sb(f"region{r}_f32", [P, 16, S], F32, s))
            part.append(sb(f"region{r}", [P, 16, S], F32R))
        w_raw, w_low = [], []
        for r in range(RING):
            with ExitStack() as s:
                w_raw.append(sb(f"w_raw{r}", [P, 1024], F32, s))
            w_low.append(sb(f"w_low{r}", [P, 1024], F32R))
        w_high = [sb(f"w_high{r}", [P, 1024], F32R) for r in range(RING)]
        const = sb("const", [P, C_ALL])
        gains = sb("gains", [P, len(GAINS), DT])
        ones_r = sb("ones_r", [P, P], F32R)
        rstd = sb("rstd", [P, S])
        rstd_fin = sb("rstd_fin", [P, S])
        diag = sb("diag", [P, TT, P])
        sq = sb("sq", [P, 2, S])
        sq_sum = sb("sq_sum", [P, 2, S])
        std_col = sb("std_col", [P, 2 * TT])
        r_col = sb("r_col", [P, 4 * TT])
        eps_col = sb("eps_col", [P, 1])
        qk_gain = sb("qk_gain", [P, 2])
        pool_gain = sb("pool_gain", [P, 4])
        far = sb("far", [P, HEADS])
        conv_w = sb("conv_w", [P, CONV, 4])
        conv_b = sb("conv_b", [P, 4])
        gate_b = sb("gate_b", [P, 2])
        lam_in = sb("lam_in", [P, 4])
        lam_pr = sb("lam_pr", [P, 2])
        lam_ex = sb("lam_ex", [P, 2])
        neg_lam = sb("neg_lam", [P, 1])
        diff_gain = sb("diff_gain", [P, 1])
        mlstm_gain = sb("mlstm_gain", [P, MH])
        rel_rows = sb("rel_rows", [HEADS, 384])

        with ExitStack() as s:
            ff_z = sb("ff_z", [P, 2, S], F32, s)
            ff_u = sb("ff_u", [P, 2, S], F32, s)
            ff_s = sb("ff_s", [P, 2, S], F32, s)
            ff_t = sb("ff_t", [P, 2, S], F32, s)
            y_tmp = sb("y_tmp", [P, 2, S], F32, s)
        with ExitStack() as s:
            u_pad = sb("u_pad", [P, 4, PAD + S], F32, s)
            win = sb("win", [P, 2, PAD + S], F32, s)
            head_r = sb("head_r", [2 * HEADS, S], F32, s)
            with ExitStack() as s2:
                head_sq = sb("head_sq", [P, 2, S], F32, s2)
                qk_full = sb("qk_full", [P, 2, S], F32, s2)
            with ExitStack() as s2:
                a_s = sb("a_s", [P, 2, S], F32, s2)
                a_p = sb("a_p", [P, 2, S], F32, s2)
                toep = sb("toep", [P, 2, 2, P], F32, s2)
                bias = sb("bias", [P, 2, S], F32, s2)
                a_min = sb("a_min", [P, 4 * HEADS], F32, s2)
                a_sum = sb("a_sum", [P, 4 * HEADS], F32, s2)
                a_rec = sb("a_rec", [P, 4 * HEADS], F32, s2)
        with ExitStack() as s:
            rows = sb("rows", [36, S], F32, s)
            a_col = sb("a_col", [P, TT, MH], F32, s)
            head_r2 = sb("head_r2", [MH, S], F32, s)
            sig = sb("sig", [P, MH, S], F32, s)
            with ExitStack() as s2:
                scan = sb("scan", [MH, 5, SCAN_PAD + S], F32, s2)
            with ExitStack() as s2:
                rope_y = sb("rope_y", [P, 4, S], F32, s2)
                rope_c = sb("rope_c", [P, 2, S], F32, s2)
                rope_s = sb("rope_s", [P, 2, S], F32, s2)
            with ExitStack() as s2:
                d_s = sb("d_s", [P, 2, S], F32, s2)
                d_p = sb("d_p", [P, 4, S], F32, s2)
                d_mask = sb("d_mask", [P, S], F32, s2)
                d_min = sb("d_min", [P, 32], F32, s2)
                d_sum = sb("d_sum", [P, 32], F32, s2)
                d_rec = sb("d_rec", [P, 32], F32, s2)
                d_lam = sb("d_lam", [P, 16], F32, s2)
                d_sq = sb("d_sq", [P, S], F32, s2)
                d_full = sb("d_full", [P, 2, S], F32, s2)
            with ExitStack() as s2:
                c_pad = sb("c_pad", [P, 2, 4 + S], F32, s2)
                c_acc = sb("c_acc", [P, 2, S], F32, s2)
            with ExitStack() as s2:
                m_num = sb("m_num", [P, MH, S], F32, s2)
                m_e = sb("m_e", [P, 2, S], F32, s2)
                m_dm = sb("m_dm", [P, 2, P], F32, s2)
                m_eg = sb("m_eg", [P, S], F32, s2)
                m_den = sb("m_den", [P, S], F32, s2)
                m_sq = sb("m_sq", [P, S], F32, s2)
                m_full = m_e

        x_tok = over[2][:, 0:8, :].rearrange("p a b -> p (a b)").rearrange("p (t d) -> p t d", t=TT)
        qk_raw = over[2][:, 8:16, :]
        mixed = over[2][:, 0:8, :]
        x_back = over[0][:, 0:8, :]
        out_tok = over[1][:, 0:8, :].rearrange("p a b -> p (a b)").rearrange("p (t d) -> p t d", t=TT)
        o_diff = over[0][:, 0:4, :]

        bank = [ctx.enter_context(nc.psum_tensor(f"bank{i}", [P, S], F32)) for i in range(8)]

        landed = [sem(f"landed{r}") for r in range(RING)]
        x_in, small_in, rel_in, toep_in = sem("x_in"), sem("small_in"), sem("rel_in"), [sem("toep_in0"), sem("toep_in1")]
        rel_padded, rel_stored = sem("rel_padded"), sem("rel_stored")
        consts_made, small_made = sem("consts_made"), sem("small_made")
        w_hi, w_lo, w_used = sem("w_hi"), sem("w_lo"), sem("w_used")
        acc_ready, acc_free = sem("acc_ready"), sem("acc_free")
        x_new, xt_hi, xt_lo = sem("x_new"), sem("xt_hi"), sem("xt_lo")
        sq_ready, sq_added = sem("sq_ready"), sem("sq_added")
        stat_ready, std_ready, rcol_ready, diag_ready = sem("stat_ready"), sem("std_ready"), sem("rcol_ready"), sem("diag_ready")
        bc_ready, rstd_ready = sem("bc_ready"), sem("rstd_ready")
        z_ready, s_ready, t_ready, hid_hi, hid_done = sem("z_ready"), sem("s_ready"), sem("t_ready"), sem("hid_hi"), sem("hid_done")
        ev_hi = sem("ev_hi")
        v1 = sem("dve_step")
        pool_step = sem("pool_step")
        gate_in, gain_in, lam_made, lam_summed = sem("gate_in"), sem("gain_in"), sem("lam_products_ready"), sem("lam_summed")
        x_unit, pads_zero = sem("x_unit_ready"), sem("pads_zero")

        w_dram = {n: t[n][0] for n in ("ffn1_w_gate", "ffn1_w_up", "ffn1_w_down", "w_in", "w_out",
                                       "ffn2_w_gate", "ffn2_w_up", "ffn2_w_down", "w_in_2", "w_out_2",
                                       "w_up_2", "w_down_2")}
        w_dram = {n: a.rearrange("(k p) n -> p k n", p=P) for n, a in w_dram.items()}

        CI = lambda c, n=P, rows=P: const[0:rows, c:c + n]

        def split3(pe, out, a_hi, a_lo, b_hi, b_lo, start, stop, new_block=False):
            mm = pe.matmul(out, a_hi, b_hi, start=start, stop=False)
            if new_block:
                mm.then_inc(w_used, 1)
            pe.matmul(out, a_hi, b_lo, start=False, stop=False)
            return pe.matmul(out, a_lo, b_hi, start=False, stop=stop)

        def free_bank(pe, r, it=None, step=0):
            n = r - BANKS + 1
            if it is not None:
                pe.wait_ge(acc_free, it * step + n)
            elif n > 0:
                pe.wait_ge(acc_free, n)

        def block_ready(pe, b, it=None, step=0):
            pe.wait_ge(w_lo, b + 1 if it is None else it * step + (b + 1))

        def block_parts(b, it):
            if it is None and b == BLK["poolw"]:
                return [lambda a: a[:, 0:4 * P]]
            if it is None and b == BLK["gate"]:
                return [lambda a, c=c: a[:].rearrange("p (k n) -> p k n", n=P)[:, :, c:c + MH] for c in (0, 32)]
            return [lambda a: a[:]]

        def w_tiles(b, width=P):
            hi, lo = w_high[b % RING], w_low[b % RING]
            return (hi[:].rearrange("p (k n) -> p k n", n=width), lo[:].rearrange("p (k n) -> p k n", n=width))

        def fetch(sp, b, src, it=None, step=0, width=P):
            if it is not None:
                sp.wait_ge(w_used, it * step + (b - RING + 1))
            elif b >= RING:
                sp.wait_ge(w_used, b - RING + 1)
            dst = w_raw[b % RING][:].rearrange("p (k n) -> p k n", n=width)
            nk = src.shape[1]
            sp.dma_start(dst[:, 0:nk, :], src).then_inc(landed[b % RING], 16)

        def sp_up(sp, name, mats, ht0, tiles):
            per = RING // len(mats)
            def turn(it):
                q = 0
                for j in range(per):
                    for m in mats:
                        b = BLK[name] + q
                        if it is None:
                            src = w_dram[m][:, :, (ht0 + j) * P:(ht0 + j + 1) * P]
                        else:
                            src = w_dram[m][:, :, bass.ds(it * (per * P) + (ht0 + j) * P, P)]
                        fetch(sp, b, src, it, RING)
                        q += 1
            first = 1 if BLK[name] < RING else 0
            if first:
                turn(None)
            with sp.Fori(first, tiles // per) as it:
                turn(it)

        def sp_down(sp, name, m, k0, nk):
            pieces = [(min(k, k0 + nk - 8), 8) for k in range(k0, k0 + nk, 8)]
            per = RING // len(pieces)
            with sp.Fori(0, DT // per) as it:
                q = 0
                for j in range(per):
                    for k, n in pieces:
                        fetch(sp, BLK[name] + q, w_dram[m][:, k:k + n, bass.ds(it * (per * P) + j * P, P)], it, RING)
                        q += 1

        def sp_cols(sp, name, m, tiles, col0):
            for j in range(tiles):
                fetch(sp, BLK[name] + j, w_dram[m][:, :, col0 + j * P:col0 + (j + 1) * P])

        def sp_rows(sp, name, m, col0):
            for j in range(4):
                fetch(sp, BLK[name] + j, w_dram[m][:, 2 * j:2 * j + 2, col0:col0 + S], width=S)

        out_stored, x_spilled, x_returned, y_final = sem("out_stored"), sem("x_spilled"), sem("x_returned"), sem("out_tile_ready")
        x_spill = nc.dram_tensor("x_spill", [P, DT, S], F32).ap()
        rel_pad_dram = nc.dram_tensor("rel_padded_rows", [HEADS, 384], F32).ap()

        y_sq, h_stat, h_std, h_rec, h_bc, qk_full_ready, qk_hi, qk_lo = (sem(n) for n in (
            "head_sq_ready", "head_stat_added", "head_std_ready", "head_rstd_ready", "head_bc_ready",
            "qk_full_ready", "qk_hi_ready", "qk_lo_ready"))
        b_mm, b_done = sem("bias_product"), sem("bias_ready")
        a_score, a_biased, a_exp, a_prob, a_turned, a_thi, a_tlo, a_out, a_ohi, a_olo = (sem(n) for n in (
            "scores_ready", "scores_biased", "exp_ready", "probs_ready", "probs_turned", "turned_hi",
            "turned_lo", "head_out_ready", "head_out_hi", "head_out_lo"))
        pool_done, pd_hi, pd_lo = sem("pooled"), sem("pooled_hi"), sem("pooled_lo")
        x_scaled = sem("x_scaled")
        g_abs, g_exp, g_ln, g_rows, g_turn, g_cols = (sem(n) for n in (
            "gate_abs", "gate_exp", "gate_ln", "gate_rows_ready", "gate_turned", "gate_cols_ready"))
        r_perm, r_cos = sem("rope_swapped"), sem("rope_cos_ready")
        r_full, r_hi, r_lo = sem("rope_ready"), sem("rope_hi"), sem("rope_lo")
        e_score, e_biased, e_exp, e_prob, e_turned, e_thi, e_tlo, e_out, e_sq, e_copied, e_stat, e_std, e_rec, e_bc, e_full, e_hi, e_lo = (
            sem("d_" + n) for n in ("scores_ready", "scores_masked", "exp_ready", "probs_ready", "probs_turned",
                                    "turned_hi", "turned_lo", "out_ready", "sq_ready", "out_copied", "stat_added",
                                    "std_ready", "rstd_ready", "bc_ready", "normed", "normed_hi", "normed_lo"))
        c_sum, c_act, c_hi, c_lo, mo_z, mo_sig = (sem(n) for n in (
            "conv_ready", "conv_silu", "conv_hi", "conv_lo", "gate_o_ready", "gate_o_sigmoid"))
        m_bc, m_score, m_diag, m_exp, m_prod, m_phi, m_plo, m_pv, m_egr, m_nsq, m_ncp, m_dn, m_dsq, m_sqs, m_stat, m_std, m_rec, m_bcr, m_norm, m_hi, m_lo = (
            sem("m_" + n) for n in ("rows_spread", "scores_ready", "diag_ready", "exp_ready", "weights_ready",
                                    "weights_hi", "weights_lo", "values_added", "exp_g_ready", "num_sq_ready",
                                    "num_copied", "den_ready", "den_sq_ready", "sq_sum_ready", "stat_added",
                                    "std_ready", "rstd_ready", "bc_ready", "normed", "normed_hi", "normed_lo"))

        block = ctx.enter_context(nc.Block())

        @block.sync
        def _(sp):
            sp.dma_start(x_tok, t["x"][0].rearrange("(t p) d -> p t d", p=P)).then_inc(x_in, 16)
            sp.dma_start(const[:], t["const"]).then_inc(x_in, 16)
            sp_up(sp, "f1_up0", ("ffn1_w_gate", "ffn1_w_up"), 0, HALF)
            sp_down(sp, "f1_dn0", "ffn1_w_down", 0, HALF)
            sp_up(sp, "f1_up1", ("ffn1_w_gate", "ffn1_w_up"), HALF, FT - HALF)
            sp_down(sp, "f1_dn1", "ffn1_w_down", HALF, FT - HALF)
            sp_cols(sp, "qk", "w_in", 8, 0)
            sp_rows(sp, "v", "w_in", S * 2)
            sp_cols(sp, "u", "w_in", 4, S * 3)
            fetch(sp, BLK["poolw"], t["pool_w"][0].rearrange("g c d -> c g d"))
            sp_cols(sp, "out1", "w_out", 8, 0)
            sp_up(sp, "f2_up0", ("ffn2_w_gate", "ffn2_w_up"), 0, HALF)
            sp_down(sp, "f2_dn0", "ffn2_w_down", 0, HALF)
            sp_up(sp, "f2_up1", ("ffn2_w_gate", "ffn2_w_up"), HALF, FT - HALF)
            sp_down(sp, "f2_dn1", "ffn2_w_down", HALF, FT - HALF)
            b = BLK["gate"]
            sp.wait_ge(w_used, b - RING + 1)
            gw = w_raw[b % RING][:].rearrange("p (k n) -> p k n", n=P)
            with nc.allow_non_contiguous_dma("eight columns of w_in_2"):
                sp.dma_start(gw[:, :, 0:MH], w_dram["w_in_2"][:, :, 3072:3076]).then_inc(landed[b % RING], 16)
                sp.dma_start(gw[:, :, 32:32 + MH], w_dram["w_in_2"][:, :, 3076:3080]).then_inc(gate_in, 16)
            sp_cols(sp, "dqk", "w_in_2", 8, 0)
            sp_rows(sp, "dv", "w_in_2", 1024)
            sp_cols(sp, "mqk", "w_in_2", 4, 1536)
            sp_rows(sp, "mv", "w_in_2", 2048)
            sp_cols(sp, "mo", "w_in_2", 4, 2560)
            sp_cols(sp, "out2", "w_out_2", 8, 0)
            sp_up(sp, "f3_up0", ("w_up_2",), 0, HALF)
            sp_down(sp, "f3_dn0", "w_down_2", 0, HALF)
            sp_up(sp, "f3_up1", ("w_up_2",), HALF, HALF)
            sp_down(sp, "f3_dn1", "w_down_2", HALF, HALF)
            for n in range(DT):
                sp.wait_ge(y_final, n + 1)
                sp.dma_start(t["out"][0].rearrange("(t p) d -> p t d", p=P)[:, :, n * P:(n + 1) * P],
                             out_tok[:, :, n * P:(n + 1) * P]).then_inc(out_stored, 16)
            sp.wait_ge(out_stored, 16 * DT)

        SMALL = []

        @block.scalar
        def _(act):
            def load(dst, src):
                SMALL.append(1)
                with nc.allow_non_contiguous_dma("small vectors, once"):
                    act.dma_start(dst, src).then_inc(small_in, 16)

            def column(v):
                return v.rearrange("(n p) -> p n", p=P)

            act.dma_start(rel_rows[:, 0:257], t["rel_bias"][0]).then_inc(rel_in, 16)
            with nc.allow_non_contiguous_dma("small vectors, once"):
                act.dma_start(gains[:, 0, :], column(t[GAINS[0]][0])).then_inc(gain_in, 16)
            for i, n in enumerate(GAINS[1:]):
                load(gains[:, i + 1, :], column(t[n][0]))
            for i, n in enumerate(("q_norm", "k_norm")):
                for half in range(2):
                    load(qk_gain[64 * half:64 * half + 64, i:i + 1], t[n].rearrange("a d -> d a"))
            load(pool_gain[:], column(t["pool_scale"][0]))
            load(far[:], t["rel_bias"][0][:, 256:257].rearrange("h a -> a h").broadcast_to([P, HEADS]))
            for j in range(CONV):
                load(conv_w[:, j, :], column(t["conv_w_2"][0, j]))
            load(conv_b[:], column(t["conv_b_2"][0]))
            load(gate_b[0:MH, 0:1], t["b_igate_2"].rearrange("a d -> d a"))
            load(gate_b[0:MH, 1:2], t["b_fgate_2"].rearrange("a d -> d a"))
            for i, n in enumerate(("lambda_q1_2", "lambda_k1_2", "lambda_q2_2", "lambda_k2_2")):
                load(lam_in[0:64, i:i + 1], t[n].rearrange("a d -> d a"))
            load(diff_gain[:], t["diff_norm_2"].rearrange("a d -> d a"))
            load(mlstm_gain[:], t["mlstm_norm_2"][0].rearrange("h d -> d h"))
            act.wait_ge(rel_padded, 1)
            act.dma_start(rel_pad_dram, rel_rows[:]).then_inc(rel_stored, 16)

            def split_hi(b, it=None, step=0):
                if it is None:
                    if b >= NBLK:
                        return
                    act.wait_ge(landed[b % RING], 16 * (b // RING + 1))
                    if b >= RING:
                        act.wait_ge(w_used, b - RING + 1)
                    if b == BLK["gate"]:
                        act.wait_ge(gate_in, 16)
                else:
                    act.wait_ge(landed[b % RING], it * (16 * step // RING) + 16 * (b // RING + 1))
                    act.wait_ge(w_used, it * step + (b - RING + 1))
                for piece in block_parts(b, it):
                    last = act.copy(piece(w_high[b % RING]), piece(w_raw[b % RING]))
                last.then_inc(w_hi, 1)

            def residual(sqk, n, g, dst):
                act.activation(dst[:, n, :], x[:, n, :], ACT.Identity, scale=gains[:, g, n:n + 1]).then_inc(xt_hi, 1)
                if sqk is not None:
                    square(sqk + n, x[:, n, :])

            def square(i, src, scale=1.0):
                if i >= 2:
                    act.wait_ge(sq_added, i - 1)
                act.activation(sq[:, i % 2, :], src, ACT.Square, scale=scale).then_inc(sq_ready, 1)

            def norm_std(name):
                act.wait_ge(stat_ready, NORM[name] + 1)
                act.activation(std_col[:, 0:TT], bank[4][:, 0:TT], ACT.Sqrt, scale=1.0 / D, bias=eps_col[:]).then_inc(std_ready, 1)

            def norm_copy(name, dst, extra=0):
                act.wait_ge(bc_ready, SPREAD[name] + 1 + extra)
                act.copy(dst[:], bank[5][:]).then_inc(rstd_ready, 1)

            def up(name, dst, gated, head=None):
                per = 2 if gated else 4
                tiles = FT - HALF if (gated and name.endswith("1")) else HALF
                def turn(it):
                    for j in range(per):
                        c = HID[name] + j
                        val = lambda n: n if it is None else it * per + n
                        def nxt(q):
                            b = BLK[name] + q + AHEAD
                            split_hi(b) if it is None else split_hi(b, it, RING)
                        idx = j if it is None else it * per + j
                        if gated:
                            nxt(2 * j)
                            act.wait_ge(z_ready, val(c + 1))
                            act.activation(ff_s[:, j % 2, :], ff_z[:, j % 2, :], ACT.Silu).then_inc(s_ready, 1)
                            nxt(2 * j + 1)
                            act.wait_ge(t_ready, val(c + 1))
                        else:
                            nxt(j)
                            act.wait_ge(acc_free, val(RES[name] + j + 1))
                            if c >= 2:
                                act.wait_ge(hid_done, val(c - 1))
                            act.activation(ff_t[:, j % 2, :], ff_z[:, j % 2, :], ACT.Square).then_inc(t_ready, 1)
                            act.wait_ge(t_ready, val(c + 1))
                        act.copy(dst[:, bass.ds(idx, 1), :] if it is not None else dst[:, idx, :],
                                 ff_t[:, j % 2, :]).then_inc(hid_hi, 1)
                if head is not None:
                    head()
                    turn(None)
                with act.Fori(0 if head is None else 1, tiles // per) as it:
                    turn(it)

            def down(name, blocks, each=None):
                for n in range(DT):
                    for q in range(blocks):
                        split_hi(BLK[name] + n * blocks + q + AHEAD)
                    if each is not None:
                        each(n)

            def head(name):
                def run():
                    norm_std(name)
                    norm_copy(name, rstd)
                return run

            act.wait_ge(consts_made, 2)
            act.wait_ge(x_in, 32)
            act.copy(ones_r[:], CI(C_ONES)).then_inc(ev_hi, 1)
            for b in range(AHEAD):
                split_hi(b)
            act.wait_ge(gain_in, 16)
            for n in range(DT):
                act.wait_ge(acc_free, RES["input"] + n + 1)
                residual(SQ["f1"], n, 0, part[0])
            act.wait_ge(lam_summed, 1)
            act.activation(lam_ex[:], bank[5][:, 0:2], ACT.Exp).then_inc(ev_hi, 1)

            def ffn(f, hid):
                up(f"f{f}_up0", hid, True, head(f"f{f}"))
                down(f"f{f}_dn0", 2)
                up(f"f{f}_up1", hid, True)
                def each(n):
                    act.wait_ge(acc_free, RES[f"f{f}_dn1"] + n + 1)
                    if f == 1:
                        residual(SQ["m1"], n, 1, part[0])
                    else:
                        square(SQ["m2"] + 2 * n, y_tmp[:, n % 2, :])
                        act.wait_ge(x_new, n + 1)
                        residual(None, n, 4, part[1])
                        square(SQ["m2"] + 2 * n + 1, x[:, n, :])
                down(f"f{f}_dn1", 1, each)

            ffn(1, part[1])

            for i in range(8):
                split_hi(BLK["qk"] + i + AHEAD)
                if i == 0:
                    head("m1")()
                act.wait_ge(acc_free, RES["qk"] + i + 1)
                if i >= 2:
                    act.wait_ge(h_stat, i - 1)
                act.activation(head_sq[:, i % 2, :], qk_raw[:, i, :], ACT.Square).then_inc(y_sq, 1)
            for i in range(4):
                split_hi(BLK["v"] + i + AHEAD)
            act.wait_ge(h_stat, 8)
            act.activation(head_r[:], bank[4][0:2 * HEADS, :], ACT.Sqrt, scale=1.0 / 64, bias=eps_col[0:2 * HEADS]).then_inc(h_std, 1)
            for i in range(TT):
                act.wait_ge(acc_ready, RES["v"] + i + 1)
                act.activation(part[2][:, i, :], bank[(RES["v"] + i) % BANKS][:], ACT.Identity,
                               scale=r_col[:, i:i + 1]).then_inc(ev_hi, 1)
            for i in range(4):
                split_hi(BLK["u"] + i + AHEAD)
            for i in range(8):
                act.wait_ge(qk_full_ready, i + 1)
                act.copy(part[1][:, i, :], qk_full[:, i % 2, :]).then_inc(qk_hi, 1)
            def toeplitz(h):
                if h >= 2:
                    act.wait_ge(b_mm, h - 1)
                src = rel_pad_dram[h:h + 1, 1:2].copy()
                src = bass.AP(src.tensor, src.offset, [[1, P], [128, 2], [1, P]])
                act.dma_start(toep[:, h % 2, :, :], src).then_inc(toep_in[h % 2], 16)
            act.wait_ge(rel_stored, 16)
            act.wait_ge(qk_lo, 8)
            for h in range(2):
                toeplitz(h)

            def a_expo(u):
                h, q = divmod(u, TT)
                n = (q + 1) * P
                act.wait_ge(a_biased, u + 1)
                if u >= 2:
                    act.wait_ge(a_turned, u - 1)
                act.activation(a_p[:, u % 2, 0:n], a_s[:, u % 2, 0:n], ACT.Exp, scale=-1.0,
                               bias=a_min[:, u:u + 1], accum_out=a_sum[:, u:u + 1]).then_inc(a_exp, 1)

            def turned_hi(u, ready, done, out_sem):
                h, q = divmod(u, TT)
                act.wait_ge(ready, u + 1)
                if h >= 1:
                    act.wait_ge(out_sem, h)
                act.copy(part[2][:, 8:9 + q, q * P:(q + 1) * P],
                         bank[6 + u % 2][:, 0:(q + 1) * P].rearrange("p (k n) -> p k n", n=P)).then_inc(done, 1)

            def a_head_out(h):
                r = 64 * (h % 2)
                act.wait_ge(a_out, h + 1)
                act.copy(part[0][r:r + 64, h // 2, :], bank[h % 2][r:r + 64, :]).then_inc(a_ohi, 1)

            for u in range(4 * HEADS + 4):
                if u < 4 * HEADS:
                    a_expo(u)
                    if u % TT == 3 and u // TT + 2 < HEADS:
                        toeplitz(u // TT + 2)
                if 2 <= u < 4 * HEADS + 2:
                    turned_hi(u - 2, a_turned, a_thi, a_out)
                if u >= 7 and (u - 7) % TT == 0:
                    a_head_out((u - 7) // TT)
            for g in range(4):
                act.wait_ge(pool_done, g + 1)
                act.copy(part[0][:, 4 + g, :], u_pad[:, g, PAD:]).then_inc(pd_hi, 1)
            split_hi(BLK["poolw"] + AHEAD)
            for g in range(4):
                act.wait_ge(acc_ready, RES["poolw"] + g + 1)
                act.activation(part[0][:, 4 + g, :], bank[(RES["poolw"] + g) % BANKS][:], ACT.Identity,
                               scale=pool_gain[:, g:g + 1]).then_inc(ev_hi, 1)
            for n in range(DT):
                split_hi(BLK["out1"] + n + AHEAD)
                act.wait_ge(acc_free, RES["out1"] + n + 1)
                residual(SQ["f2"], n, 2, part[1])

            ffn(2, part[0])

            def rope_hi(act, i):
                act.wait_ge(r_full, i + 1)
                act.copy(part[0][:, i, :], rope_c[:, i % 2, :]).then_inc(r_hi, 1)

            norm_std("m2")
            act.wait_ge(rcol_ready, 1)
            act.activation(std_col[:, TT:2 * TT], r_col[:, 3 * TT:4 * TT], ACT.Sqrt, scale=1.0 / D, bias=eps_col[:]).then_inc(std_ready, 1)
            norm_copy("m2", rstd)
            norm_copy("m2", rstd_fin, 1)
            split_hi(BLK["gate"] + AHEAD)
            act.wait_ge(acc_free, RES["gate"] + 1)
            act.activation(scan[:, 2, 0:S], scan[:, 4, 0:S], ACT.Abs, bias=gate_b[0:MH, 1:2]).then_inc(g_abs, 1)
            act.wait_ge(g_abs, 1)
            act.activation(scan[:, 2, 0:S], scan[:, 2, 0:S], ACT.Exp, scale=-1.0).then_inc(g_exp, 1)
            act.wait_ge(g_exp, 1)
            act.activation(scan[:, 2, 0:S], scan[:, 2, 0:S], ACT.Ln, bias=1.0).then_inc(g_ln, 1)
            for i in range(8):
                split_hi(BLK["dqk"] + i + AHEAD)
                if i >= 2:
                    rope_hi(act, i - 2)
            for i in range(6, 8):
                rope_hi(act, i)
            for i in range(4):
                split_hi(BLK["dv"] + i + AHEAD)
            for i in range(TT):
                act.wait_ge(acc_ready, RES["dv"] + i + 1)
                act.activation(part[2][:, i, :], bank[(RES["dv"] + i) % BANKS][:], ACT.Identity,
                               scale=r_col[:, TT + i:TT + i + 1]).then_inc(ev_hi, 1)

            def d_expo(u):
                n = (u // 2 % TT + 1) * P
                act.wait_ge(e_biased, u + 1)
                if u >= 4:
                    act.wait_ge(e_turned, u // 2 - 1)
                act.activation(d_p[:, u % 4, 0:n], d_s[:, u % 2, 0:n], ACT.Exp, scale=-1.0,
                               bias=d_min[:, u:u + 1], accum_out=d_sum[:, u:u + 1]).then_inc(e_exp, 1)

            def d_square(h):
                act.wait_ge(e_out, h + 1)
                if h >= 1:
                    act.wait_ge(e_stat, h)
                act.activation(d_sq[:], bank[h % 2][:], ACT.Square).then_inc(e_sq, 1)

            for w in range(4 * DH + 4):
                if w < 4 * DH:
                    d_expo(2 * w)
                    d_expo(2 * w + 1)
                if 1 <= w <= 4 * DH:
                    turned_hi(w - 1, e_turned, e_thi, e_out)
                if w >= 6 and (w - 6) % TT == 0:
                    d_square((w - 6) // TT)
            act.wait_ge(e_stat, DH)
            act.activation(head_r2[:], bank[2][0:DH, :], ACT.Sqrt, scale=1.0 / P, bias=eps_col[0:DH]).then_inc(e_std, 1)
            for h in range(DH):
                act.wait_ge(e_full, h + 1)
                act.copy(part[0][:, 4 + h, :], d_full[:, h % 2, :]).then_inc(e_hi, 1)
            for i in range(4):
                split_hi(BLK["mqk"] + i + AHEAD)
                act.wait_ge(c_sum, i + 1)
                act.activation(c_acc[:, i % 2, :], c_acc[:, i % 2, :], ACT.Silu).then_inc(c_act, 1)
                act.wait_ge(c_act, i + 1)
                act.activation(part[0][:, 8 + i, :], c_acc[:, i % 2, :], ACT.Copy, scale=0.125 if i < 2 else 1.0).then_inc(c_hi, 1)
            for i in range(4):
                split_hi(BLK["mv"] + i + AHEAD)
            for i in range(TT):
                act.wait_ge(acc_ready, RES["mv"] + i + 1)
                act.activation(part[2][:, i, :], bank[(RES["mv"] + i) % BANKS][:], ACT.Identity,
                               scale=r_col[:, TT + i:TT + i + 1]).then_inc(ev_hi, 1)
            for i in range(4):
                split_hi(BLK["mo"] + i + AHEAD)
                act.wait_ge(acc_free, RES["mo"] + i + 1)
                act.activation(sig[:, i, :], sig[:, i, :], ACT.Sigmoid).then_inc(mo_sig, 1)

            def m_expo(u):
                h, k = divmod(u, TT)
                act.wait_ge(m_diag, u + 1)
                if u >= 2:
                    act.wait_ge(m_plo, u - 1)
                last = act.activation(m_e[:, u % 2, 0:P], m_dm[:, u % 2, :], ACT.Exp, bias=a_col[:, k, h:h + 1])
                if k < TT - 1:
                    last = act.activation(m_e[:, u % 2, P:S - k * P], bank[2][:, (k + 1) * P:], ACT.Exp, bias=a_col[:, k, h:h + 1])
                last.then_inc(m_exp, 1)

            def m_high(u):
                h, k = divmod(u, TT)
                act.wait_ge(m_prod, u + 1)
                if h >= 1:
                    act.wait_ge(m_pv, u - 3)
                act.copy(part[2][:, 8 + k, k * P:], m_e[:, u % 2, 0:S - k * P]).then_inc(m_phi, 1)

            def m_head(h):
                act.wait_ge(m_bc, 2 * h + 2)
                if h >= 1:
                    act.wait_ge(m_dn, h)
                act.activation(m_eg[:], bank[3][:], ACT.Exp).then_inc(m_egr, 1)
                act.wait_ge(m_pv, TT * (h + 1))
                if h >= 1:
                    act.wait_ge(m_stat, h)
                act.activation(m_sq[:], bank[h % 2][:], ACT.Square, scale=float(P) ** -0.5).then_inc(m_nsq, 1)
                act.wait_ge(m_dn, h + 1)
                act.activation(m_den[:], m_den[:], ACT.Square, scale=(EPS / P) ** 0.5).then_inc(m_dsq, 1)

            for h in range(MH):
                for k in range(TT):
                    m_expo(h * TT + k)
                    m_high(h * TT + k)
                m_head(h)
            act.wait_ge(m_stat, MH)
            act.activation(head_r2[:], bank[7][0:MH, :], ACT.Sqrt).then_inc(m_std, 1)
            for h in range(MH):
                act.wait_ge(m_norm, h + 1)
                act.copy(part[1][:, h, :], m_full[:, h % 2, :]).then_inc(m_hi, 1)

            for n in range(DT):
                split_hi(BLK["out2"] + n + AHEAD)
                act.wait_ge(acc_free, RES["out2"] + n + 1)
                square(SQ["post1"] + n, mixed[:, n, :])
            head("post1")()
            for n in range(DT):
                act.wait_ge(x_new, DT + n + 1)
                residual(SQ["f3"], n, 6, part[0])
            act.dma_start(x_spill, x[:]).then_inc(x_spilled, 16)

            up("f3_up0", part[1], False, head("f3"))
            down("f3_dn0", 2)
            up("f3_up1", part[1], False)
            def last(n):
                if n == 0:
                    act.wait_ge(acc_ready, RES["f3_dn1"] + 1)
                    act.wait_ge(x_spilled, 16)
                    act.dma_start(x_back, x_spill).then_inc(x_returned, 16)
                act.wait_ge(acc_free, RES["f3_dn1"] + n + 1)
                square(SQ["post2"] + n, x[:, n, :])
            down("f3_dn1", 2, last)
            head("post2")()
            for n in range(DT):
                act.wait_ge(acc_ready, RES["final"] + n + 1)
                act.copy(out_tok[:, :, n * P:(n + 1) * P],
                         bank[(RES["final"] + n) % BANKS][:].rearrange("p (t d) -> p t d", t=TT)).then_inc(y_final, 1)

        @block.vector
        def _(dve):
            chained = [0]

            def link(ins):
                chained[0] += 1
                ins.then_inc(v1, 1)
                dve.wait_ge(v1, chained[0])

            def split_lo(b, it=None, step=0):
                if it is None:
                    if b >= NBLK:
                        return
                    dve.wait_ge(w_hi, b + 1)
                else:
                    dve.wait_ge(w_hi, it * step + (b + 1))
                for piece in block_parts(b, it):
                    last = dve.tensor_tensor(piece(w_low[b % RING]), piece(w_raw[b % RING]), piece(w_high[b % RING]).bitcast(F32),
                                             ALU.subtract)
                last.then_inc(w_lo, 1)

            def result(r):
                dve.wait_ge(acc_ready, r + 1)
                return bank[r % BANKS]

            def residual_lo(gen, n, g, dst):
                dve.wait_ge(xt_hi, GEN[gen] + n + 1)
                dve.scalar_tensor_tensor(dst[:, 8 + n, :], x[:, n, :], gains[:, g, n:n + 1], dst[:, n, :].bitcast(F32),
                                         ALU.mult, ALU.subtract).then_inc(xt_lo, 1)

            def norm_spread(col, n_diag):
                if n_diag > 0:
                    dve.wait_ge(bc_ready, n_diag)
                for i in range(TT):
                    last = dve.tensor_scalar(diag[:, i, :], CI(C_IDENT), r_col[:, col + i:col + i + 1], None, ALU.mult)
                last.then_inc(diag_ready, 1)

            def norm(name):
                dve.wait_ge(std_ready, SPREAD[name] + 1)
                link(dve.reciprocal(r_col[:, 0:TT], std_col[:, 0:TT]))
                norm_spread(0, SPREAD[name])
                dve.wait_ge(rstd_ready, SPREAD[name] + 1)

            def up(name, dst, gated, head=None):
                per = 2 if gated else 4
                tiles = FT - HALF if (gated and name.endswith("1")) else HALF
                def turn(it):
                    for j in range(per):
                        c = HID[name] + j
                        val = lambda n: n if it is None else it * per + n
                        rval = lambda n: n if it is None else it * BANKS + n
                        def nxt(q):
                            b = BLK[name] + q + AHEAD
                            split_lo(b) if it is None else split_lo(b, it, RING)
                        idx = j if it is None else it * per + j
                        place = dst[:, idx, :] if it is None else dst[:, bass.ds(idx, 1), :]
                        if gated:
                            r = RES[name] + 2 * j
                            dve.wait_ge(acc_ready, rval(r + 1))
                            dve.tensor_tensor(ff_z[:, j % 2, :], bank[r % BANKS][:], rstd[:], ALU.mult).then_inc(z_ready, 1)
                            nxt(2 * j)
                            dve.wait_ge(acc_ready, rval(r + 2))
                            dve.tensor_tensor(ff_u[:, j % 2, :], bank[(r + 1) % BANKS][:], rstd[:], ALU.mult).then_inc(acc_free, 2)
                            dve.wait_ge(acc_free, rval(r + 2))
                            dve.wait_ge(s_ready, val(c + 1))
                            dve.tensor_tensor(ff_t[:, j % 2, :], ff_s[:, j % 2, :], ff_u[:, j % 2, :], ALU.mult).then_inc(t_ready, 1)
                            nxt(2 * j + 1)
                        else:
                            r = RES[name] + j
                            dve.wait_ge(acc_ready, rval(r + 1))
                            dve.scalar_tensor_tensor(ff_z[:, j % 2, :], bank[r % BANKS][:], 0.0, rstd[:],
                                                     ALU.max, ALU.mult).then_inc(acc_free, 1)
                            nxt(j)
                        dve.wait_ge(hid_hi, val(c + 1))
                        dve.tensor_tensor(low_of(dst, place, idx, it), ff_t[:, j % 2, :], place.bitcast(F32), ALU.subtract).then_inc(hid_done, 1)
                low_of = lambda d, place, idx, it: part[2][:, idx, :] if it is None else part[2][:, bass.ds(idx, 1), :]
                if head is not None:
                    head()
                    turn(None)
                with dve.Fori(0 if head is None else 1, tiles // per) as it:
                    turn(it)

            def down(name, blocks, each):
                for n in range(DT):
                    r = RES[name] + n
                    b = BLK[name] + n * blocks + AHEAD
                    if blocks == 2:
                        split_lo(b)
                    acc = result(r)
                    each(n, acc)
                    split_lo(b + blocks - 1)

            def add_half(n, acc):
                dve.scalar_tensor_tensor(x[:, n, :], acc[:], 0.5, x[:, n, :], ALU.mult, ALU.add).then_inc(acc_free, 1)

            dve.memset(eps_col[:], EPS).then_inc(consts_made, 1)
            dve.memset(r_col[:], 0.0).then_inc(consts_made, 1)
            dve.wait_ge(rel_in, 16)
            dve.wait_ge(x_in, 32)
            dve.tensor_scalar(rel_rows[:, 257:384], CI(C_ONES, 127, HEADS), rel_rows[:, 256:257], None, ALU.mult).then_inc(rel_padded, 1)
            for n in range(DT):
                acc = result(RES["input"] + n)
                dve.tensor_copy(x[:, n, :], acc[:]).then_inc(acc_free, 1)
                if n >= 1:
                    residual_lo("f1", n - 1, 0, part[0])
                if n in (1, 2):
                    split_lo(n - 1)
            residual_lo("f1", DT - 1, 0, part[0])
            dve.wait_ge(small_in, 16 * len(SMALL))
            for i in range(2):
                last = dve.tensor_tensor(lam_pr[0:64, i:i + 1], lam_in[0:64, 2 * i:2 * i + 1],
                                         lam_in[0:64, 2 * i + 1:2 * i + 2], ALU.mult)
            last.then_inc(lam_made, 1)
            link(dve.tensor_scalar(qk_gain[:, 0:1], qk_gain[:, 0:1], -0.125, None, ALU.mult))
            link(dve.tensor_scalar(far[:], far[:], -1.0, None, ALU.mult))
            link(dve.tensor_scalar(diff_gain[:], diff_gain[:], 1.0 - LAM_INIT, None, ALU.mult))
            dve.wait_ge(ev_hi, 2)
            link(dve.tensor_tensor(neg_lam[:], lam_ex[:, 1:2], lam_ex[:, 0:1], ALU.subtract))
            link(dve.tensor_scalar(neg_lam[:], neg_lam[:], -LAM_INIT, None, ALU.add))

            def ffn(f, hid):
                up(f"f{f}_up0", hid, True, lambda: norm(f"f{f}"))
                down(f"f{f}_dn0", 2, add_half)
                up(f"f{f}_up1", hid, True)
                def one(n, acc):
                    add_half(n, acc)
                    residual_lo("m1", n, 1, part[0])
                def two(n, acc):
                    dve.scalar_tensor_tensor(y_tmp[:, n % 2, :], acc[:], 0.5, x[:, n, :], ALU.mult, ALU.add).then_inc(acc_free, 1)
                    dve.wait_ge(acc_free, RES["f2_dn1"] + n + 1)
                    dve.tensor_scalar(x[:, n, :], y_tmp[:, n % 2, :], gains[:, 3, n:n + 1], None, ALU.mult).then_inc(x_new, 1)
                    residual_lo("m2", n, 4, part[1])
                down(f"f{f}_dn1", 1, one if f == 1 else two)

            ffn(1, part[1])

            norm("m1")
            for g in range(4):
                dve.memset(u_pad[:, g, 0:PAD], 0.0)
            dve.memset(win[:, 0, 0:PAD], 0.0)
            dve.memset(win[:, 1, 0:PAD], 0.0).then_inc(pads_zero, 1)
            for i in range(8):
                acc = result(RES["qk"] + i)
                dve.tensor_tensor(qk_raw[:, i, :], acc[:], rstd[:], ALU.mult).then_inc(acc_free, 1)
                split_lo(BLK["qk"] + i + AHEAD)
            for i in range(4):
                split_lo(BLK["v"] + i + AHEAD)
            def values_lo(name, col, seen):
                for i in range(TT):
                    acc = result(RES[name] + i)
                    dve.wait_ge(ev_hi, seen + i + 1)
                    dve.scalar_tensor_tensor(part[2][:, 4 + i, :], acc[:], r_col[:, col + i:col + i + 1],
                                             part[2][:, i, :].bitcast(F32), ALU.mult, ALU.subtract).then_inc(acc_free, 1)
            values_lo("v", 0, 2)
            dve.wait_ge(h_std, 1)
            dve.reciprocal(head_r[:], head_r[:]).then_inc(h_rec, 1)
            for i in range(4):
                split_lo(BLK["u"] + i + AHEAD)
                acc = result(RES["u"] + i)
                dve.tensor_tensor(u_pad[:, i, PAD:], acc[:], rstd[:], ALU.mult).then_inc(acc_free, 1)
            for i in range(8):
                dve.wait_ge(h_bc, i + 1)
                if i >= 2:
                    dve.wait_ge(qk_lo, i - 1)
                dve.scalar_tensor_tensor(qk_full[:, i % 2, :], qk_raw[:, i, :], qk_gain[:, i // 4:i // 4 + 1],
                                         bank[6 + i % 2][:], ALU.mult, ALU.mult).then_inc(qk_full_ready, 1)
                if i >= 1:
                    dve.wait_ge(qk_hi, i)
                    dve.tensor_tensor(part[1][:, 7 + i, :], qk_full[:, (i - 1) % 2, :], part[1][:, i - 1, :].bitcast(F32),
                                      ALU.subtract).then_inc(qk_lo, 1)
            dve.wait_ge(qk_hi, 8)
            dve.tensor_tensor(part[1][:, 15, :], qk_full[:, 1, :], part[1][:, 7, :].bitcast(F32), ALU.subtract).then_inc(qk_lo, 1)

            def a_bias(h):
                dve.wait_ge(b_mm, h + 1)
                o = bias[:, h % 2, :]
                dve.tensor_scalar(o[:, 0:256], const[:, C_ONES:C_ONES + 1].broadcast_to([P, 256]), far[:, h:h + 1], None, ALU.mult)
                dve.tensor_copy(o[0:64, 256:448], bank[2][0:64, 0:192])
                dve.tensor_copy(o[64:128, 256:512], bank[2][64:128, 0:256]).then_inc(b_done, 1)

            def a_min_of(u):
                h, q = divmod(u, TT)
                n = (q + 1) * P
                dve.wait_ge(a_score, u + 1)
                if q == 0:
                    dve.wait_ge(b_done, h + 1)
                if u >= 2:
                    dve.wait_ge(a_exp, u - 1)
                dve.tensor_tensor_reduce(out=a_s[:, u % 2, 0:n], in0=bank[4 + u % 2][:, 0:n],
                                         in1=bias[:, h % 2, S - n:S], scale=1.0, scalar=3e38, op0=ALU.add,
                                         op1=ALU.min, accum_out=a_min[:, u:u + 1]).then_inc(a_biased, 1)

            def a_normal(u):
                n = (u % TT + 1) * P
                dve.wait_ge(a_exp, u + 1)
                link(dve.reciprocal(a_rec[:, u:u + 1], a_sum[:, u:u + 1]))
                dve.tensor_scalar(a_p[:, u % 2, 0:n], a_p[:, u % 2, 0:n], a_rec[:, u:u + 1], None, ALU.mult).then_inc(a_prob, 1)

            def turned_lo(u, hi_sem, lo_sem):
                h, q = divmod(u, TT)
                dve.wait_ge(hi_sem, u + 1)
                dve.tensor_tensor(part[2][:, 12:13 + q, q * P:(q + 1) * P],
                                  bank[6 + u % 2][:, 0:(q + 1) * P].rearrange("p (k n) -> p k n", n=P),
                                  part[2][:, 8:9 + q, q * P:(q + 1) * P].bitcast(F32), ALU.subtract).then_inc(lo_sem, 1)

            def a_head_lo(h):
                r = 64 * (h % 2)
                dve.wait_ge(a_ohi, h + 1)
                dve.tensor_tensor(part[0][r:r + 64, 8 + h // 2, :], bank[h % 2][r:r + 64, :],
                                  part[0][r:r + 64, h // 2, :].bitcast(F32), ALU.subtract).then_inc(a_olo, 1)

            for s_ in range(2):
                link(dve.memset(bias[0:64, s_, 448:512], BIG))
            for h in range(2):
                a_bias(h)
            for u in range(4 * HEADS + 4):
                if u < 4 * HEADS:
                    a_min_of(u)
                    if u % TT == 3 and 2 <= u // TT + 1 < HEADS:
                        a_bias(u // TT + 1)
                if 1 <= u < 4 * HEADS + 1:
                    a_normal(u - 1)
                if 2 <= u < 4 * HEADS + 2:
                    turned_lo(u - 2, a_thi, a_tlo)
                if u >= 7 and (u - 7) % TT == 0:
                    a_head_lo((u - 7) // TT)
            for g in range(4):
                dve.wait_ge(pd_hi, g + 1)
                dve.tensor_tensor(part[0][:, 12 + g, :], u_pad[:, g, PAD:], part[0][:, 4 + g, :].bitcast(F32),
                                  ALU.subtract).then_inc(pd_lo, 1)
            split_lo(BLK["poolw"] + AHEAD)
            for g in range(4):
                acc = result(RES["poolw"] + g)
                dve.wait_ge(ev_hi, 2 + TT + g + 1)
                dve.scalar_tensor_tensor(part[0][:, 12 + g, :], acc[:], pool_gain[:, g:g + 1], part[0][:, 4 + g, :].bitcast(F32),
                                         ALU.mult, ALU.subtract).then_inc(acc_free, 1)
            for n in range(DT):
                acc = result(RES["out1"] + n)
                dve.tensor_tensor(x[:, n, :], acc[:], x[:, n, :], ALU.add).then_inc(acc_free, 1)
                residual_lo("f2", n, 2, part[1])
                split_lo(BLK["out1"] + n + AHEAD)

            ffn(2, part[0])

            dve.wait_ge(std_ready, SPREAD["m2"] + 1)
            link(dve.reciprocal(r_col[:, 0:TT], std_col[:, 0:TT]))
            link(dve.tensor_tensor(r_col[:, 2 * TT:3 * TT], r_col[:, 0:TT], r_col[:, 0:TT], ALU.mult))
            dve.tensor_tensor(r_col[:, 3 * TT:4 * TT], bank[4][:, TT:2 * TT], r_col[:, 2 * TT:3 * TT], ALU.mult).then_inc(rcol_ready, 1)
            dve.wait_ge(std_ready, SPREAD["m2"] + 2)
            link(dve.reciprocal(r_col[:, 2 * TT:3 * TT], std_col[:, TT:2 * TT]))
            link(dve.tensor_tensor(r_col[:, TT:2 * TT], r_col[:, 0:TT], r_col[:, 2 * TT:3 * TT], ALU.mult))
            norm_spread(TT, SPREAD["m2"])
            norm_spread(0, SPREAD["m2"] + 1)
            dve.wait_ge(rstd_ready, SPREAD["m2"] + 1)

            for k in range(2):
                link(dve.memset(scan[:, k, 0:SCAN_PAD], 0.0))
            data = lambda k: scan[:, k, SCAN_PAD:]
            acc = result(RES["gate"])
            link(dve.tensor_tensor(scan[:, 3, 0:S], acc[0:MH, :], rstd[0:MH, :], ALU.mult))
            dve.tensor_tensor(scan[:, 4, 0:S], acc[32:32 + MH, :], rstd[32:32 + MH, :], ALU.mult).then_inc(acc_free, 1)
            dve.wait_ge(acc_free, RES["gate"] + 1)
            link(dve.tensor_scalar(data(0), scan[:, 4, 0:S], gate_b[0:MH, 1:2], 0.0, ALU.add, ALU.min))
            split_lo(BLK["gate"] + AHEAD)
            dve.wait_ge(g_ln, 1)
            link(dve.tensor_tensor(data(0), data(0), scan[:, 2, 0:S], ALU.subtract))

            def doubling(op):
                for k in range(9):
                    a, b = k % 2, 1 - k % 2
                    sh = 2 ** k
                    link(dve.tensor_tensor(data(b), data(a), scan[:, a, SCAN_PAD - sh:SCAN_PAD - sh + S], op))
            doubling(ALU.add)
            link(dve.tensor_copy(scan[:, 4, 0:S], data(1)))
            link(dve.scalar_tensor_tensor(data(0), scan[:, 3, 0:S], gate_b[0:MH, 0:1], scan[:, 4, 0:S], ALU.add, ALU.subtract))
            link(dve.tensor_copy(scan[:, 2, 0:S], data(0)))
            doubling(ALU.max)
            link(dve.tensor_scalar(rows[0:MH, :], data(1), 0.0, -1.0, ALU.max, ALU.mult))
            dve.tensor_tensor(rows[32:32 + MH, :], rows[0:MH, :], scan[:, 4, 0:S], ALU.subtract).then_inc(g_rows, 1)

            def rope_in(i):
                acc = result(RES["dqk"] + i)
                dve.scalar_tensor_tensor(rope_y[:, i % 4, :], acc[:], -0.125 if i < 4 else 1.0, rstd[:], ALU.mult, ALU.mult).then_inc(acc_free, 1)

            def rope_sum(i):
                dve.wait_ge(r_perm, i + 1)
                link(dve.tensor_tensor(rope_s[:, i % 2, :], bank[6 + i % 2][:], const[:, C_SIN:C_SIN + S], ALU.mult))
                dve.wait_ge(r_cos, i + 1)
                dve.tensor_tensor(rope_c[:, i % 2, :], rope_c[:, i % 2, :], rope_s[:, i % 2, :], ALU.add).then_inc(r_full, 1)
                dve.wait_ge(r_hi, i + 1)
                dve.tensor_tensor(part[0][:, 8 + i, :], rope_c[:, i % 2, :], part[0][:, i, :].bitcast(F32), ALU.subtract).then_inc(r_lo, 1)

            dve.wait_ge(g_turn, 1)
            dve.tensor_copy(a_col[:].rearrange("p t h -> p (t h)"), bank[5][:, 0:TT * MH]).then_inc(g_cols, 1)
            for i in range(8):
                rope_in(i)
                split_lo(BLK["dqk"] + i + AHEAD)
                if i >= 2:
                    rope_sum(i - 2)
            for i in range(6, 8):
                rope_sum(i)
            for i in range(4):
                split_lo(BLK["dv"] + i + AHEAD)
            values_lo("dv", TT, 2 + TT + 4)

            link(dve.memset(d_mask[:, 0:S - P], 0.0))
            link(dve.tensor_copy(d_mask[:, S - P:], CI(C_CAUSAL)))

            def d_min_of(u):
                n = (u // 2 % TT + 1) * P
                dve.wait_ge(e_score, u + 1)
                if u >= 2:
                    dve.wait_ge(e_exp, u - 1)
                dve.tensor_tensor_reduce(out=d_s[:, u % 2, 0:n], in0=bank[4 + u % 2][:, 0:n],
                                         in1=d_mask[:, S - n:S], scale=1.0, scalar=3e38, op0=ALU.add,
                                         op1=ALU.min, accum_out=d_min[:, u:u + 1]).then_inc(e_biased, 1)

            def d_combine(w):
                n = (w % TT + 1) * P
                p0, p1 = d_p[:, 2 * w % 4, 0:n], d_p[:, 2 * w % 4 + 1, 0:n]
                dve.wait_ge(e_exp, 2 * w + 2)
                link(dve.reciprocal(d_rec[:, 2 * w:2 * w + 2], d_sum[:, 2 * w:2 * w + 2]))
                link(dve.tensor_scalar(d_lam[:, w % 16:w % 16 + 1], d_rec[:, 2 * w + 1:2 * w + 2], neg_lam[:], None, ALU.mult))
                link(dve.tensor_scalar(p0, p0, d_rec[:, 2 * w:2 * w + 1], None, ALU.mult))
                dve.scalar_tensor_tensor(p0, p1, d_lam[:, w % 16:w % 16 + 1], p0, ALU.mult, ALU.add).then_inc(e_prob, 1)

            def d_copy(h):
                dve.wait_ge(e_sq, h + 1)
                dve.tensor_copy(o_diff[:, h, :], bank[h % 2][:]).then_inc(e_copied, 1)

            for w in range(4 * DH + 4):
                if w < 4 * DH:
                    d_min_of(2 * w)
                    d_min_of(2 * w + 1)
                if 1 <= w <= 4 * DH:
                    d_combine(w - 1)
                if 2 <= w <= 4 * DH + 1:
                    turned_lo(w - 2, e_thi, e_tlo)
                if w >= 6 and (w - 6) % TT == 0:
                    d_copy((w - 6) // TT)
            dve.wait_ge(e_std, 1)
            dve.reciprocal(head_r2[:], head_r2[:]).then_inc(e_rec, 1)
            for h in range(DH):
                dve.wait_ge(e_bc, h + 1)
                if h >= 2:
                    dve.wait_ge(e_lo, h - 1)
                dve.scalar_tensor_tensor(d_full[:, h % 2, :], o_diff[:, h, :], diff_gain[:], bank[4 + h % 2][:],
                                         ALU.mult, ALU.mult).then_inc(e_full, 1)
                dve.wait_ge(e_hi, h + 1)
                dve.tensor_tensor(part[0][:, 12 + h, :], d_full[:, h % 2, :], part[0][:, 4 + h, :].bitcast(F32),
                                  ALU.subtract).then_inc(e_lo, 1)

            for k in range(2):
                link(dve.memset(c_pad[:, k, 0:4], 0.0))
            for i in range(4):
                acc = result(RES["mqk"] + i)
                dve.tensor_tensor(c_pad[:, i % 2, 4:], acc[:], rstd[:], ALU.mult).then_inc(acc_free, 1)
                dve.wait_ge(acc_free, RES["mqk"] + i + 1)
                split_lo(BLK["mqk"] + i + AHEAD)
                o = c_acc[:, i % 2, :]
                if i >= 2:
                    dve.wait_ge(c_lo, i - 1)
                link(dve.tensor_scalar(o, c_pad[:, i % 2, 1:1 + S], conv_w[:, 0, i:i + 1], conv_b[:, i:i + 1], ALU.mult, ALU.add))
                for j in range(1, CONV):
                    ins = dve.scalar_tensor_tensor(o, c_pad[:, i % 2, 1 + j:1 + j + S], conv_w[:, j, i:i + 1], o, ALU.mult, ALU.add)
                    if j < CONV - 1:
                        link(ins)
                ins.then_inc(c_sum, 1)
                dve.wait_ge(c_hi, i + 1)
                dve.scalar_tensor_tensor(part[0][:, i, :], o, 0.125 if i < 2 else 1.0,
                                         part[0][:, 8 + i, :].bitcast(F32), ALU.mult, ALU.subtract).then_inc(c_lo, 1)
            for i in range(4):
                split_lo(BLK["mv"] + i + AHEAD)
            values_lo("mv", TT, 2 + TT + 4 + TT)
            for i in range(4):
                split_lo(BLK["mo"] + i + AHEAD)
                acc = result(RES["mo"] + i)
                dve.tensor_tensor(sig[:, i, :], acc[:], rstd[:], ALU.mult).then_inc(acc_free, 1)

            def m_diag_of(u):
                h, k = divmod(u, TT)
                dve.wait_ge(m_bc, 2 * h + 1)
                if u >= 2:
                    dve.wait_ge(m_exp, u - 1)
                dve.tensor_tensor(m_dm[:, u % 2, :], bank[2][:, k * P:(k + 1) * P], CI(C_MASKT), ALU.add).then_inc(m_diag, 1)

            def m_weigh(u):
                h, k = divmod(u, TT)
                n = S - k * P
                dve.wait_ge(m_exp, u + 1)
                dve.wait_ge(m_score, u + 1)
                dve.tensor_tensor(m_e[:, u % 2, 0:n], m_e[:, u % 2, 0:n], bank[4 + u % 2][:, 0:n], ALU.mult).then_inc(m_prod, 1)
                dve.wait_ge(m_phi, u + 1)
                dve.tensor_tensor(part[2][:, 12 + k, k * P:], m_e[:, u % 2, 0:n], part[2][:, 8 + k, k * P:].bitcast(F32),
                                  ALU.subtract).then_inc(m_plo, 1)

            def m_head(h):
                dve.wait_ge(m_nsq, h + 1)
                dve.tensor_copy(m_num[:, h, :], bank[h % 2][:]).then_inc(m_ncp, 1)
                dve.wait_ge(m_egr, h + 1)
                link(dve.scalar_tensor_tensor(m_den[:], bank[6][:], -1.0, m_eg[:], ALU.mult, ALU.max))
                dve.tensor_tensor(m_den[:], bank[6][:], m_den[:], ALU.max).then_inc(m_dn, 1)
                dve.wait_ge(m_dsq, h + 1)
                dve.tensor_tensor(m_sq[:], m_sq[:], m_den[:], ALU.add).then_inc(m_sqs, 1)

            for u in range(MH * TT):
                m_diag_of(u)
                m_weigh(u)
                if u % TT == TT - 1:
                    m_head(u // TT)
            dve.wait_ge(m_std, 1)
            dve.reciprocal(head_r2[:], head_r2[:]).then_inc(m_rec, 1)
            for h in range(MH):
                dve.wait_ge(m_bcr, h + 1)
                if h >= 2:
                    dve.wait_ge(m_lo, h - 1)
                link(dve.scalar_tensor_tensor(m_full[:, h % 2, :], m_num[:, h, :], mlstm_gain[:, h:h + 1],
                                              bank[4 + h % 2][:], ALU.mult, ALU.mult))
                dve.wait_ge(mo_sig, h + 1)
                dve.tensor_tensor(m_full[:, h % 2, :], m_full[:, h % 2, :], sig[:, h, :], ALU.mult).then_inc(m_norm, 1)
                dve.wait_ge(m_hi, h + 1)
                dve.tensor_tensor(part[1][:, 8 + h, :], m_full[:, h % 2, :], part[1][:, h, :].bitcast(F32), ALU.subtract).then_inc(m_lo, 1)

            for n in range(DT):
                acc = result(RES["out2"] + n)
                dve.tensor_copy(mixed[:, n, :], acc[:]).then_inc(acc_free, 1)
                split_lo(BLK["out2"] + n + AHEAD)
            norm("post1")
            for n in range(DT):
                link(dve.scalar_tensor_tensor(mixed[:, n, :], mixed[:, n, :], gains[:, 5, n:n + 1], rstd[:], ALU.mult, ALU.mult))
                if n == 0:
                    dve.wait_ge(x_unit, DT)
                dve.tensor_tensor(x[:, n, :], x[:, n, :], mixed[:, n, :], ALU.add).then_inc(x_new, 1)
                if n >= 1:
                    residual_lo("f3", n - 1, 6, part[0])
            residual_lo("f3", DT - 1, 6, part[0])

            up("f3_up0", part[1], False, lambda: norm("f3"))
            def first(n, acc):
                if n == 0:
                    dve.wait_ge(x_spilled, 16)
                dve.tensor_copy(x[:, n, :], acc[:]).then_inc(acc_free, 1)
            down("f3_dn0", 2, first)
            up("f3_up1", part[1], False)
            down("f3_dn1", 2, lambda n, acc: dve.tensor_tensor(x[:, n, :], acc[:], x[:, n, :], ALU.add).then_inc(acc_free, 1))
            norm("post2")
            dve.wait_ge(x_returned, 16)
            for n in range(DT):
                link(dve.scalar_tensor_tensor(x[:, n, :], x[:, n, :], gains[:, 7, n:n + 1], rstd[:], ALU.mult, ALU.mult))
                dve.tensor_tensor(x[:, n, :], x[:, n, :], x_back[:, n, :], ALU.add).then_inc(x_new, 1)

        @block.gpsimd
        def _(pool):
            stepped = [0]

            def link(ins):
                stepped[0] += 1
                ins.then_inc(pool_step, 1)
                pool.wait_ge(pool_step, stepped[0])

            def add_square(i, which, first):
                pool.wait_ge(sq_ready, i + 1)
                if first:
                    pool.tensor_copy(sq_sum[:, which, :], sq[:, i % 2, :]).then_inc(sq_added, 1)
                else:
                    pool.wait_ge(sq_added, i)
                    pool.tensor_tensor(sq_sum[:, which, :], sq_sum[:, which, :], sq[:, i % 2, :], ALU.add).then_inc(sq_added, 1)

            def sum_squares(name):
                if NORM[name]:
                    pool.wait_ge(stat_ready, NORM[name])
                for n in range(DT):
                    add_square(SQ[name] + n, 0, n == 0)

            sum_squares("f1")
            sum_squares("m1")
            for g in range(4):
                pool.wait_ge(acc_free, RES["u"] + g + 1)
                pool.wait_ge(pads_zero, 1)
                src = u_pad[:, g, :]
                for k in range(g + 1):
                    dst = win[:, k % 2, :]
                    link(pool.tensor_tensor(dst[:, PAD:], src[:, PAD:], src[:, PAD - 2 ** k:PAD - 2 ** k + S], ALU.add))
                    src = dst
                link(pool.tensor_tensor(src[:, PAD:2 * PAD], src[:, PAD:2 * PAD], const[:, C_POOL + 16 * g:C_POOL + 16 * (g + 1)], ALU.mult))
                link(pool.tensor_scalar(src[:, PAD:], src[:, PAD:], 0.5 ** (g + 1), None, ALU.mult))
                pool.tensor_tensor(u_pad[:, g, PAD:], src[:, PAD:], u_pad[:, g, PAD:], ALU.subtract).then_inc(pool_done, 1)
                pool.wait_ge(pool_done, g + 1)
            sum_squares("f2")
            pool.wait_ge(stat_ready, NORM["m2"])
            for n in range(DT):
                for which in range(2):
                    add_square(SQ["m2"] + 2 * n + which, which, n == 0)
            for i in range(8):
                pool.wait_ge(acc_free, RES["dqk"] + i + 1)
                if i >= 2:
                    pool.wait_ge(r_lo, i - 1)
                pool.tensor_tensor(rope_c[:, i % 2, :], rope_y[:, i % 4, :], const[:, C_COS:C_COS + S], ALU.mult).then_inc(r_cos, 1)
            pool.wait_ge(rstd_ready, SPREAD["m2"] + 2)
            for n in range(DT):
                pool.tensor_tensor(x[:, n, :], x[:, n, :], rstd_fin[:], ALU.mult).then_inc(x_unit, 1)
            sum_squares("post1")
            sum_squares("f3")
            sum_squares("post2")

        @block.tensor
        def _(pe):
            def parts(region, k):
                return part[region][:, k, :], part[region][:, 8 + k, :]

            def finish(mm):
                mm.then_inc(acc_ready, 1)

            def norm_stat(name, sums=1):
                pe.wait_ge(sq_added, SQ[name] + DT * sums)
                for s_ in range(sums):
                    for i in range(TT):
                        mm = pe.matmul(bank[4][:, s_ * TT + i:s_ * TT + i + 1], sq_sum[:, s_, i * P:(i + 1) * P],
                                       const[:, C_ONES:C_ONES + 1], start=True, stop=True)
                mm.then_inc(stat_ready, 1)

            def norm_spread(name, extra=0):
                n = SPREAD[name] + extra
                pe.wait_ge(diag_ready, n + 1)
                if n > 0:
                    pe.wait_ge(rstd_ready, n)
                for i in range(TT):
                    mm = pe.matmul(bank[5][:, i * P:(i + 1) * P], CI(C_ONES), diag[:, i, :], start=True, stop=True)
                mm.then_inc(bc_ready, 1)

            def tile(b, r, src, k0=0, nk=8, skip=0, start=True, stop=True, need=None, order=None, m=P, very_first=False):
                hi, lo = w_tiles(b)
                order = order or list(range(nk))
                for k in order:
                    if need is not None:
                        need(k0 + k)
                    x_hi, x_lo = src(k0 + k)
                    mm = split3(pe, bank[r % BANKS][0:m, :], hi[:, skip + k, 0:m], lo[:, skip + k, 0:m], x_hi, x_lo,
                                start and k == order[0], stop and k == order[-1], k == order[0] and not very_first)
                return mm

            def up(name, src, gated, gen=None, after=()):
                tiles = 2 * (FT - HALF if name.endswith("1") else HALF) if gated else HALF
                def turn(it):
                    for q in range(RING):
                        b, r = BLK[name] + q, RES[name] + q
                        block_ready(pe, b, it, RING)
                        free_bank(pe, r, it, RING)
                        need = (lambda k: pe.wait_ge(xt_lo, GEN[gen] + k + 1)) if it is None and q == 0 else None
                        finish(tile(b, r, src, need=need, very_first=b == 0 and it is None))
                        if it is None and q < len(after):
                            after[q]()
                if gen is not None:
                    turn(None)
                with pe.Fori(0 if gen is None else 1, tiles // RING) as it:
                    turn(it)

            def down(name, blocks, hid, h0, tiles):
                def turn(it):
                    for j in range(BANKS):
                        r = RES[name] + j
                        free_bank(pe, r, it, BANKS)
                        for c in range(blocks):
                            b = BLK[name] + j * blocks + c
                            block_ready(pe, b, it, BANKS * blocks)
                            def need(k):
                                if k == 0:
                                    pe.wait_ge(hid_done, h0 + tiles - 2)
                                if k == tiles - 2:
                                    pe.wait_ge(hid_done, h0 + tiles)
                            nk = min(8, tiles - 8 * c)
                            mm = tile(b, r, lambda k: (part[hid][:, k, :], part[2][:, k, :]), 8 * c, nk, 8 - nk, c == 0, c == blocks - 1, need=need)
                        finish(mm)
                with pe.Fori(0, DT // BANKS) as it:
                    turn(it)

            def columns(name, n, src, after=None, need=None):
                for i in range(n):
                    block_ready(pe, BLK[name] + i)
                    free_bank(pe, RES[name] + i)
                    finish(tile(BLK[name] + i, RES[name] + i, src, need=need if i == 0 else None))
                    if after is not None:
                        after(i)

            def values(name, region, after=None):
                for j in range(4):
                    b = BLK[name] + j
                    block_ready(pe, b)
                    hi, lo = w_tiles(b, S)
                    for kk in range(2):
                        k = 2 * j + kk
                        x_hi, x_lo = parts(region, k)
                        for i in range(TT):
                            if k == 0:
                                free_bank(pe, RES[name] + i)
                            mm = split3(pe, bank[(RES[name] + i) % BANKS][:], x_hi[:, i * P:(i + 1) * P], x_lo[:, i * P:(i + 1) * P],
                                        hi[:, kk, :], lo[:, kk, :], k == 0, k == DT - 1, kk == 0 and i == 0)
                            if k == DT - 1:
                                finish(mm)
                    if after is not None:
                        after(j)

            pe.wait_ge(x_in, 32)
            for n in range(DT):
                free_bank(pe, RES["input"] + n)
                for i in range(TT):
                    mm = pe.transpose(bank[(RES["input"] + n) % BANKS][:, i * P:(i + 1) * P],
                                      x_tok[:, i, n * P:(n + 1) * P], CI(C_IDENT))
                finish(mm)
            def lam_sum():
                pe.wait_ge(lam_made, 1)
                pe.matmul(bank[5][:, 0:2], const[0:64, C_ONES:C_ONES + P], lam_pr[0:64, :], start=True, stop=True).then_inc(lam_summed, 1)
            lam_sum()

            def norm_steps(name):
                return (lambda: norm_stat(name), lambda: norm_spread(name))

            def ffn(f, region, hid):
                src = lambda k: parts(region, k)
                up(f"f{f}_up0", src, True, f"f{f}", norm_steps(f"f{f}"))
                down(f"f{f}_dn0", 2, hid, HID[f"f{f}_up0"], HALF)
                up(f"f{f}_up1", src, True)
                down(f"f{f}_dn1", 1, hid, HID[f"f{f}_up1"], FT - HALF)

            ffn(1, 0, 1)

            def head_stat(i):
                pe.wait_ge(y_sq, i + 1)
                pe.matmul(bank[4][0:16, :], const[:, C_HSUM + 16 * i:C_HSUM + 16 * (i + 1)], head_sq[:, i % 2, :],
                          start=(i == 0), stop=(i == 7)).then_inc(h_stat, 1)

            def after_qk(i):
                if i < 2:
                    norm_steps("m1")[i]()
                if i >= 3:
                    head_stat(i - 3)
            x_in1 = lambda k: parts(0, k)
            columns("qk", 8, x_in1, after_qk, need=lambda k: pe.wait_ge(xt_lo, GEN["m1"] + k + 1))
            def after_v(j):
                if j == 0:
                    for i in range(5, 8):
                        head_stat(i)
            values("v", 0, after_v)
            columns("u", 4, x_in1)
            pe.wait_ge(h_rec, 1)
            for i in range(8):
                if i >= 2:
                    pe.wait_ge(qk_full_ready, i - 1)
                pe.matmul(bank[6 + i % 2][:], const[0:16, C_HROW + P * i:C_HROW + P * (i + 1)], head_r[:],
                          start=True, stop=True).then_inc(h_bc, 1)

            def a_bias(h):
                pe.wait_ge(toep_in[h % 2], 16 * (h // 2 + 1))
                if h >= 1:
                    pe.wait_ge(b_done, h)
                pe.matmul(bank[2][:, 0:P], toep[:, h % 2, 1, :], CI(C_FLIP), start=True, stop=True)
                pe.matmul(bank[2][:, P:2 * P], toep[:, h % 2, 0, :], CI(C_FLIP), start=True, stop=True).then_inc(b_mm, 1)

            def a_scores(u):
                h, q = divmod(u, TT)
                n, r = (q + 1) * P, 64 * (h % 2)
                if u >= 2:
                    pe.wait_ge(a_biased, u - 1)
                rows_ = slice(r, r + 64)
                qt, kt = h // 2, 4 + h // 2
                split3(pe, bank[4 + u % 2][:, 0:n], part[1][rows_, qt, q * P:(q + 1) * P], part[1][rows_, 8 + qt, q * P:(q + 1) * P],
                       part[1][rows_, kt, 0:n], part[1][rows_, 8 + kt, 0:n], True, True).then_inc(a_score, 1)

            def turn_probs(u, probs, ready, lo_sem, done):
                q = u % TT
                pe.wait_ge(ready, u + 1)
                if u >= 2:
                    pe.wait_ge(lo_sem, u - 1)
                for k in range(q + 1):
                    mm = pe.transpose(bank[6 + u % 2][:, k * P:(k + 1) * P], probs[:, k * P:(k + 1) * P], CI(C_IDENT))
                mm.then_inc(done, 1)

            def weigh_values(h, col, last_unit, lo_sem, done, copied):
                pe.wait_ge(lo_sem, last_unit + 1)
                if h >= 2:
                    pe.wait_ge(copied, h - 1)
                for k in range(TT):
                    mm = split3(pe, bank[h % 2][:, k * P:], part[2][:, k, col:col + P], part[2][:, 4 + k, col:col + P],
                                part[2][:, 8 + k, k * P:], part[2][:, 12 + k, k * P:], k == 0, k == TT - 1)
                mm.then_inc(done, 1)

            pe.wait_ge(acc_free, RES["u"] + 4)
            for h in range(2):
                a_bias(h)
            pe.wait_ge(qk_lo, 8)
            for u in range(4 * HEADS + 4):
                if u < 4 * HEADS:
                    a_scores(u)
                    if u % TT == 1 and 2 <= u // TT + 1 < HEADS:
                        a_bias(u // TT + 1)
                if 2 <= u < 4 * HEADS + 2:
                    turn_probs(u - 2, a_p[:, u % 2, :], a_prob, a_tlo, a_turned)
                if u >= 6 and (u - 6) % TT == 0 and (u - 6) // TT < HEADS:
                    h = (u - 6) // TT
                    weigh_values(h, P * (h // 2), 4 * h + 3, a_tlo, a_out, a_olo)
            pe.wait_ge(a_olo, HEADS)
            block_ready(pe, BLK["poolw"])
            hi, lo = w_tiles(BLK["poolw"])
            for g in range(4):
                free_bank(pe, RES["poolw"] + g)
                pe.wait_ge(pd_lo, g + 1)
                finish(split3(pe, bank[(RES["poolw"] + g) % BANKS][:], hi[:, g, :], lo[:, g, :], part[0][:, 4 + g, :],
                              part[0][:, 12 + g, :], True, True, g == 0))
            def mixed_in(k):
                if k >= 4:
                    pe.wait_ge(acc_free, RES["poolw"] + k - 3)
            for i in range(DT):
                block_ready(pe, BLK["out1"] + i)
                free_bank(pe, RES["out1"] + i)
                finish(tile(BLK["out1"] + i, RES["out1"] + i, x_in1, need=mixed_in if i == 0 else None))

            ffn(2, 1, 0)

            x_in2 = lambda k: parts(1, k)
            block_ready(pe, BLK["gate"])
            free_bank(pe, RES["gate"])
            finish(tile(BLK["gate"], RES["gate"], x_in2, need=lambda k: pe.wait_ge(xt_lo, GEN["m2"] + k + 1), m=36))
            norm_stat("m2", 2)

            def swap_halves(i):
                pe.wait_ge(acc_free, RES["dqk"] + i + 1)
                if i >= 2:
                    pe.wait_ge(r_full, i - 1)
                pe.matmul(bank[6 + i % 2][:], CI(C_SWAP), rope_y[:, i % 4, :], start=True, stop=True).then_inc(r_perm, 1)

            def after_dqk(i):
                if i == 0:
                    norm_spread("m2")
                    norm_spread("m2", 1)
                if i == 1:
                    pe.wait_ge(g_rows, 1)
                    pe.wait_ge(rstd_ready, SPREAD["m2"] + 2)
                    for j in range(TT):
                        mm = pe.transpose(bank[5][:, j * MH:(j + 1) * MH], scan[:, 2, j * P:(j + 1) * P], const[0:MH, C_IDENT:C_IDENT + MH])
                    mm.then_inc(g_turn, 1)
                if i >= 3:
                    swap_halves(i - 3)
            columns("dqk", 8, x_in2, after_dqk)
            def after_dv(j):
                for i in ((5, 6), (7,), (), ())[j]:
                    swap_halves(i)
            values("dv", 1, after_dv)

            def d_scores(u):
                w, c = divmod(u, 2)
                h, q = divmod(w, TT)
                n, rows_ = (q + 1) * P, slice(64 * c, 64 * c + 64)
                if u >= 2:
                    pe.wait_ge(e_biased, u - 1)
                split3(pe, bank[4 + u % 2][:, 0:n], part[0][rows_, h, q * P:(q + 1) * P], part[0][rows_, 8 + h, q * P:(q + 1) * P],
                       part[0][rows_, 4 + h, 0:n], part[0][rows_, 12 + h, 0:n], True, True).then_inc(e_score, 1)

            def d_stat(h):
                pe.wait_ge(e_sq, h + 1)
                pe.matmul(bank[2][0:DH, :], const[:, C_HOT + 4 * h:C_HOT + 4 * h + 4], d_sq[:], start=(h == 0),
                          stop=(h == DH - 1)).then_inc(e_stat, 1)

            pe.wait_ge(acc_free, RES["dv"] + 4)
            pe.wait_ge(r_lo, 8)
            for w in range(4 * DH + 4):
                if w < 4 * DH:
                    d_scores(2 * w)
                    d_scores(2 * w + 1)
                if 1 <= w <= 4 * DH:
                    turn_probs(w - 1, d_p[:, 2 * (w - 1) % 4, :], e_prob, e_tlo, e_turned)
                if w >= 5 and (w - 5) % TT == 0 and (w - 5) // TT < DH:
                    h = (w - 5) // TT
                    weigh_values(h, P * h, 4 * h + 3, e_tlo, e_out, e_copied)
                if w >= 7 and (w - 7) % TT == 0:
                    d_stat((w - 7) // TT)
            pe.wait_ge(e_copied, DH)
            pe.wait_ge(e_std, 1)

            def after_mqk(i):
                if i == 0:
                    pe.wait_ge(e_rec, 1)
                    for h in range(DH):
                        if h >= 2:
                            pe.wait_ge(e_full, h - 1)
                        pe.matmul(bank[4 + h % 2][:], const[0:DH, C_SEL4 + P * h:C_SEL4 + P * (h + 1)], head_r2[:],
                                  start=True, stop=True).then_inc(e_bc, 1)
            columns("mqk", 4, x_in2, after_mqk)
            values("mv", 1)
            columns("mo", 4, x_in2)

            def m_spread(h):
                if h >= 1:
                    pe.wait_ge(m_exp, TT * h)
                pe.matmul(bank[2][:], const[0:MH, C_SEL4 + P * h:C_SEL4 + P * (h + 1)], rows[0:MH, :], start=True, stop=True).then_inc(m_bc, 1)
                if h >= 1:
                    pe.wait_ge(m_egr, h)
                pe.matmul(bank[3][:], const[32:32 + MH, C_SEL4 + P * h:C_SEL4 + P * (h + 1)], rows[32:32 + MH, :], start=True, stop=True).then_inc(m_bc, 1)

            def m_scores(u):
                h, k = divmod(u, TT)
                rows_ = slice(64 * (h % 2), 64 * (h % 2) + 64)
                qt, kt = h // 2, 2 + h // 2
                if u >= 2:
                    pe.wait_ge(m_prod, u - 1)
                split3(pe, bank[4 + u % 2][:, 0:S - k * P], part[0][rows_, 8 + kt, k * P:(k + 1) * P], part[0][rows_, kt, k * P:(k + 1) * P],
                       part[0][rows_, 8 + qt, k * P:], part[0][rows_, qt, k * P:], True, True).then_inc(m_score, 1)

            def m_values(u):
                h, k = divmod(u, TT)
                pe.wait_ge(m_plo, u + 1)
                if k == 0 and h >= 2:
                    pe.wait_ge(m_ncp, h - 1)
                split3(pe, bank[h % 2][:, k * P:], part[2][:, k, P * h:P * (h + 1)], part[2][:, 4 + k, P * h:P * (h + 1)],
                       part[2][:, 8 + k, k * P:], part[2][:, 12 + k, k * P:], k == 0, k == TT - 1)
                if k == 0 and h >= 1:
                    pe.wait_ge(m_dn, h)
                pe.matmul(bank[6][:, k * P:], ones_r[:], part[2][:, 8 + k, k * P:], start=(k == 0), stop=False)
                pe.matmul(bank[6][:, k * P:], ones_r[:], part[2][:, 12 + k, k * P:], start=False, stop=(k == TT - 1)).then_inc(m_pv, 1)

            def m_stat_of(h):
                pe.wait_ge(m_sqs, h + 1)
                pe.matmul(bank[7][0:MH, :], const[:, C_HOT + 4 * h:C_HOT + 4 * h + 4], m_sq[:], start=(h == 0),
                          stop=(h == MH - 1)).then_inc(m_stat, 1)

            pe.wait_ge(acc_free, RES["mo"] + 4)
            pe.wait_ge(c_lo, 4)
            for u in range(MH * TT + 3):
                if u < MH * TT:
                    if u % TT == 0:
                        m_spread(u // TT)
                    m_scores(u)
                if 1 <= u <= MH * TT:
                    m_values(u - 1)
                if u >= 6 and (u - 6) % TT == 0:
                    m_stat_of((u - 6) // TT)
            pe.wait_ge(m_rec, 1)
            for h in range(MH):
                if h >= 2:
                    pe.wait_ge(m_norm, h - 1)
                pe.matmul(bank[4 + h % 2][:], const[0:MH, C_SEL4 + P * h:C_SEL4 + P * (h + 1)], head_r2[:],
                          start=True, stop=True).then_inc(m_bcr, 1)

            def mix2(k):
                return (part[0][:, 4 + k, :], part[0][:, 12 + k, :]) if k < 4 else (part[1][:, k - 4, :], part[1][:, 4 + k, :])
            def mix2_in(k):
                if k < 4:
                    pe.wait_ge(e_lo, k + 1)
                else:
                    pe.wait_ge(m_lo, k - 3)
            columns("out2", 8, mix2, need=mix2_in)
            norm_stat("post1")
            norm_spread("post1")

            src = lambda k: parts(0, k)
            up("f3_up0", src, False, "f3", norm_steps("f3"))
            down("f3_dn0", 2, 1, HID["f3_up0"], HALF)
            up("f3_up1", src, False)
            down("f3_dn1", 2, 1, HID["f3_up1"], HALF)
            norm_stat("post2")
            norm_spread("post2")
            for n in range(DT):
                free_bank(pe, RES["final"] + n) if n < 4 else pe.wait_ge(y_final, n - 3)
                pe.wait_ge(x_new, 2 * DT + n + 1)
                for i in range(TT):
                    mm = pe.transpose(bank[(RES["final"] + n) % BANKS][:, i * P:(i + 1) * P], x[:, n, i * P:(i + 1) * P], CI(C_IDENT))
                finish(mm)


_INS = ["x", "ffn1_norm", "ffn1_w_gate", "ffn1_w_up", "ffn1_w_down", "mix_norm", "w_in", "q_norm", "k_norm", "rel_bias",
        "pool_w", "pool_scale", "w_out", "ffn2_norm", "ffn2_w_gate", "ffn2_w_up", "ffn2_w_down", "final_norm",
        "norm_mix_pre_2", "w_in_2", "conv_w_2", "conv_b_2", "b_igate_2", "b_fgate_2", "lambda_q1_2", "lambda_k1_2",
        "lambda_q2_2", "lambda_k2_2", "diff_norm_2", "mlstm_norm_2", "w_out_2", "norm_mix_post_2", "norm_mlp_pre_2",
        "w_up_2", "w_down_2", "norm_mlp_post_2"]


def kernel(**inputs):
    import concourse.bacc as _bacc
    from concourse.bass_utils import run_bass_kernel_spmd as _run

    nc = _bacc.Bacc("TRN2", target_bir_lowering=False, num_devices=1)
    arrays, t = {}, {}
    for name in _INS + ["const"]:
        a = shape_constants() if name == "const" else np.ascontiguousarray(inputs[name])
        arrays[f"in_{name}"] = a
        t[name] = nc.dram_tensor(f"in_{name}", a.shape, mybir.dt.from_np(a.dtype), kind="ExternalInput").ap()
    t["out"] = nc.dram_tensor("out_0", (1, S, D), F32, kind="ExternalOutput").ap()
    build(nc, t)
    r = _run(nc, [arrays], core_ids=[0])
    return r.results[0]["out_0"]
```

```python
from contextlib import ExitStack

import numpy as np
import concourse.bass as bass
from concourse import mybir

ALU = mybir.AluOpType
ACT = mybir.ActivationFunctionType
F32 = mybir.dt.float32
F32R = mybir.dt.float32r

P = 128
S = 512
TT = S // P
D = 1024
DT = D // P
EPS = 1e-6
BIG = 1e30
FF = 2816
FF2 = 4096
HALF = 16
HEADS = 8
DH = 4
MH = 4
LAM_INIT = 0.2
PAD = 16
CONV = 4
RING = 4
BANKS = 4
AHEAD = 2

C_IDENT, C_FLIP, C_SWAP, C_HSUM, C_ONES, C_MASKT, C_CAUSAL = (128 * i for i in range(7))
C_HROW = 7 * 128
C_COS, C_SIN = C_HROW, C_HROW + 512
C_SEL4 = C_HROW + 1024
C_HOT = C_SEL4 + 512
C_POOL = C_HOT + 16
C_ALL = C_POOL + 64


def shape_constants():
    c = np.zeros((P, C_ALL + 2 * S), np.float32)
    p = np.arange(P)
    c[:, C_IDENT:C_IDENT + P] = np.eye(P)
    c[p, C_FLIP + P - 1 - p] = -1.0
    partner = np.where(p % 64 < 32, p + 32, p - 32)
    c[partner, C_SWAP + p] = 1.0
    for t in range(8):
        c[p, C_HSUM + 16 * t + 2 * t + p // 64] = 1.0
        c[2 * t + p // 64, C_HROW + P * t + p] = 1.0
    c[:, C_ONES:C_ONES + P] = 1.0
    c[:, C_MASKT:C_MASKT + P] = np.where(p[:, None] > p[None, :], -BIG, 0.0)
    c[:, C_CAUSAL:C_CAUSAL + P] = np.where(p[None, :] > p[:, None], BIG, 0.0)
    for h in range(4):
        c[h, C_SEL4 + P * h:C_SEL4 + P * (h + 1)] = 1.0
        c[32 + h, C_SEL4 + P * h:C_SEL4 + P * (h + 1)] = 1.0
        c[:, C_HOT + 4 * h + h] = 1.0
    inv = np.float32(10000.0) ** (-np.arange(0, 64, 2, dtype=np.float32) / np.float32(64))
    ang = np.arange(S, dtype=np.float32)[None, :] * inv[p % 32][:, None]
    c[:, C_ALL:C_ALL + S] = np.cos(ang)
    c[:, C_ALL + S:] = np.sin(ang) * np.where(p % 64 < 32, -1.0, 1.0)[:, None]
    for g in range(4):
        w = 2 ** (g + 1)
        c[:, C_POOL + 16 * g:C_POOL + 16 * (g + 1)] = w / np.minimum(np.arange(16) + 1, w)
    return c


def numbered(sizes):
    first, n = {}, 0
    for name, size in sizes:
        first[name] = n
        n += size
    return first, n


FT = FF // P
FT2 = FF2 // P
BLK, NBLK = numbered([
    ("f1_up0", 2 * HALF), ("f1_dn0", 2 * DT), ("f1_up1", 2 * (FT - HALF)), ("f1_dn1", DT),
    ("qk", 8), ("v", 4), ("u", 4), ("poolw", 1), ("out1", 8),
    ("f2_up0", 2 * HALF), ("f2_dn0", 2 * DT), ("f2_up1", 2 * (FT - HALF)), ("f2_dn1", DT),
    ("gate", 1), ("dqk", 8), ("dv", 4), ("mqk", 4), ("mo", 4), ("mv", 4), ("out2", 8),
    ("f3_up0", HALF), ("f3_dn0", 2 * DT), ("f3_up1", HALF), ("f3_dn1", 2 * DT)])
RES, NRES = numbered([
    ("input", 8),
    ("f1_up0", 2 * HALF), ("f1_dn0", DT), ("f1_up1", 2 * (FT - HALF)), ("f1_dn1", DT),
    ("qk", 8), ("v", 4), ("u", 4), ("poolw", 4), ("out1", 8),
    ("f2_up0", 2 * HALF), ("f2_dn0", DT), ("f2_up1", 2 * (FT - HALF)), ("f2_dn1", DT),
    ("gate", 1), ("dqk", 8), ("dv", 4), ("mqk", 4), ("mo", 4), ("mv", 4), ("out2", 8),
    ("f3_up0", HALF), ("f3_dn0", DT), ("f3_up1", HALF), ("f3_dn1", DT), ("final", 8)])
HID, NHID = numbered([("f1_up0", HALF), ("f1_up1", FT - HALF), ("f2_up0", HALF), ("f2_up1", FT - HALF),
                      ("f3_up0", HALF), ("f3_up1", HALF)])
GEN, _ = numbered([("f1", 8), ("m1", 8), ("f2", 8), ("m2", 8), ("f3", 8)])
SQ, _ = numbered([("f1", 8), ("m1", 8), ("f2", 8), ("m2", 16), ("post1", 8), ("f3", 8), ("post2", 8)])
SPREAD, _ = numbered([("f1", 1), ("m1", 1), ("f2", 1), ("m2", 2), ("post1", 1), ("f3", 1), ("post2", 1)])
NORM = {n: i for i, n in enumerate(["f1", "m1", "f2", "m2", "post1", "f3", "post2"])}
GAINS = ["ffn1_norm", "mix_norm", "ffn2_norm", "final_norm", "norm_mix_pre_2", "norm_mix_post_2",
         "norm_mlp_pre_2", "norm_mlp_post_2"]


def build(nc, t):
    with ExitStack() as ctx:
        def sb(name, shape, dt=F32, stack=ctx):
            return stack.enter_context(nc.sbuf_tensor(name, shape, dt))

        def sem(name):
            return ctx.enter_context(nc.semaphore(name))

        x = sb("x", [P, DT, S])
        part = []
        over = []
        for r in range(3):
            with ExitStack() as s:
                over.append(sb(f"region{r}_f32", [P, 16, S], F32, s))
            part.append(sb(f"region{r}", [P, 16 if r < 2 else 18, S], F32R))
        w_raw, w_low = [], []
        for r in range(RING):
            with ExitStack() as s:
                w_raw.append(sb(f"w_raw{r}", [P, 1024], F32, s))
            w_low.append(sb(f"w_low{r}", [P, 1024], F32R))
        w_high = [sb(f"w_high{r}", [P, 1024], F32R) for r in range(RING)]
        const = sb("const", [P, C_ALL])
        gains = sb("gains", [P, len(GAINS), DT])
        ones_r = sb("ones_r", [P, P], F32R)
        rstd = sb("rstd", [P, S])
        rstd_fin = sb("rstd_fin", [P, S])
        diag = sb("diag", [P, TT, P])
        sq = sb("sq", [P, 2, S])
        sq_sum = sb("sq_sum", [P, 2, S])
        std_col = sb("std_col", [P, 2 * TT])
        r_col = sb("r_col", [P, 4 * TT])
        eps_col = sb("eps_col", [P, 1])
        qk_gain = sb("qk_gain", [P, 2])
        pool_gain = sb("pool_gain", [P, 4])
        far = sb("far", [P, HEADS])
        conv_w = sb("conv_w", [P, CONV, 4])
        conv_b = sb("conv_b", [P, 4])
        gate_b = sb("gate_b", [P, 2])
        lam_in = sb("lam_in", [P, 4])
        lam_pr = sb("lam_pr", [P, 2])
        lam_ex = sb("lam_ex", [P, 2])
        neg_lam = sb("neg_lam", [P, 1])
        diff_gain = sb("diff_gain", [P, 1])
        mlstm_gain = sb("mlstm_gain", [P, MH])
        rel_rows = sb("rel_rows", [HEADS, 384])

        with ExitStack() as s:
            ff_z = sb("ff_z", [P, 2, S], F32, s)
            ff_u = sb("ff_u", [P, 2, S], F32, s)
            ff_s = sb("ff_s", [P, 2, S], F32, s)
            ff_t = sb("ff_t", [P, 2, S], F32, s)
            y_tmp = sb("y_tmp", [P, 2, S], F32, s)
        with ExitStack() as s:
            u_pad = sb("u_pad", [P, 4, PAD + S], F32, s)
            win = sb("win", [P, 2, PAD + S], F32, s)
            head_r = sb("head_r", [2 * HEADS, S], F32, s)
            with ExitStack() as s2:
                head_sq = sb("head_sq", [P, 2, S], F32, s2)
                qk_full = sb("qk_full", [P, 2, S], F32, s2)
            with ExitStack() as s2:
                a_s = sb("a_s", [P, 2, S], F32, s2)
                a_p = sb("a_p", [P, 3, S], F32, s2)
                toep = sb("toep", [P, 2, 2, P], F32, s2)
                bias = sb("bias", [P, 2, S], F32, s2)
                a_min = sb("a_min", [P, 4 * HEADS], F32, s2)
                a_sum = sb("a_sum", [P, 4 * HEADS], F32, s2)
                a_rec = sb("a_rec", [P, 4 * HEADS], F32, s2)
        with ExitStack() as s:
            rows = sb("rows", [36, S], F32, s)
            a_col = sb("a_col", [P, TT, MH], F32, s)
            head_r2 = sb("head_r2", [MH, S], F32, s)
            with ExitStack() as s2:
                scan = sb("scan", [MH, 5, S], F32, s2)
                rope_y = sb("rope_y", [P, 4, S], F32, s2)
                rope_c = sb("rope_c", [P, 2, S], F32, s2)
                rope_s = sb("rope_s", [P, 2, S], F32, s2)
            with ExitStack() as s2:
                d_s = sb("d_s", [P, 2, S], F32, s2)
                d_p = sb("d_p", [P, 6, S], F32, s2)
                d_mask = sb("d_mask", [P, S], F32, s2)
                d_min = sb("d_min", [P, 32], F32, s2)
                d_sum = sb("d_sum", [P, 32], F32, s2)
                d_rec = sb("d_rec", [P, 32], F32, s2)
                d_lam = sb("d_lam", [P, 16], F32, s2)
                d_sq = sb("d_sq", [P, S], F32, s2)
                d_full = d_s
                c_acc = sb("c_acc", [P, 4, S], F32, s2)
            with ExitStack() as s2:
                m_num = sb("m_num", [P, MH, S], F32, s2)
                m_e = sb("m_e", [P, 3, S], F32, s2)
                m_dm = sb("m_dm", [P, TT, P], F32, s2)
                m_eg = sb("m_eg", [P, S], F32, s2)
                m_den = sb("m_den", [P, S], F32, s2)
                m_sq = sb("m_sq", [P, S], F32, s2)
                m_full = m_e

        x_tok = over[2][:, 0:8, :].rearrange("p a b -> p (a b)").rearrange("p (t d) -> p t d", t=TT)
        qk_raw = over[2][:, 8:16, :]
        mixed = over[2][:, 0:8, :]
        x_back = over[1][:, 0:8, :]
        out_tok = over[0][:, 0:8, :].rearrange("p a b -> p (a b)").rearrange("p (t d) -> p t d", t=TT)
        o_diff = over[1][:, 0:4, :]
        mqk_raw = x[:, 0:4, :]
        sig = x[:, 4:8, :]

        turned = part[2][:, 8:18, :].rearrange("p a b -> p (a b)").rearrange("p (s b n) -> p s b n", s=2, n=P)

        def turned_unit(h, q, low):
            first, step = (q + 1, 5) if h % 2 == 0 else (15 - 5 * q, 6)
            return turned[:, low, first:first + step * q + 1:step, :]

        def turned_keys(h, k, low):
            first = 6 * k + 1 if h % 2 == 0 else 5 * (3 - k)
            return turned[:, low, first:first + TT - k, :].rearrange("p b n -> p (b n)")

        bank = [ctx.enter_context(nc.psum_tensor(f"bank{i}", [P, S], F32)) for i in range(8)]

        landed = [sem(f"landed{r}") for r in range(RING)]
        x_in, small_in, rel_in, toep_in = sem("x_in"), sem("small_in"), sem("rel_in"), [sem("toep_in0"), sem("toep_in1")]
        rel_padded, rel_stored = sem("rel_padded"), sem("rel_stored")
        consts_made, small_made = sem("consts_made"), sem("small_made")
        w_hi, w_lo, w_used = sem("w_hi"), sem("w_lo"), sem("w_used")
        acc_ready, acc_free = sem("acc_ready"), sem("acc_free")
        x_new, xt_hi, xt_lo = sem("x_new"), sem("xt_hi"), sem("xt_lo")
        sq_ready, sq_added = sem("sq_ready"), sem("sq_added")
        stat_ready, std_ready, rcol_ready, diag_ready = sem("stat_ready"), sem("std_ready"), sem("rcol_ready"), sem("diag_ready")
        bc_ready, rstd_ready = sem("bc_ready"), sem("rstd_ready")
        z_ready, s_ready, t_ready, hid_hi, hid_done = sem("z_ready"), sem("s_ready"), sem("t_ready"), sem("hid_hi"), sem("hid_done")
        ev_hi = sem("ev_hi")
        v1 = sem("dve_step")
        pool_step = sem("pool_step")
        gate_in, gain_in, lam_made, lam_summed = sem("gate_in"), sem("gain_in"), sem("lam_products_ready"), sem("lam_summed")
        x_unit, pads_zero = sem("x_unit_ready"), sem("pads_zero")

        w_dram = {n: t[n][0] for n in ("ffn1_w_gate", "ffn1_w_up", "ffn1_w_down", "w_in", "w_out",
                                       "ffn2_w_gate", "ffn2_w_up", "ffn2_w_down", "w_in_2", "w_out_2",
                                       "w_up_2", "w_down_2")}
        w_dram = {n: a.rearrange("(k p) n -> p k n", p=P) for n, a in w_dram.items()}

        CI = lambda c, n=P, rows=P: const[0:rows, c:c + n]

        def split3(pe, out, a_hi, a_lo, b_hi, b_lo, start, stop, new_block=False):
            mm = pe.matmul(out, a_hi, b_hi, start=start, stop=False)
            if new_block:
                mm.then_inc(w_used, 1)
            pe.matmul(out, a_hi, b_lo, start=False, stop=False)
            return pe.matmul(out, a_lo, b_hi, start=False, stop=stop)

        def free_bank(pe, r, it=None, step=0):
            n = r - BANKS + 1
            if it is not None:
                pe.wait_ge(acc_free, it * step + n)
            elif n > 0:
                pe.wait_ge(acc_free, n)

        def block_ready(pe, b, it=None, step=0):
            pe.wait_ge(w_lo, b + 1 if it is None else it * step + (b + 1))

        def block_parts(b, it):
            if it is None and b == BLK["poolw"]:
                return [lambda a: a[:, 0:4 * P]]
            if it is None and b == BLK["gate"]:
                return [lambda a, c=c: a[:].rearrange("p (k n) -> p k n", n=P)[:, :, c:c + MH] for c in (0, 32)]
            return [lambda a: a[:]]

        def w_tiles(b, width=P):
            hi, lo = w_high[b % RING], w_low[b % RING]
            return (hi[:].rearrange("p (k n) -> p k n", n=width), lo[:].rearrange("p (k n) -> p k n", n=width))

        def fetch(sp, b, src, it=None, step=0, width=P):
            if it is not None:
                sp.wait_ge(w_used, it * step + (b - RING + 1))
            elif b >= RING:
                sp.wait_ge(w_used, b - RING + 1)
            dst = w_raw[b % RING][:].rearrange("p (k n) -> p k n", n=width)
            nk = src.shape[1]
            sp.dma_start(dst[:, 0:nk, :], src).then_inc(landed[b % RING], 16)

        def sp_up(sp, name, mats, ht0, tiles):
            per = RING // len(mats)
            def turn(it):
                q = 0
                for j in range(per):
                    for m in mats:
                        b = BLK[name] + q
                        if it is None:
                            src = w_dram[m][:, :, (ht0 + j) * P:(ht0 + j + 1) * P]
                        else:
                            src = w_dram[m][:, :, bass.ds(it * (per * P) + (ht0 + j) * P, P)]
                        fetch(sp, b, src, it, RING)
                        q += 1
            first = 1 if BLK[name] < RING else 0
            if first:
                turn(None)
            with sp.Fori(first, tiles // per) as it:
                turn(it)

        def sp_down(sp, name, m, k0, nk):
            pieces = [(min(k, k0 + nk - 8), 8) for k in range(k0, k0 + nk, 8)]
            per = RING // len(pieces)
            with sp.Fori(0, DT // per) as it:
                q = 0
                for j in range(per):
                    for k, n in pieces:
                        fetch(sp, BLK[name] + q, w_dram[m][:, k:k + n, bass.ds(it * (per * P) + j * P, P)], it, RING)
                        q += 1

        def sp_cols(sp, name, m, tiles, col0):
            for j in range(tiles):
                fetch(sp, BLK[name] + j, w_dram[m][:, :, col0 + j * P:col0 + (j + 1) * P])

        def sp_rows(sp, name, m, col0):
            for j in range(4):
                fetch(sp, BLK[name] + j, w_dram[m][:, 2 * j:2 * j + 2, col0:col0 + S], width=S)

        out_stored, x_spilled, x_returned, y_final = sem("out_stored"), sem("x_spilled"), sem("x_returned"), sem("out_tile_ready")
        x_spill = [nc.dram_tensor(f"x_spill{i}", [P, DT, S], F32).ap() for i in range(2)]
        rel_pad_dram = nc.dram_tensor("rel_padded_rows", [HEADS, 384], F32).ap()

        y_sq, h_stat, h_std, h_rec, h_bc, qk_full_ready, qk_hi, qk_lo = (sem(n) for n in (
            "head_sq_ready", "head_stat_added", "head_std_ready", "head_rstd_ready", "head_bc_ready",
            "qk_full_ready", "qk_hi_ready", "qk_lo_ready"))
        b_mm, b_done = sem("bias_product"), sem("bias_ready")
        a_score, a_biased, a_exp, a_prob, a_turned, a_thi, a_tlo, a_out, a_ohi, a_olo = (sem(n) for n in (
            "scores_ready", "scores_biased", "exp_ready", "probs_ready", "probs_turned", "turned_hi",
            "turned_lo", "head_out_ready", "head_out_hi", "head_out_lo"))
        pool_done, pd_hi, pd_lo = sem("pooled"), sem("pooled_hi"), sem("pooled_lo")
        x_scaled = sem("x_scaled")
        g_abs, g_exp, g_ln, g_rows, g_turn, g_cols = (sem(n) for n in (
            "gate_abs", "gate_exp", "gate_ln", "gate_rows_ready", "gate_turned", "gate_cols_ready"))
        rope_in_sem = sem("rope_tables_in")
        r_perm, r_cos = sem("rope_swapped"), sem("rope_cos_ready")
        r_full, r_hi, r_lo = sem("rope_ready"), sem("rope_hi"), sem("rope_lo")
        e_score, e_biased, e_exp, e_prob, e_turned, e_thi, e_tlo, e_out, e_sq, e_copied, e_stat, e_std, e_rec, e_bc, e_full, e_hi, e_lo = (
            sem("d_" + n) for n in ("scores_ready", "scores_masked", "exp_ready", "probs_ready", "probs_turned",
                                    "turned_hi", "turned_lo", "out_ready", "sq_ready", "out_copied", "stat_added",
                                    "std_ready", "rstd_ready", "bc_ready", "normed", "normed_hi", "normed_lo"))
        c_sum, c_act, c_hi, c_lo, mo_z, mo_sig = (sem(n) for n in (
            "conv_ready", "conv_silu", "conv_hi", "conv_lo", "gate_o_ready", "gate_o_sigmoid"))
        m_bc, m_score, m_diag, m_exp, m_prod, m_phi, m_plo, m_pv, m_egr, m_nsq, m_ncp, m_dn, m_dsq, m_sqs, m_stat, m_std, m_rec, m_bcr, m_norm, m_hi, m_lo = (
            sem("m_" + n) for n in ("rows_spread", "scores_ready", "diag_ready", "exp_ready", "weights_ready",
                                    "weights_hi", "weights_lo", "values_added", "exp_g_ready", "num_sq_ready",
                                    "num_copied", "den_ready", "den_sq_ready", "sq_sum_ready", "stat_added",
                                    "std_ready", "rstd_ready", "bc_ready", "normed", "normed_hi", "normed_lo"))

        block = ctx.enter_context(nc.Block())

        @block.sync
        def _(sp):
            sp.dma_start(x_tok, t["x"][0].rearrange("(t p) d -> p t d", p=P)).then_inc(x_in, 16)
            sp.dma_start(const[:], t["const"][:, 0:C_ALL]).then_inc(x_in, 16)
            sp_up(sp, "f1_up0", ("ffn1_w_gate", "ffn1_w_up"), 0, HALF)
            sp_down(sp, "f1_dn0", "ffn1_w_down", 0, HALF)
            sp_up(sp, "f1_up1", ("ffn1_w_gate", "ffn1_w_up"), HALF, FT - HALF)
            sp_down(sp, "f1_dn1", "ffn1_w_down", HALF, FT - HALF)
            sp_cols(sp, "qk", "w_in", 8, 0)
            sp_rows(sp, "v", "w_in", S * 2)
            sp_cols(sp, "u", "w_in", 4, S * 3)
            fetch(sp, BLK["poolw"], t["pool_w"][0].rearrange("g c d -> c g d"))
            sp_cols(sp, "out1", "w_out", 8, 0)
            sp.wait_ge(qk_full_ready, 8)
            sp.dma_start(const[:, C_COS:C_COS + 2 * S], t["const"][:, C_ALL:]).then_inc(rope_in_sem, 16)
            sp_up(sp, "f2_up0", ("ffn2_w_gate", "ffn2_w_up"), 0, HALF)
            sp_down(sp, "f2_dn0", "ffn2_w_down", 0, HALF)
            sp_up(sp, "f2_up1", ("ffn2_w_gate", "ffn2_w_up"), HALF, FT - HALF)
            sp_down(sp, "f2_dn1", "ffn2_w_down", HALF, FT - HALF)
            b = BLK["gate"]
            sp.wait_ge(w_used, b - RING + 1)
            gw = w_raw[b % RING][:].rearrange("p (k n) -> p k n", n=P)
            with nc.allow_non_contiguous_dma("eight columns of w_in_2"):
                sp.dma_start(gw[:, :, 0:MH], w_dram["w_in_2"][:, :, 3072:3076]).then_inc(landed[b % RING], 16)
                sp.dma_start(gw[:, :, 32:32 + MH], w_dram["w_in_2"][:, :, 3076:3080]).then_inc(gate_in, 16)
            sp_cols(sp, "dqk", "w_in_2", 8, 0)
            sp_rows(sp, "dv", "w_in_2", 1024)
            sp_cols(sp, "mqk", "w_in_2", 4, 1536)
            sp_cols(sp, "mo", "w_in_2", 4, 2560)
            sp_rows(sp, "mv", "w_in_2", 2048)
            sp_cols(sp, "out2", "w_out_2", 8, 0)
            sp_up(sp, "f3_up0", ("w_up_2",), 0, HALF)
            sp_down(sp, "f3_dn0", "w_down_2", 0, HALF)
            sp_up(sp, "f3_up1", ("w_up_2",), HALF, HALF)
            sp_down(sp, "f3_dn1", "w_down_2", HALF, HALF)
            for n in range(DT):
                sp.wait_ge(y_final, n + 1)
                sp.dma_start(t["out"][0].rearrange("(t p) d -> p t d", p=P)[:, :, n * P:(n + 1) * P],
                             out_tok[:, :, n * P:(n + 1) * P]).then_inc(out_stored, 16)
            sp.wait_ge(out_stored, 16 * DT)

        SMALL = []

        @block.scalar
        def _(act):
            def load(dst, src):
                SMALL.append(1)
                with nc.allow_non_contiguous_dma("small vectors, once"):
                    act.dma_start(dst, src).then_inc(small_in, 16)

            def column(v):
                return v.rearrange("(n p) -> p n", p=P)

            act.dma_start(rel_rows[:, 0:257], t["rel_bias"][0]).then_inc(rel_in, 16)
            with nc.allow_non_contiguous_dma("small vectors, once"):
                act.dma_start(gains[:, 0, :], column(t[GAINS[0]][0])).then_inc(gain_in, 16)
            for i, n in enumerate(GAINS[1:]):
                load(gains[:, i + 1, :], column(t[n][0]))
            for i, n in enumerate(("q_norm", "k_norm")):
                for half in range(2):
                    load(qk_gain[64 * half:64 * half + 64, i:i + 1], t[n].rearrange("a d -> d a"))
            load(pool_gain[:], column(t["pool_scale"][0]))
            load(far[:], t["rel_bias"][0][:, 256:257].rearrange("h a -> a h").broadcast_to([P, HEADS]))
            for j in range(CONV):
                load(conv_w[:, j, :], column(t["conv_w_2"][0, j]))
            load(conv_b[:], column(t["conv_b_2"][0]))
            load(gate_b[0:MH, 0:1], t["b_igate_2"].rearrange("a d -> d a"))
            load(gate_b[0:MH, 1:2], t["b_fgate_2"].rearrange("a d -> d a"))
            for i, n in enumerate(("lambda_q1_2", "lambda_k1_2", "lambda_q2_2", "lambda_k2_2")):
                load(lam_in[0:64, i:i + 1], t[n].rearrange("a d -> d a"))
            load(diff_gain[:], t["diff_norm_2"].rearrange("a d -> d a"))
            load(mlstm_gain[:], t["mlstm_norm_2"][0].rearrange("h d -> d h"))
            act.wait_ge(rel_padded, 1)
            act.dma_start(rel_pad_dram, rel_rows[:]).then_inc(rel_stored, 16)

            def split_hi(b, it=None, step=0):
                if it is None:
                    if b >= NBLK:
                        return
                    act.wait_ge(landed[b % RING], 16 * (b // RING + 1))
                    if b >= RING:
                        act.wait_ge(w_used, b - RING + 1)
                    if b == BLK["gate"]:
                        act.wait_ge(gate_in, 16)
                else:
                    act.wait_ge(landed[b % RING], it * (16 * step // RING) + 16 * (b // RING + 1))
                    act.wait_ge(w_used, it * step + (b - RING + 1))
                for piece in block_parts(b, it):
                    last = act.copy(piece(w_high[b % RING]), piece(w_raw[b % RING]))
                last.then_inc(w_hi, 1)

            def residual(sqk, n, g, dst):
                act.activation(dst[:, n, :], x[:, n, :], ACT.Identity, scale=gains[:, g, n:n + 1]).then_inc(xt_hi, 1)
                if sqk is not None:
                    square(sqk + n, x[:, n, :])

            def square(i, src, scale=1.0):
                if i >= 2:
                    act.wait_ge(sq_added, i - 1)
                act.activation(sq[:, i % 2, :], src, ACT.Square, scale=scale).then_inc(sq_ready, 1)

            def norm_std(name):
                act.wait_ge(stat_ready, NORM[name] + 1)
                act.activation(std_col[:, 0:TT], bank[4][:, 0:TT], ACT.Sqrt, scale=1.0 / D, bias=eps_col[:]).then_inc(std_ready, 1)

            def norm_copy(name, dst, extra=0):
                act.wait_ge(bc_ready, SPREAD[name] + 1 + extra)
                act.copy(dst[:], bank[5][:]).then_inc(rstd_ready, 1)

            def up(name, dst, gated, head=None):
                per = 2 if gated else 4
                tiles = FT - HALF if (gated and name.endswith("1")) else HALF
                def turn(it):
                    for j in range(per):
                        c = HID[name] + j
                        val = lambda n: n if it is None else it * per + n
                        def nxt(q):
                            b = BLK[name] + q + AHEAD
                            split_hi(b) if it is None else split_hi(b, it, RING)
                        idx = j if it is None else it * per + j
                        if gated:
                            nxt(2 * j)
                            act.wait_ge(z_ready, val(c + 1))
                            act.activation(ff_s[:, j % 2, :], ff_z[:, j % 2, :], ACT.Silu).then_inc(s_ready, 1)
                            nxt(2 * j + 1)
                            act.wait_ge(t_ready, val(c + 1))
                        else:
                            nxt(j)
                            act.wait_ge(acc_free, val(RES[name] + j + 1))
                            if c >= 2:
                                act.wait_ge(hid_done, val(c - 1))
                            act.activation(ff_t[:, j % 2, :], ff_z[:, j % 2, :], ACT.Square).then_inc(t_ready, 1)
                            act.wait_ge(t_ready, val(c + 1))
                        act.copy(dst[:, bass.ds(idx, 1), :] if it is not None else dst[:, idx, :],
                                 ff_t[:, j % 2, :]).then_inc(hid_hi, 1)
                if head is not None:
                    head()
                    turn(None)
                with act.Fori(0 if head is None else 1, tiles // per) as it:
                    turn(it)

            def down(name, blocks, each=None):
                for n in range(DT):
                    for q in range(blocks):
                        split_hi(BLK[name] + n * blocks + q + AHEAD)
                    if each is not None:
                        each(n)

            def head(name):
                def run():
                    norm_std(name)
                    norm_copy(name, rstd)
                return run

            act.wait_ge(consts_made, 2)
            act.wait_ge(x_in, 32)
            act.copy(ones_r[:], CI(C_ONES)).then_inc(ev_hi, 1)
            for b in range(AHEAD):
                split_hi(b)
            act.wait_ge(gain_in, 16)
            for n in range(DT):
                act.wait_ge(acc_free, RES["input"] + n + 1)
                residual(SQ["f1"], n, 0, part[0])
            act.wait_ge(lam_summed, 1)
            act.activation(lam_ex[:], bank[5][:, 0:2], ACT.Exp).then_inc(ev_hi, 1)

            def ffn(f, hid):
                up(f"f{f}_up0", hid, True, head(f"f{f}"))
                down(f"f{f}_dn0", 2)
                up(f"f{f}_up1", hid, True)
                def each(n):
                    act.wait_ge(acc_free, RES[f"f{f}_dn1"] + n + 1)
                    if f == 1:
                        residual(SQ["m1"], n, 1, part[0])
                    else:
                        square(SQ["m2"] + 2 * n, y_tmp[:, n % 2, :])
                        act.wait_ge(x_new, n + 1)
                        residual(None, n, 4, part[0])
                        square(SQ["m2"] + 2 * n + 1, x[:, n, :])
                down(f"f{f}_dn1", 1, each)

            ffn(1, part[1])

            for i in range(8):
                split_hi(BLK["qk"] + i + AHEAD)
                if i == 0:
                    head("m1")()
                act.wait_ge(acc_free, RES["qk"] + i + 1)
                if i >= 2:
                    act.wait_ge(h_stat, i - 1)
                act.activation(head_sq[:, i % 2, :], qk_raw[:, i, :], ACT.Square).then_inc(y_sq, 1)
            for i in range(3):
                split_hi(BLK["v"] + i + AHEAD)
            act.wait_ge(h_stat, 8)
            act.activation(head_r[:], bank[4][0:2 * HEADS, :], ACT.Sqrt, scale=1.0 / 64, bias=eps_col[0:2 * HEADS]).then_inc(h_std, 1)
            split_hi(BLK["v"] + 3 + AHEAD)
            for i in range(8):
                act.wait_ge(qk_full_ready, i + 1)
                act.copy(part[1][:, i, :], qk_full[:, i % 2, :]).then_inc(qk_hi, 1)
            for i in range(TT):
                act.wait_ge(acc_ready, RES["v"] + i + 1)
                act.activation(part[2][:, i, :], bank[(RES["v"] + i) % BANKS][:], ACT.Identity,
                               scale=r_col[:, i:i + 1]).then_inc(ev_hi, 1)
            def toeplitz(h):
                if h >= 2:
                    act.wait_ge(b_mm, h - 1)
                src = rel_pad_dram[h:h + 1, 1:2].copy()
                src = bass.AP(src.tensor, src.offset, [[1, P], [128, 2], [1, P]])
                act.dma_start(toep[:, h % 2, :, :], src).then_inc(toep_in[h % 2], 16)
            act.wait_ge(rel_stored, 16)
            act.wait_ge(qk_lo, 8)
            for h in range(2):
                toeplitz(h)

            def a_expo(u):
                h, q = divmod(u, TT)
                n = (q + 1) * P
                act.wait_ge(a_biased, u + 1)
                if u >= 3:
                    act.wait_ge(a_turned, u - 2)
                act.activation(a_p[:, u % 3, 0:n], a_s[:, u % 2, 0:n], ACT.Exp, scale=-1.0,
                               bias=a_min[:, u:u + 1], accum_out=a_sum[:, u:u + 1]).then_inc(a_exp, 1)

            def turned_hi(u, ready, done, out_sem):
                h, q = divmod(u, TT)
                act.wait_ge(ready, u + 1)
                if h >= 2:
                    act.wait_ge(out_sem, h - 1)
                act.copy(turned_unit(h, q, 0),
                         bank[6 + u % 2][:, 0:(q + 1) * P].rearrange("p (k n) -> p k n", n=P)).then_inc(done, 1)

            def a_head_out(h):
                r = 64 * (h % 2)
                act.wait_ge(a_out, h + 1)
                act.copy(part[1][r:r + 64, h // 2, :], bank[h % 2][r:r + 64, :]).then_inc(a_ohi, 1)

            for u in range(4 * HEADS + 8):
                if u < 4 * HEADS and u % 8 == 4:
                    split_hi(BLK["u"] + u // 8 + AHEAD)
                if u < 4 * HEADS:
                    a_expo(u)
                    if u % TT == 3 and u // TT + 2 < HEADS:
                        toeplitz(u // TT + 2)
                if 2 <= u < 4 * HEADS + 2:
                    turned_hi(u - 2, a_turned, a_thi, a_out)
                if u >= 11 and (u - 11) % TT == 0:
                    a_head_out((u - 11) // TT)
            for g in range(4):
                act.wait_ge(pool_done, g + 1)
                act.copy(part[1][:, 4 + g, :], u_pad[:, g, PAD:]).then_inc(pd_hi, 1)
            split_hi(BLK["poolw"] + AHEAD)
            for g in range(4):
                act.wait_ge(acc_ready, RES["poolw"] + g + 1)
                act.activation(part[1][:, 4 + g, :], bank[(RES["poolw"] + g) % BANKS][:], ACT.Identity,
                               scale=pool_gain[:, g:g + 1]).then_inc(ev_hi, 1)
            for n in range(DT):
                split_hi(BLK["out1"] + n + AHEAD)
                act.wait_ge(acc_free, RES["out1"] + n + 1)
                residual(SQ["f2"], n, 2, part[0])

            ffn(2, part[1])

            def rope_hi(act, i):
                act.wait_ge(r_full, i + 1)
                act.copy(part[1][:, i, :], rope_c[:, i % 2, :]).then_inc(r_hi, 1)

            act.wait_ge(x_new, DT)
            act.dma_start(x_spill[0], x[:]).then_inc(x_spilled, 16)
            norm_std("m2")
            act.wait_ge(rcol_ready, 1)
            act.activation(std_col[:, TT:2 * TT], r_col[:, 3 * TT:4 * TT], ACT.Sqrt, scale=1.0 / D, bias=eps_col[:]).then_inc(std_ready, 1)
            norm_copy("m2", rstd)
            norm_copy("m2", rstd_fin, 1)
            split_hi(BLK["gate"] + AHEAD)
            act.wait_ge(acc_free, RES["gate"] + 1)
            act.activation(scan[:, 2, 0:S], scan[:, 4, 0:S], ACT.Abs, bias=gate_b[0:MH, 1:2]).then_inc(g_abs, 1)
            act.wait_ge(g_abs, 1)
            act.activation(scan[:, 2, 0:S], scan[:, 2, 0:S], ACT.Exp, scale=-1.0).then_inc(g_exp, 1)
            act.wait_ge(g_exp, 1)
            act.activation(scan[:, 2, 0:S], scan[:, 2, 0:S], ACT.Ln, bias=1.0).then_inc(g_ln, 1)
            for i in range(8):
                split_hi(BLK["dqk"] + i + AHEAD)
                if i >= 2:
                    rope_hi(act, i - 2)
            for i in range(6, 8):
                rope_hi(act, i)
            for i in range(4):
                split_hi(BLK["dv"] + i + AHEAD)
            for i in range(TT):
                act.wait_ge(acc_ready, RES["dv"] + i + 1)
                act.activation(part[2][:, i, :], bank[(RES["dv"] + i) % BANKS][:], ACT.Identity,
                               scale=r_col[:, TT + i:TT + i + 1]).then_inc(ev_hi, 1)

            def d_expo(u):
                n = (u // 2 % TT + 1) * P
                act.wait_ge(e_biased, u + 1)
                if u >= 6:
                    act.wait_ge(e_turned, u // 2 - 2)
                act.activation(d_p[:, u % 6, 0:n], d_s[:, u % 2, 0:n], ACT.Exp, scale=-1.0,
                               bias=d_min[:, u:u + 1], accum_out=d_sum[:, u:u + 1]).then_inc(e_exp, 1)

            def d_square(h):
                act.wait_ge(e_out, h + 1)
                if h >= 1:
                    act.wait_ge(e_stat, h)
                act.activation(d_sq[:], bank[h % 2][:], ACT.Square).then_inc(e_sq, 1)

            for w in range(4 * DH + 8):
                if w < 4 * DH:
                    if w % 2 == 0:
                        split_hi(BLK["mqk"] + w // 2 + AHEAD)
                    d_expo(2 * w)
                    d_expo(2 * w + 1)
                if 2 <= w < 4 * DH + 2:
                    turned_hi(w - 2, e_turned, e_thi, e_out)
                if w >= 11 and (w - 11) % TT == 0:
                    d_square((w - 11) // TT)
            act.wait_ge(e_stat, DH)
            act.activation(head_r2[:], bank[2][0:DH, :], ACT.Sqrt, scale=1.0 / P, bias=eps_col[0:DH]).then_inc(e_std, 1)
            for i in range(2):
                split_hi(BLK["mv"] + i + AHEAD)
            for i in range(4):
                act.wait_ge(c_sum, i + 1)
                act.activation(c_acc[:, i, :], c_acc[:, i, :], ACT.Silu).then_inc(c_act, 1)
            for i in range(4):
                act.wait_ge(c_act, i + 1)
                act.activation(part[1][:, 8 + i, :], c_acc[:, i, :], ACT.Copy, scale=0.125 if i < 2 else 1.0).then_inc(c_hi, 1)
            for h in range(DH):
                act.wait_ge(e_full, h + 1)
                act.copy(part[1][:, 4 + h, :], d_full[:, h % 2, :]).then_inc(e_hi, 1)
            for i in range(2, 4):
                split_hi(BLK["mv"] + i + AHEAD)
            act.wait_ge(acc_free, RES["mo"] + 4)
            for i in range(4):
                act.activation(sig[:, i, :], sig[:, i, :], ACT.Sigmoid).then_inc(mo_sig, 1)
            for i in range(TT):
                act.wait_ge(acc_ready, RES["mv"] + i + 1)
                act.activation(part[2][:, i, :], bank[(RES["mv"] + i) % BANKS][:], ACT.Identity,
                               scale=r_col[:, TT + i:TT + i + 1]).then_inc(ev_hi, 1)

            def m_expo(u):
                h, k = divmod(u, TT)
                act.wait_ge(m_diag, h + 1)
                if u >= 3:
                    act.wait_ge(m_plo, u - 2)
                last = act.activation(m_e[:, u % 3, 0:P], m_dm[:, k, :], ACT.Exp, bias=a_col[:, k, h:h + 1])
                if k < TT - 1:
                    last = act.activation(m_e[:, u % 3, P:S - k * P], bank[2][:, (k + 1) * P:], ACT.Exp, bias=a_col[:, k, h:h + 1])
                last.then_inc(m_exp, 1)

            def m_high(u):
                h, k = divmod(u, TT)
                act.wait_ge(m_prod, u + 1)
                if h >= 1:
                    act.wait_ge(m_pv, u - 3)
                act.copy(part[2][:, 8 + k, k * P:], m_e[:, u % 3, 0:S - k * P]).then_inc(m_phi, 1)

            def m_head(h):
                act.wait_ge(m_bc, 2 * h + 2)
                if h >= 1:
                    act.wait_ge(m_dn, h)
                act.activation(m_eg[:], bank[3][:], ACT.Exp).then_inc(m_egr, 1)
                act.wait_ge(m_pv, TT * (h + 1))
                if h >= 1:
                    act.wait_ge(m_stat, h)
                act.activation(m_sq[:], bank[h % 2][:], ACT.Square, scale=float(P) ** -0.5).then_inc(m_nsq, 1)

            def m_den_square(h):
                act.wait_ge(m_dn, h + 1)
                act.activation(m_den[:], m_den[:], ACT.Square, scale=(EPS / P) ** 0.5).then_inc(m_dsq, 1)

            m_expo(0)
            for u in range(MH * TT + 2):
                if u + 1 < MH * TT:
                    m_expo(u + 1)
                if u < MH * TT:
                    m_high(u)
                if u >= 4 and (u - 4) % TT == 0:
                    m_head((u - 4) // TT)
                if u >= 5 and (u - 5) % TT == 0:
                    m_den_square((u - 5) // TT)
            act.wait_ge(m_stat, MH)
            act.activation(head_r2[:], bank[7][0:MH, :], ACT.Sqrt).then_inc(m_std, 1)
            split_hi(BLK["out2"] + AHEAD)
            for h in range(MH):
                act.wait_ge(m_norm, h + 1)
                act.copy(part[0][:, h, :], m_full[:, h % 2, :]).then_inc(m_hi, 1)
            act.wait_ge(x_spilled, 16)
            act.dma_start(x[:], x_spill[0]).then_inc(x_returned, 16)

            for n in range(DT):
                if n > 0:
                    split_hi(BLK["out2"] + n + AHEAD)
                act.wait_ge(acc_free, RES["out2"] + n + 1)
                square(SQ["post1"] + n, mixed[:, n, :])
            head("post1")()
            for n in range(DT):
                act.wait_ge(x_new, DT + n + 1)
                residual(SQ["f3"], n, 6, part[1])
            act.dma_start(x_spill[1], x[:]).then_inc(x_spilled, 16)

            up("f3_up0", part[0], False, head("f3"))
            down("f3_dn0", 2)
            up("f3_up1", part[0], False)
            def last(n):
                if n == 0:
                    act.wait_ge(acc_ready, RES["f3_dn1"] + 1)
                    act.wait_ge(x_spilled, 32)
                    act.dma_start(x_back, x_spill[1]).then_inc(x_returned, 16)
                act.wait_ge(acc_free, RES["f3_dn1"] + n + 1)
                square(SQ["post2"] + n, x[:, n, :])
            down("f3_dn1", 2, last)
            head("post2")()
            for n in range(DT):
                act.wait_ge(acc_ready, RES["final"] + n + 1)
                act.copy(out_tok[:, :, n * P:(n + 1) * P],
                         bank[(RES["final"] + n) % BANKS][:].rearrange("p (t d) -> p t d", t=TT)).then_inc(y_final, 1)

        @block.vector
        def _(dve):
            chained = [0]

            def link(ins):
                chained[0] += 1
                ins.then_inc(v1, 1)
                dve.wait_ge(v1, chained[0])

            def split_lo(b, it=None, step=0):
                if it is None:
                    if b >= NBLK:
                        return
                    dve.wait_ge(w_hi, b + 1)
                else:
                    dve.wait_ge(w_hi, it * step + (b + 1))
                for piece in block_parts(b, it):
                    last = dve.tensor_tensor(piece(w_low[b % RING]), piece(w_raw[b % RING]), piece(w_high[b % RING]).bitcast(F32),
                                             ALU.subtract)
                last.then_inc(w_lo, 1)

            def result(r):
                dve.wait_ge(acc_ready, r + 1)
                return bank[r % BANKS]

            def residual_lo(gen, n, g, dst):
                dve.wait_ge(xt_hi, GEN[gen] + n + 1)
                dve.scalar_tensor_tensor(dst[:, 8 + n, :], x[:, n, :], gains[:, g, n:n + 1], dst[:, n, :].bitcast(F32),
                                         ALU.mult, ALU.subtract).then_inc(xt_lo, 1)

            def norm_spread(col, n_diag):
                if n_diag > 0:
                    dve.wait_ge(bc_ready, n_diag)
                for i in range(TT):
                    last = dve.tensor_scalar(diag[:, i, :], CI(C_IDENT), r_col[:, col + i:col + i + 1], None, ALU.mult)
                last.then_inc(diag_ready, 1)

            def norm(name):
                dve.wait_ge(std_ready, SPREAD[name] + 1)
                link(dve.reciprocal(r_col[:, 0:TT], std_col[:, 0:TT]))
                norm_spread(0, SPREAD[name])
                dve.wait_ge(rstd_ready, SPREAD[name] + 1)

            def up(name, dst, gated, head=None):
                per = 2 if gated else 4
                tiles = FT - HALF if (gated and name.endswith("1")) else HALF
                def turn(it):
                    for j in range(per):
                        c = HID[name] + j
                        val = lambda n: n if it is None else it * per + n
                        rval = lambda n: n if it is None else it * BANKS + n
                        def nxt(q):
                            b = BLK[name] + q + AHEAD
                            split_lo(b) if it is None else split_lo(b, it, RING)
                        idx = j if it is None else it * per + j
                        place = dst[:, idx, :] if it is None else dst[:, bass.ds(idx, 1), :]
                        if gated:
                            r = RES[name] + 2 * j
                            dve.wait_ge(acc_ready, rval(r + 1))
                            dve.tensor_tensor(ff_z[:, j % 2, :], bank[r % BANKS][:], rstd[:], ALU.mult).then_inc(z_ready, 1)
                            nxt(2 * j)
                            dve.wait_ge(acc_ready, rval(r + 2))
                            dve.tensor_tensor(ff_u[:, j % 2, :], bank[(r + 1) % BANKS][:], rstd[:], ALU.mult).then_inc(acc_free, 2)
                            dve.wait_ge(acc_free, rval(r + 2))
                            dve.wait_ge(s_ready, val(c + 1))
                            dve.tensor_tensor(ff_t[:, j % 2, :], ff_s[:, j % 2, :], ff_u[:, j % 2, :], ALU.mult).then_inc(t_ready, 1)
                            nxt(2 * j + 1)
                        else:
                            r = RES[name] + j
                            nxt(j)
                            dve.wait_ge(acc_ready, rval(r + 1))
                            dve.scalar_tensor_tensor(ff_z[:, j % 2, :], bank[r % BANKS][:], 0.0, rstd[:],
                                                     ALU.max, ALU.mult).then_inc(acc_free, 1)
                        dve.wait_ge(hid_hi, val(c + 1))
                        dve.tensor_tensor(low_of(dst, place, idx, it), ff_t[:, j % 2, :], place.bitcast(F32), ALU.subtract).then_inc(hid_done, 1)
                low_of = lambda d, place, idx, it: part[2][:, idx, :] if it is None else part[2][:, bass.ds(idx, 1), :]
                if head is not None:
                    head()
                    turn(None)
                with dve.Fori(0 if head is None else 1, tiles // per) as it:
                    turn(it)

            def down(name, blocks, each):
                for n in range(DT):
                    r = RES[name] + n
                    b = BLK[name] + n * blocks + AHEAD
                    if blocks == 2:
                        split_lo(b)
                    acc = result(r)
                    each(n, acc)
                    split_lo(b + blocks - 1)

            def add_half(n, acc):
                dve.scalar_tensor_tensor(x[:, n, :], acc[:], 0.5, x[:, n, :], ALU.mult, ALU.add).then_inc(acc_free, 1)

            dve.memset(eps_col[:], EPS).then_inc(consts_made, 1)
            dve.memset(r_col[:], 0.0).then_inc(consts_made, 1)
            dve.wait_ge(rel_in, 16)
            dve.wait_ge(x_in, 32)
            dve.tensor_scalar(rel_rows[:, 257:384], CI(C_ONES, 127, HEADS), rel_rows[:, 256:257], None, ALU.mult).then_inc(rel_padded, 1)
            for n in range(DT):
                acc = result(RES["input"] + n)
                dve.tensor_copy(x[:, n, :], acc[:]).then_inc(acc_free, 1)
                if n >= 1:
                    residual_lo("f1", n - 1, 0, part[0])
                if n in (1, 2):
                    split_lo(n - 1)
            residual_lo("f1", DT - 1, 0, part[0])
            dve.wait_ge(small_in, 16 * len(SMALL))
            for i in range(2):
                last = dve.tensor_tensor(lam_pr[0:64, i:i + 1], lam_in[0:64, 2 * i:2 * i + 1],
                                         lam_in[0:64, 2 * i + 1:2 * i + 2], ALU.mult)
            last.then_inc(lam_made, 1)
            link(dve.tensor_scalar(qk_gain[:, 0:1], qk_gain[:, 0:1], -0.125, None, ALU.mult))
            link(dve.tensor_scalar(far[:], far[:], -1.0, None, ALU.mult))
            link(dve.tensor_scalar(diff_gain[:], diff_gain[:], 1.0 - LAM_INIT, None, ALU.mult))
            dve.wait_ge(ev_hi, 2)
            link(dve.tensor_tensor(neg_lam[:], lam_ex[:, 1:2], lam_ex[:, 0:1], ALU.subtract))
            link(dve.tensor_scalar(neg_lam[:], neg_lam[:], -LAM_INIT, None, ALU.add))

            def ffn(f, hid):
                up(f"f{f}_up0", hid, True, lambda: norm(f"f{f}"))
                down(f"f{f}_dn0", 2, add_half)
                up(f"f{f}_up1", hid, True)
                def one(n, acc):
                    add_half(n, acc)
                    residual_lo("m1", n, 1, part[0])
                def two(n, acc):
                    dve.scalar_tensor_tensor(y_tmp[:, n % 2, :], acc[:], 0.5, x[:, n, :], ALU.mult, ALU.add).then_inc(acc_free, 1)
                    dve.wait_ge(acc_free, RES["f2_dn1"] + n + 1)
                    dve.tensor_scalar(x[:, n, :], y_tmp[:, n % 2, :], gains[:, 3, n:n + 1], None, ALU.mult).then_inc(x_new, 1)
                    residual_lo("m2", n, 4, part[0])
                down(f"f{f}_dn1", 1, one if f == 1 else two)

            ffn(1, part[1])

            norm("m1")
            for g in range(4):
                dve.memset(u_pad[:, g, 0:PAD], 0.0)
            dve.memset(win[:, 0, 0:PAD], 0.0)
            dve.memset(win[:, 1, 0:PAD], 0.0).then_inc(pads_zero, 1)
            for i in range(8):
                acc = result(RES["qk"] + i)
                dve.tensor_tensor(qk_raw[:, i, :], acc[:], rstd[:], ALU.mult).then_inc(acc_free, 1)
                split_lo(BLK["qk"] + i + AHEAD)
            def values_lo(name, col, seen):
                for i in range(TT):
                    acc = result(RES[name] + i)
                    dve.wait_ge(ev_hi, seen + i + 1)
                    dve.scalar_tensor_tensor(part[2][:, 4 + i, :], acc[:], r_col[:, col + i:col + i + 1],
                                             part[2][:, i, :].bitcast(F32), ALU.mult, ALU.subtract).then_inc(acc_free, 1)
            for i in range(3):
                split_lo(BLK["v"] + i + AHEAD)
            dve.wait_ge(h_std, 1)
            dve.reciprocal(head_r[:], head_r[:]).then_inc(h_rec, 1)
            def qk_norm_lo(i):
                dve.wait_ge(qk_hi, i + 1)
                dve.tensor_tensor(part[1][:, 8 + i, :], qk_full[:, i % 2, :], part[1][:, i, :].bitcast(F32),
                                  ALU.subtract).then_inc(qk_lo, 1)
            for i in range(8):
                dve.wait_ge(h_bc, i + 1)
                if i >= 2:
                    dve.wait_ge(qk_lo, i - 1)
                dve.scalar_tensor_tensor(qk_full[:, i % 2, :], qk_raw[:, i, :], qk_gain[:, i // 4:i // 4 + 1],
                                         bank[6 + i % 2][:], ALU.mult, ALU.mult).then_inc(qk_full_ready, 1)
                if i == 0:
                    split_lo(BLK["v"] + 3 + AHEAD)
                else:
                    qk_norm_lo(i - 1)
            qk_norm_lo(7)
            values_lo("v", 0, 2)

            def a_bias(h):
                dve.wait_ge(b_mm, h + 1)
                o = bias[:, h % 2, :]
                dve.tensor_scalar(o[:, 0:256], const[:, C_ONES:C_ONES + 1].broadcast_to([P, 256]), far[:, h:h + 1], None, ALU.mult)
                dve.tensor_copy(o[0:64, 256:448], bank[2][0:64, 0:192])
                dve.tensor_copy(o[64:128, 256:512], bank[2][64:128, 0:256]).then_inc(b_done, 1)

            def a_min_of(u):
                h, q = divmod(u, TT)
                n = (q + 1) * P
                dve.wait_ge(a_score, u + 1)
                if q == 0:
                    dve.wait_ge(b_done, h + 1)
                if u >= 2:
                    dve.wait_ge(a_exp, u - 1)
                dve.tensor_tensor_reduce(out=a_s[:, u % 2, 0:n], in0=bank[4 + u % 2][:, 0:n],
                                         in1=bias[:, h % 2, S - n:S], scale=1.0, scalar=3e38, op0=ALU.add,
                                         op1=ALU.min, accum_out=a_min[:, u:u + 1]).then_inc(a_biased, 1)

            def a_normal(u):
                n = (u % TT + 1) * P
                dve.wait_ge(a_exp, u + 1)
                link(dve.reciprocal(a_rec[:, u:u + 1], a_sum[:, u:u + 1]))
                dve.tensor_scalar(a_p[:, u % 3, 0:n], a_p[:, u % 3, 0:n], a_rec[:, u:u + 1], None, ALU.mult).then_inc(a_prob, 1)

            def turned_lo(u, hi_sem, lo_sem):
                h, q = divmod(u, TT)
                dve.wait_ge(hi_sem, u + 1)
                dve.tensor_tensor(turned_unit(h, q, 1),
                                  bank[6 + u % 2][:, 0:(q + 1) * P].rearrange("p (k n) -> p k n", n=P),
                                  turned_unit(h, q, 0).bitcast(F32), ALU.subtract).then_inc(lo_sem, 1)

            def a_head_lo(h):
                r = 64 * (h % 2)
                dve.wait_ge(a_ohi, h + 1)
                dve.tensor_tensor(part[1][r:r + 64, 8 + h // 2, :], bank[h % 2][r:r + 64, :],
                                  part[1][r:r + 64, h // 2, :].bitcast(F32), ALU.subtract).then_inc(a_olo, 1)

            for s_ in range(2):
                link(dve.memset(bias[0:64, s_, 448:512], BIG))
            for h in range(2):
                a_bias(h)
            for u in range(4 * HEADS + 8):
                if u < 4 * HEADS:
                    a_min_of(u)
                    if u % TT == 3 and 2 <= u // TT + 1 < HEADS:
                        a_bias(u // TT + 1)
                if 1 <= u < 4 * HEADS + 1:
                    a_normal(u - 1)
                if 3 <= u < 4 * HEADS + 3:
                    turned_lo(u - 3, a_thi, a_tlo)
                if u >= 11 and (u - 11) % TT == 0:
                    a_head_lo((u - 11) // TT)
                if u < 4 * HEADS and u % 8 == 4:
                    split_lo(BLK["u"] + u // 8 + AHEAD)
                if u < 4 * HEADS and u % 8 == 7:
                    i = u // 8
                    dve.wait_ge(acc_ready, RES["u"] + i + 1)
                    dve.tensor_tensor(u_pad[:, i, PAD:], bank[3][:], rstd[:], ALU.mult).then_inc(acc_free, 1)
            for g in range(4):
                dve.wait_ge(pd_hi, g + 1)
                dve.tensor_tensor(part[1][:, 12 + g, :], u_pad[:, g, PAD:], part[1][:, 4 + g, :].bitcast(F32),
                                  ALU.subtract).then_inc(pd_lo, 1)
            split_lo(BLK["poolw"] + AHEAD)
            for g in range(4):
                acc = result(RES["poolw"] + g)
                dve.wait_ge(ev_hi, 2 + TT + g + 1)
                dve.scalar_tensor_tensor(part[1][:, 12 + g, :], acc[:], pool_gain[:, g:g + 1], part[1][:, 4 + g, :].bitcast(F32),
                                         ALU.mult, ALU.subtract).then_inc(acc_free, 1)
            for n in range(DT):
                acc = result(RES["out1"] + n)
                dve.tensor_tensor(x[:, n, :], acc[:], x[:, n, :], ALU.add).then_inc(acc_free, 1)
                residual_lo("f2", n, 2, part[0])
                split_lo(BLK["out1"] + n + AHEAD)

            ffn(2, part[1])

            dve.wait_ge(std_ready, SPREAD["m2"] + 1)
            link(dve.reciprocal(r_col[:, 0:TT], std_col[:, 0:TT]))
            link(dve.tensor_tensor(r_col[:, 2 * TT:3 * TT], r_col[:, 0:TT], r_col[:, 0:TT], ALU.mult))
            dve.tensor_tensor(r_col[:, 3 * TT:4 * TT], bank[4][:, TT:2 * TT], r_col[:, 2 * TT:3 * TT], ALU.mult).then_inc(rcol_ready, 1)
            dve.wait_ge(std_ready, SPREAD["m2"] + 2)
            link(dve.reciprocal(r_col[:, 2 * TT:3 * TT], std_col[:, TT:2 * TT]))
            link(dve.tensor_tensor(r_col[:, TT:2 * TT], r_col[:, 0:TT], r_col[:, 2 * TT:3 * TT], ALU.mult))
            norm_spread(TT, SPREAD["m2"])
            norm_spread(0, SPREAD["m2"] + 1)
            dve.wait_ge(rstd_ready, SPREAD["m2"] + 1)

            acc = result(RES["gate"])
            dve.memset(scan[:, 1, :], 0.0)
            dve.tensor_tensor(scan[:, 3, :], acc[0:MH, :], rstd[0:MH, :], ALU.mult)
            dve.tensor_tensor(scan[:, 4, :], acc[32:32 + MH, :], rstd[32:32 + MH, :], ALU.mult).then_inc(acc_free, 1)
            dve.wait_ge(acc_free, RES["gate"] + 1)
            link(dve.tensor_scalar(scan[:, 0, :], scan[:, 4, :], gate_b[0:MH, 1:2], 0.0, ALU.add, ALU.min))
            split_lo(BLK["gate"] + AHEAD)

            def gate_rows():
                dve.wait_ge(g_ln, 1)
                link(dve.tensor_tensor(scan[:, 0, :], scan[:, 0, :], scan[:, 2, :], ALU.subtract))
                link(dve.tensor_tensor_scan(scan[:, 4, :], scan[:, 0, :], scan[:, 1, :], 0.0, ALU.add, ALU.min))
                link(dve.scalar_tensor_tensor(scan[:, 2, :], scan[:, 3, :], gate_b[0:MH, 0:1], scan[:, 4, :], ALU.add, ALU.subtract))
                link(dve.tensor_tensor_scan(scan[:, 0, :], scan[:, 2, :], scan[:, 1, :], 0.0, ALU.max, ALU.max))
                link(dve.tensor_scalar(rows[0:MH, :], scan[:, 0, :], -1.0, None, ALU.mult))
                dve.tensor_tensor(rows[32:32 + MH, :], rows[0:MH, :], scan[:, 4, :], ALU.subtract).then_inc(g_rows, 1)

            dve.wait_ge(rope_in_sem, 16)

            def rope_in(i):
                acc = result(RES["dqk"] + i)
                dve.scalar_tensor_tensor(rope_y[:, i % 4, :], acc[:], -0.125 if i < 4 else 1.0, rstd[:], ALU.mult, ALU.mult).then_inc(acc_free, 1)

            def rope_sum(i):
                dve.wait_ge(r_perm, i + 1)
                link(dve.tensor_tensor(rope_s[:, i % 2, :], bank[6 + i % 2][:], const[:, C_SIN:C_SIN + S], ALU.mult))
                dve.wait_ge(r_cos, i + 1)
                dve.tensor_tensor(rope_c[:, i % 2, :], rope_c[:, i % 2, :], rope_s[:, i % 2, :], ALU.add).then_inc(r_full, 1)
                dve.wait_ge(r_hi, i + 1)
                dve.tensor_tensor(part[1][:, 8 + i, :], rope_c[:, i % 2, :], part[1][:, i, :].bitcast(F32), ALU.subtract).then_inc(r_lo, 1)

            for i in range(8):
                split_lo(BLK["dqk"] + i + AHEAD)
                rope_in(i)
                if i >= 2:
                    rope_sum(i - 2)
                if i == 3:
                    gate_rows()
            for i in range(6, 8):
                rope_sum(i)
            for i in range(3):
                split_lo(BLK["dv"] + i + AHEAD)
            dve.wait_ge(g_turn, 1)
            dve.tensor_copy(a_col[:].rearrange("p t h -> p (t h)"), bank[5][:, 0:TT * MH]).then_inc(g_cols, 1)
            split_lo(BLK["dv"] + 3 + AHEAD)
            values_lo("dv", TT, 2 + TT + 4)

            link(dve.memset(d_mask[:, 0:S - P], 0.0))
            link(dve.tensor_copy(d_mask[:, S - P:], CI(C_CAUSAL)))

            def d_min_of(u):
                n = (u // 2 % TT + 1) * P
                dve.wait_ge(e_score, u + 1)
                if u >= 2:
                    dve.wait_ge(e_exp, u - 1)
                dve.tensor_tensor_reduce(out=d_s[:, u % 2, 0:n], in0=bank[4 + u % 2][:, 0:n],
                                         in1=d_mask[:, S - n:S], scale=1.0, scalar=3e38, op0=ALU.add,
                                         op1=ALU.min, accum_out=d_min[:, u:u + 1]).then_inc(e_biased, 1)

            def d_combine(w):
                n = (w % TT + 1) * P
                p0, p1 = d_p[:, 2 * w % 6, 0:n], d_p[:, 2 * w % 6 + 1, 0:n]
                dve.wait_ge(e_exp, 2 * w + 2)
                link(dve.reciprocal(d_rec[:, 2 * w:2 * w + 2], d_sum[:, 2 * w:2 * w + 2]))
                link(dve.tensor_scalar(d_lam[:, w % 16:w % 16 + 1], d_rec[:, 2 * w + 1:2 * w + 2], neg_lam[:], None, ALU.mult))
                link(dve.tensor_scalar(p0, p0, d_rec[:, 2 * w:2 * w + 1], None, ALU.mult))
                dve.scalar_tensor_tensor(p0, p1, d_lam[:, w % 16:w % 16 + 1], p0, ALU.mult, ALU.add).then_inc(e_prob, 1)

            def d_copy(h):
                dve.wait_ge(e_sq, h + 1)
                dve.tensor_copy(o_diff[:, h, :], bank[h % 2][:]).then_inc(e_copied, 1)

            def convolve(i):
                o, y = c_acc[:, i, :], mqk_raw[:, i, :]
                link(dve.tensor_scalar(o, y, conv_w[:, CONV - 1, i:i + 1], conv_b[:, i:i + 1], ALU.mult, ALU.add))
                for back in range(1, CONV):
                    ins = dve.scalar_tensor_tensor(o[:, back:], y[:, 0:S - back], conv_w[:, CONV - 1 - back, i:i + 1], o[:, back:], ALU.mult, ALU.add)
                    if back < CONV - 1:
                        link(ins)
                ins.then_inc(c_sum, 1)

            dve.wait_ge(x_spilled, 16)
            for w in range(4 * DH + 8):
                if w < 4 * DH:
                    d_min_of(2 * w)
                    d_min_of(2 * w + 1)
                    if w % 2 == 0:
                        split_lo(BLK["mqk"] + w // 2 + AHEAD)
                if 1 <= w <= 4 * DH:
                    d_combine(w - 1)
                if 3 <= w < 4 * DH + 3:
                    turned_lo(w - 3, e_thi, e_tlo)
                if w >= 11 and (w - 11) % TT == 0:
                    d_copy((w - 11) // TT)
                if w < 4 * DH and w % 2 == 1:
                    i = w // 2
                    dve.wait_ge(acc_ready, RES["mqk"] + i + 1)
                    dve.tensor_tensor(x[:, i, :], bank[3][:], rstd[:], ALU.mult).then_inc(acc_free, 1)
                if w in (2, 4, 6, 8):
                    dve.wait_ge(acc_free, RES["mqk"] + w // 2)
                    convolve(w // 2 - 1)
            dve.wait_ge(e_std, 1)
            dve.reciprocal(head_r2[:], head_r2[:]).then_inc(e_rec, 1)
            for i in range(2):
                split_lo(BLK["mv"] + i + AHEAD)
            for h in range(DH):
                dve.wait_ge(e_bc, h + 1)
                if h >= 2:
                    dve.wait_ge(e_lo, h - 1)
                dve.scalar_tensor_tensor(d_full[:, h % 2, :], o_diff[:, h, :], diff_gain[:], bank[4 + h % 2][:],
                                         ALU.mult, ALU.mult).then_inc(e_full, 1)
                dve.wait_ge(e_hi, h + 1)
                dve.tensor_tensor(part[1][:, 12 + h, :], d_full[:, h % 2, :], part[1][:, 4 + h, :].bitcast(F32),
                                  ALU.subtract).then_inc(e_lo, 1)
            for i in range(4):
                dve.wait_ge(c_hi, i + 1)
                dve.scalar_tensor_tensor(part[1][:, i, :], c_acc[:, i, :], 0.125 if i < 2 else 1.0,
                                         part[1][:, 8 + i, :].bitcast(F32), ALU.mult, ALU.subtract).then_inc(c_lo, 1)
            for i in range(2, 4):
                split_lo(BLK["mv"] + i + AHEAD)
            values_lo("mv", TT, 2 + TT + 4 + TT)

            def m_diag_of(h):
                dve.wait_ge(m_bc, 2 * h + 1)
                dve.tensor_tensor(m_dm[:], bank[2][:].rearrange("p (k n) -> p k n", n=P),
                                  const[:, C_MASKT:C_MASKT + P].rearrange("p (a n) -> p a n", a=1).broadcast_to([P, TT, P]),
                                  ALU.add).then_inc(m_diag, 1)

            def m_weigh(u):
                n = S - u % TT * P
                dve.wait_ge(m_exp, u + 1)
                dve.wait_ge(m_score, u + 1)
                dve.tensor_tensor(m_e[:, u % 3, 0:n], m_e[:, u % 3, 0:n], bank[4 + u % 2][:, 0:n], ALU.mult).then_inc(m_prod, 1)

            def m_low(u):
                k = u % TT
                dve.wait_ge(m_phi, u + 1)
                dve.tensor_tensor(part[2][:, 12 + k, k * P:], m_e[:, u % 3, 0:S - k * P], part[2][:, 8 + k, k * P:].bitcast(F32),
                                  ALU.subtract).then_inc(m_plo, 1)

            def m_head(h):
                dve.wait_ge(m_pv, TT * (h + 1))
                dve.wait_ge(m_egr, h + 1)
                if h >= 1:
                    dve.wait_ge(m_sqs, h)
                link(dve.scalar_tensor_tensor(m_den[:], bank[6][:], -1.0, m_eg[:], ALU.mult, ALU.max))
                dve.tensor_tensor(m_den[:], bank[6][:], m_den[:], ALU.max).then_inc(m_dn, 1)
                dve.wait_ge(m_nsq, h + 1)
                dve.tensor_copy(m_num[:, h, :], bank[h % 2][:]).then_inc(m_ncp, 1)

            def m_sum(h):
                dve.wait_ge(m_nsq, h + 1)
                dve.wait_ge(m_dsq, h + 1)
                dve.tensor_tensor(m_sq[:], m_sq[:], m_den[:], ALU.add).then_inc(m_sqs, 1)

            m_diag_of(0)
            for u in range(MH * TT + 3):
                if u + 1 < MH * TT and u % TT == TT - 1:
                    m_diag_of(u // TT + 1)
                if u < MH * TT:
                    m_weigh(u)
                if 1 <= u <= MH * TT:
                    m_low(u - 1)
                if u >= 4 and (u - 4) % TT == 0:
                    m_head((u - 4) // TT)
                if u >= 6 and (u - 6) % TT == 0:
                    m_sum((u - 6) // TT)
            dve.wait_ge(m_std, 1)
            dve.reciprocal(head_r2[:], head_r2[:]).then_inc(m_rec, 1)
            split_lo(BLK["out2"] + AHEAD)
            for h in range(MH):
                dve.wait_ge(m_bcr, h + 1)
                if h >= 2:
                    dve.wait_ge(m_lo, h - 1)
                link(dve.scalar_tensor_tensor(m_full[:, h % 2, :], m_num[:, h, :], mlstm_gain[:, h:h + 1],
                                              bank[4 + h % 2][:], ALU.mult, ALU.mult))
                dve.wait_ge(mo_sig, h + 1)
                dve.tensor_tensor(m_full[:, h % 2, :], m_full[:, h % 2, :], sig[:, h, :], ALU.mult).then_inc(m_norm, 1)
                dve.wait_ge(m_hi, h + 1)
                dve.tensor_tensor(part[0][:, 8 + h, :], m_full[:, h % 2, :], part[0][:, h, :].bitcast(F32), ALU.subtract).then_inc(m_lo, 1)

            for n in range(DT):
                if n > 0:
                    split_lo(BLK["out2"] + n + AHEAD)
                acc = result(RES["out2"] + n)
                dve.tensor_copy(mixed[:, n, :], acc[:]).then_inc(acc_free, 1)
            norm("post1")
            for n in range(DT):
                link(dve.scalar_tensor_tensor(mixed[:, n, :], mixed[:, n, :], gains[:, 5, n:n + 1], rstd[:], ALU.mult, ALU.mult))
                if n == 0:
                    dve.wait_ge(x_unit, DT)
                dve.tensor_tensor(x[:, n, :], x[:, n, :], mixed[:, n, :], ALU.add).then_inc(x_new, 1)
                if n >= 1:
                    residual_lo("f3", n - 1, 6, part[1])
            residual_lo("f3", DT - 1, 6, part[1])

            up("f3_up0", part[0], False, lambda: norm("f3"))
            def first(n, acc):
                if n == 0:
                    dve.wait_ge(x_spilled, 32)
                dve.tensor_copy(x[:, n, :], acc[:]).then_inc(acc_free, 1)
            down("f3_dn0", 2, first)
            up("f3_up1", part[0], False)
            down("f3_dn1", 2, lambda n, acc: dve.tensor_tensor(x[:, n, :], acc[:], x[:, n, :], ALU.add).then_inc(acc_free, 1))
            norm("post2")
            dve.wait_ge(x_returned, 32)
            for n in range(DT):
                link(dve.scalar_tensor_tensor(x[:, n, :], x[:, n, :], gains[:, 7, n:n + 1], rstd[:], ALU.mult, ALU.mult))
                dve.tensor_tensor(x[:, n, :], x[:, n, :], x_back[:, n, :], ALU.add).then_inc(x_new, 1)

        @block.gpsimd
        def _(pool):
            stepped = [0]

            def link(ins):
                stepped[0] += 1
                ins.then_inc(pool_step, 1)
                pool.wait_ge(pool_step, stepped[0])

            def add_square(i, which, first):
                pool.wait_ge(sq_ready, i + 1)
                if first:
                    pool.tensor_copy(sq_sum[:, which, :], sq[:, i % 2, :]).then_inc(sq_added, 1)
                else:
                    pool.wait_ge(sq_added, i)
                    pool.tensor_tensor(sq_sum[:, which, :], sq_sum[:, which, :], sq[:, i % 2, :], ALU.add).then_inc(sq_added, 1)

            def sum_squares(name):
                if NORM[name]:
                    pool.wait_ge(stat_ready, NORM[name])
                for n in range(DT):
                    add_square(SQ[name] + n, 0, n == 0)

            sum_squares("f1")
            sum_squares("m1")
            for g in range(4):
                pool.wait_ge(acc_free, RES["u"] + g + 1)
                pool.wait_ge(pads_zero, 1)
                src = u_pad[:, g, :]
                for k in range(g + 1):
                    dst = win[:, k % 2, :]
                    link(pool.tensor_tensor(dst[:, PAD:], src[:, PAD:], src[:, PAD - 2 ** k:PAD - 2 ** k + S], ALU.add))
                    src = dst
                link(pool.tensor_tensor(src[:, PAD:2 * PAD], src[:, PAD:2 * PAD], const[:, C_POOL + 16 * g:C_POOL + 16 * (g + 1)], ALU.mult))
                link(pool.tensor_scalar(src[:, PAD:], src[:, PAD:], 0.5 ** (g + 1), None, ALU.mult))
                pool.tensor_tensor(u_pad[:, g, PAD:], src[:, PAD:], u_pad[:, g, PAD:], ALU.subtract).then_inc(pool_done, 1)
                pool.wait_ge(pool_done, g + 1)
            sum_squares("f2")
            pool.wait_ge(stat_ready, NORM["m2"])
            for n in range(DT):
                for which in range(2):
                    add_square(SQ["m2"] + 2 * n + which, which, n == 0)
            pool.wait_ge(rope_in_sem, 16)
            for i in range(8):
                pool.wait_ge(acc_free, RES["dqk"] + i + 1)
                if i >= 2:
                    pool.wait_ge(r_lo, i - 1)
                pool.tensor_tensor(rope_c[:, i % 2, :], rope_y[:, i % 4, :], const[:, C_COS:C_COS + S], ALU.mult).then_inc(r_cos, 1)
            pool.wait_ge(rstd_ready, SPREAD["m2"] + 2)
            pool.wait_ge(x_returned, 16)
            pool.wait_ge(stat_ready, NORM["post1"])
            for n in range(DT):
                pool.tensor_tensor(x[:, n, :], x[:, n, :], rstd_fin[:], ALU.mult).then_inc(x_unit, 1)
                add_square(SQ["post1"] + n, 0, n == 0)
            sum_squares("f3")
            sum_squares("post2")

        @block.tensor
        def _(pe):
            def parts(region, k):
                return part[region][:, k, :], part[region][:, 8 + k, :]

            def finish(mm):
                mm.then_inc(acc_ready, 1)

            def norm_stat(name, sums=1):
                pe.wait_ge(sq_added, SQ[name] + DT * sums)
                for s_ in range(sums):
                    for i in range(TT):
                        mm = pe.matmul(bank[4][:, s_ * TT + i:s_ * TT + i + 1], sq_sum[:, s_, i * P:(i + 1) * P],
                                       const[:, C_ONES:C_ONES + 1], start=True, stop=True)
                mm.then_inc(stat_ready, 1)

            def norm_spread(name, extra=0):
                n = SPREAD[name] + extra
                pe.wait_ge(diag_ready, n + 1)
                if n > 0:
                    pe.wait_ge(rstd_ready, n)
                for i in range(TT):
                    mm = pe.matmul(bank[5][:, i * P:(i + 1) * P], CI(C_ONES), diag[:, i, :], start=True, stop=True)
                mm.then_inc(bc_ready, 1)

            def tile(b, r, src, k0=0, nk=8, skip=0, start=True, stop=True, need=None, order=None, m=P, very_first=False):
                hi, lo = w_tiles(b)
                order = order or list(range(nk))
                for k in order:
                    if need is not None:
                        need(k0 + k)
                    x_hi, x_lo = src(k0 + k)
                    mm = split3(pe, bank[r % BANKS][0:m, :], hi[:, skip + k, 0:m], lo[:, skip + k, 0:m], x_hi, x_lo,
                                start and k == order[0], stop and k == order[-1], k == order[0] and not very_first)
                return mm

            def up(name, src, gated, gen=None, after=()):
                tiles = 2 * (FT - HALF if name.endswith("1") else HALF) if gated else HALF
                def turn(it):
                    for q in range(RING):
                        b, r = BLK[name] + q, RES[name] + q
                        block_ready(pe, b, it, RING)
                        free_bank(pe, r, it, RING)
                        need = (lambda k: pe.wait_ge(xt_lo, GEN[gen] + k + 1)) if it is None and q == 0 else None
                        finish(tile(b, r, src, need=need, very_first=b == 0 and it is None))
                        if it is None and q < len(after):
                            after[q]()
                if gen is not None:
                    turn(None)
                with pe.Fori(0 if gen is None else 1, tiles // RING) as it:
                    turn(it)

            def down(name, blocks, hid, h0, tiles):
                def turn(it):
                    for j in range(BANKS):
                        r = RES[name] + j
                        free_bank(pe, r, it, BANKS)
                        for c in range(blocks):
                            b = BLK[name] + j * blocks + c
                            block_ready(pe, b, it, BANKS * blocks)
                            def need(k):
                                if k == 0:
                                    pe.wait_ge(hid_done, h0 + tiles - 2)
                                if k == tiles - 2:
                                    pe.wait_ge(hid_done, h0 + tiles)
                            nk = min(8, tiles - 8 * c)
                            mm = tile(b, r, lambda k: (part[hid][:, k, :], part[2][:, k, :]), 8 * c, nk, 8 - nk, c == 0, c == blocks - 1, need=need)
                        finish(mm)
                with pe.Fori(0, DT // BANKS) as it:
                    turn(it)

            def columns(name, n, src, after=None, need=None):
                for i in range(n):
                    block_ready(pe, BLK[name] + i)
                    free_bank(pe, RES[name] + i)
                    finish(tile(BLK[name] + i, RES[name] + i, src, need=need if i == 0 else None))
                    if after is not None:
                        after(i)

            def values(name, region, after=None):
                for j in range(4):
                    b = BLK[name] + j
                    block_ready(pe, b)
                    hi, lo = w_tiles(b, S)
                    for kk in range(2):
                        k = 2 * j + kk
                        x_hi, x_lo = parts(region, k)
                        for i in range(TT):
                            if k == 0:
                                free_bank(pe, RES[name] + i)
                            mm = split3(pe, bank[(RES[name] + i) % BANKS][:], x_hi[:, i * P:(i + 1) * P], x_lo[:, i * P:(i + 1) * P],
                                        hi[:, kk, :], lo[:, kk, :], k == 0, k == DT - 1, kk == 0 and i == 0)
                            if k == DT - 1:
                                finish(mm)
                    if after is not None:
                        after(j)

            pe.wait_ge(x_in, 32)
            for n in range(DT):
                free_bank(pe, RES["input"] + n)
                for i in range(TT):
                    mm = pe.transpose(bank[(RES["input"] + n) % BANKS][:, i * P:(i + 1) * P],
                                      x_tok[:, i, n * P:(n + 1) * P], CI(C_IDENT))
                finish(mm)
            def lam_sum():
                pe.wait_ge(lam_made, 1)
                pe.matmul(bank[5][:, 0:2], const[0:64, C_ONES:C_ONES + P], lam_pr[0:64, :], start=True, stop=True).then_inc(lam_summed, 1)
            lam_sum()

            def norm_steps(name):
                return (lambda: norm_stat(name), lambda: norm_spread(name))

            def ffn(f, region, hid):
                src = lambda k: parts(region, k)
                up(f"f{f}_up0", src, True, f"f{f}", norm_steps(f"f{f}"))
                down(f"f{f}_dn0", 2, hid, HID[f"f{f}_up0"], HALF)
                up(f"f{f}_up1", src, True)
                down(f"f{f}_dn1", 1, hid, HID[f"f{f}_up1"], FT - HALF)

            ffn(1, 0, 1)

            def head_stat(i):
                pe.wait_ge(y_sq, i + 1)
                pe.matmul(bank[4][0:16, :], const[:, C_HSUM + 16 * i:C_HSUM + 16 * (i + 1)], head_sq[:, i % 2, :],
                          start=(i == 0), stop=(i == 7)).then_inc(h_stat, 1)

            def after_qk(i):
                if i < 2:
                    norm_steps("m1")[i]()
                if i >= 3:
                    head_stat(i - 3)
            x_in1 = lambda k: parts(0, k)
            columns("qk", 8, x_in1, after_qk, need=lambda k: pe.wait_ge(xt_lo, GEN["m1"] + k + 1))
            def after_v(j):
                if j == 0:
                    for i in range(5, 8):
                        head_stat(i)
                if j == 1:
                    pe.wait_ge(h_rec, 1)
                for i in ((), (0, 1), (2, 3, 4), (5, 6, 7))[j]:
                    head_spread(i)
            def head_spread(i):
                if i >= 2:
                    pe.wait_ge(qk_full_ready, i - 1)
                pe.matmul(bank[6 + i % 2][:], const[0:16, C_HROW + P * i:C_HROW + P * (i + 1)], head_r[:],
                          start=True, stop=True).then_inc(h_bc, 1)
            values("v", 0, after_v)

            def side_steps(name, first, last, src):
                for step in range(first, last):
                    i, k = divmod(step, DT)
                    b = BLK[name] + i
                    hi, lo = w_tiles(b)
                    if k == 0:
                        block_ready(pe, b)
                        pe.wait_ge(acc_free, RES[name] + i)
                    x_hi, x_lo = src(k)
                    mm = split3(pe, bank[3][:], hi[:, k, :], lo[:, k, :], x_hi, x_lo, k == 0, k == DT - 1, k == 0)
                    if k == DT - 1:
                        finish(mm)

            def a_bias(h):
                pe.wait_ge(toep_in[h % 2], 16 * (h // 2 + 1))
                if h >= 1:
                    pe.wait_ge(b_done, h)
                pe.matmul(bank[2][:, 0:P], toep[:, h % 2, 1, :], CI(C_FLIP), start=True, stop=True)
                pe.matmul(bank[2][:, P:2 * P], toep[:, h % 2, 0, :], CI(C_FLIP), start=True, stop=True).then_inc(b_mm, 1)

            def a_scores(u):
                h, q = divmod(u, TT)
                n, r = (q + 1) * P, 64 * (h % 2)
                if u >= 2:
                    pe.wait_ge(a_biased, u - 1)
                rows_ = slice(r, r + 64)
                qt, kt = h // 2, 4 + h // 2
                split3(pe, bank[4 + u % 2][:, 0:n], part[1][rows_, qt, q * P:(q + 1) * P], part[1][rows_, 8 + qt, q * P:(q + 1) * P],
                       part[1][rows_, kt, 0:n], part[1][rows_, 8 + kt, 0:n], True, True).then_inc(a_score, 1)

            def turn_probs(u, probs, ready, lo_sem, done):
                h, q = divmod(u, TT)
                pe.wait_ge(ready, u + 1)
                if u >= 2:
                    pe.wait_ge(lo_sem, u - 1)
                for k in range(q + 1):
                    place = k if h % 2 == 0 else q - k
                    mm = pe.transpose(bank[6 + u % 2][:, place * P:(place + 1) * P], probs[:, k * P:(k + 1) * P], CI(C_IDENT))
                mm.then_inc(done, 1)

            def weigh_values(h, k, col, lo_sem, done, copied):
                if k == 0:
                    pe.wait_ge(lo_sem, TT * (h + 1))
                    if h >= 2:
                        pe.wait_ge(copied, h - 1)
                mm = split3(pe, bank[h % 2][:, k * P:], part[2][:, k, col:col + P], part[2][:, 4 + k, col:col + P],
                            turned_keys(h, k, 0), turned_keys(h, k, 1), k == 0, k == TT - 1)
                if k == TT - 1:
                    mm.then_inc(done, 1)

            pe.wait_ge(acc_free, RES["v"] + TT)
            for h in range(2):
                a_bias(h)
            pe.wait_ge(qk_lo, 8)
            for u in range(4 * HEADS + 8):
                if u < 4 * HEADS:
                    a_scores(u)
                    if u % 8 < 7:
                        side_steps("u", u + (u % 8 > 0), u + 2, x_in1)
                    if u % TT == 1 and 2 <= u // TT + 1 < HEADS:
                        a_bias(u // TT + 1)
                if 7 <= u < 4 * HEADS + 7:
                    h, k = divmod(u - 7, TT)
                    weigh_values(h, k, P * (h // 2), a_tlo, a_out, a_olo)
                if 2 <= u < 4 * HEADS + 2:
                    turn_probs(u - 2, a_p[:, (u - 2) % 3, :], a_prob, a_tlo, a_turned)
            pe.wait_ge(a_olo, HEADS)
            block_ready(pe, BLK["poolw"])
            hi, lo = w_tiles(BLK["poolw"])
            for g in range(4):
                free_bank(pe, RES["poolw"] + g)
                pe.wait_ge(pd_lo, g + 1)
                finish(split3(pe, bank[(RES["poolw"] + g) % BANKS][:], hi[:, g, :], lo[:, g, :], part[1][:, 4 + g, :],
                              part[1][:, 12 + g, :], True, True, g == 0))
            def mixed_in(k):
                if k >= 4:
                    pe.wait_ge(acc_free, RES["poolw"] + k - 3)
            columns("out1", 8, lambda k: parts(1, k), need=mixed_in)

            ffn(2, 0, 1)

            x_in2 = lambda k: parts(0, k)
            block_ready(pe, BLK["gate"])
            free_bank(pe, RES["gate"])
            finish(tile(BLK["gate"], RES["gate"], x_in2, need=lambda k: pe.wait_ge(xt_lo, GEN["m2"] + k + 1), m=36))
            norm_stat("m2", 2)

            def swap_halves(i):
                pe.wait_ge(acc_free, RES["dqk"] + i + 1)
                if i >= 2:
                    pe.wait_ge(r_full, i - 1)
                pe.matmul(bank[6 + i % 2][:], CI(C_SWAP), rope_y[:, i % 4, :], start=True, stop=True).then_inc(r_perm, 1)

            def after_dqk(i):
                if i == 0:
                    norm_spread("m2")
                    norm_spread("m2", 1)
                if i == 6:
                    pe.wait_ge(g_rows, 1)
                    pe.wait_ge(rstd_ready, SPREAD["m2"] + 2)
                    for j in range(TT):
                        mm = pe.transpose(bank[5][:, j * MH:(j + 1) * MH], scan[:, 2, j * P:(j + 1) * P], const[0:MH, C_IDENT:C_IDENT + MH])
                    mm.then_inc(g_turn, 1)
                if i >= 3:
                    swap_halves(i - 3)
            columns("dqk", 8, x_in2, after_dqk)
            def after_dv(j):
                for i in ((5, 6), (7,), (), ())[j]:
                    swap_halves(i)
            values("dv", 0, after_dv)

            def d_scores(u):
                w, c = divmod(u, 2)
                h, q = divmod(w, TT)
                n, rows_ = (q + 1) * P, slice(64 * c, 64 * c + 64)
                if u >= 2:
                    pe.wait_ge(e_biased, u - 1)
                split3(pe, bank[4 + u % 2][:, 0:n], part[1][rows_, h, q * P:(q + 1) * P], part[1][rows_, 8 + h, q * P:(q + 1) * P],
                       part[1][rows_, 4 + h, 0:n], part[1][rows_, 12 + h, 0:n], True, True).then_inc(e_score, 1)

            def d_stat(h):
                pe.wait_ge(e_sq, h + 1)
                pe.matmul(bank[2][0:DH, :], const[:, C_HOT + 4 * h:C_HOT + 4 * h + 4], d_sq[:], start=(h == 0),
                          stop=(h == DH - 1)).then_inc(e_stat, 1)

            pe.wait_ge(acc_free, RES["dv"] + 4)
            pe.wait_ge(r_lo, 8)
            for w in range(4 * DH + 8):
                if w < 4 * DH:
                    d_scores(2 * w)
                    d_scores(2 * w + 1)
                    side_steps("mqk", 4 * w, 4 * w + (4 if w % 2 else 2), x_in2)
                if 7 <= w < 4 * DH + 7:
                    h, k = divmod(w - 7, TT)
                    weigh_values(h, k, P * h, e_tlo, e_out, e_copied)
                if w < 4 * DH and w % 2 == 0:
                    side_steps("mqk", 4 * w + 2, 4 * w + 4, x_in2)
                if 2 <= w < 4 * DH + 2:
                    turn_probs(w - 2, d_p[:, 2 * (w - 2) % 6, :], e_prob, e_tlo, e_turned)
                if w >= 12 and (w - 12) % TT == 0:
                    d_stat((w - 12) // TT)
            d_stat(DH - 1)
            pe.wait_ge(e_copied, DH)
            pe.wait_ge(e_std, 1)

            def after_mv(j):
                if j == 1:
                    pe.wait_ge(e_rec, 1)
                for h in ((), (0, 1), (2, 3), ())[j]:
                    if h >= 2:
                        pe.wait_ge(e_full, h - 1)
                    pe.matmul(bank[4 + h % 2][:], const[0:DH, C_SEL4 + P * h:C_SEL4 + P * (h + 1)], head_r2[:],
                              start=True, stop=True).then_inc(e_bc, 1)
            values("mv", 0, after_mv)

            def m_spread_max(h):
                if h >= 1:
                    pe.wait_ge(m_exp, TT * h)
                pe.matmul(bank[2][:], const[0:MH, C_SEL4 + P * h:C_SEL4 + P * (h + 1)], rows[0:MH, :], start=True, stop=True).then_inc(m_bc, 1)

            def m_spread_sum(h):
                if h >= 1:
                    pe.wait_ge(m_egr, h)
                pe.matmul(bank[3][:], const[32:32 + MH, C_SEL4 + P * h:C_SEL4 + P * (h + 1)], rows[32:32 + MH, :], start=True, stop=True).then_inc(m_bc, 1)

            def m_scores(u):
                h, k = divmod(u, TT)
                rows_ = slice(64 * (h % 2), 64 * (h % 2) + 64)
                qt, kt = h // 2, 2 + h // 2
                if u >= 2:
                    pe.wait_ge(m_prod, u - 1)
                split3(pe, bank[4 + u % 2][:, 0:S - k * P], part[1][rows_, 8 + kt, k * P:(k + 1) * P], part[1][rows_, kt, k * P:(k + 1) * P],
                       part[1][rows_, 8 + qt, k * P:], part[1][rows_, qt, k * P:], True, True).then_inc(m_score, 1)

            def m_values(u):
                h, k = divmod(u, TT)
                pe.wait_ge(m_plo, u + 1)
                if k == 0 and h >= 2:
                    pe.wait_ge(m_ncp, h - 1)
                split3(pe, bank[h % 2][:, k * P:], part[2][:, k, P * h:P * (h + 1)], part[2][:, 4 + k, P * h:P * (h + 1)],
                       part[2][:, 8 + k, k * P:], part[2][:, 12 + k, k * P:], k == 0, k == TT - 1)
                if k == 0 and h >= 1:
                    pe.wait_ge(m_dn, h)
                pe.matmul(bank[6][:, k * P:], ones_r[:], part[2][:, 8 + k, k * P:], start=(k == 0), stop=False)
                pe.matmul(bank[6][:, k * P:], ones_r[:], part[2][:, 12 + k, k * P:], start=False, stop=(k == TT - 1)).then_inc(m_pv, 1)

            def m_stat_of(h):
                pe.wait_ge(m_sqs, h + 1)
                pe.matmul(bank[7][0:MH, :], const[:, C_HOT + 4 * h:C_HOT + 4 * h + 4], m_sq[:], start=(h == 0),
                          stop=(h == MH - 1)).then_inc(m_stat, 1)

            pe.wait_ge(acc_free, RES["mv"] + TT)
            pe.wait_ge(c_lo, 4)
            pe.wait_ge(e_full, DH)
            m_spread_max(0)
            for u in range(MH * TT + 4):
                if u < MH * TT:
                    m_scores(u)
                    if u % TT == 1:
                        m_spread_sum(u // TT)
                    if u % TT == 3 and u // TT + 1 < MH:
                        m_spread_max(u // TT + 1)
                if 1 <= u <= MH * TT:
                    m_values(u - 1)
                if u >= 7 and (u - 7) % TT == 0:
                    m_stat_of((u - 7) // TT)
            pe.wait_ge(m_rec, 1)
            for h in range(MH):
                if h >= 2:
                    pe.wait_ge(m_norm, h - 1)
                pe.matmul(bank[4 + h % 2][:], const[0:MH, C_SEL4 + P * h:C_SEL4 + P * (h + 1)], head_r2[:],
                          start=True, stop=True).then_inc(m_bcr, 1)

            def mix2(k):
                return (part[1][:, 4 + k, :], part[1][:, 12 + k, :]) if k < 4 else (part[0][:, k - 4, :], part[0][:, 4 + k, :])
            def mix2_in(k):
                if k < 4:
                    pe.wait_ge(e_lo, k + 1)
                else:
                    pe.wait_ge(m_lo, k - 3)
            columns("out2", 8, mix2, need=mix2_in)
            norm_stat("post1")
            norm_spread("post1")

            src = lambda k: parts(1, k)
            up("f3_up0", src, False, "f3", norm_steps("f3"))
            down("f3_dn0", 2, 0, HID["f3_up0"], HALF)
            up("f3_up1", src, False)
            down("f3_dn1", 2, 0, HID["f3_up1"], HALF)
            norm_stat("post2")
            norm_spread("post2")
            for n in range(DT):
                free_bank(pe, RES["final"] + n) if n < 4 else pe.wait_ge(y_final, n - 3)
                pe.wait_ge(x_new, 2 * DT + n + 1)
                for i in range(TT):
                    mm = pe.transpose(bank[(RES["final"] + n) % BANKS][:, i * P:(i + 1) * P], x[:, n, i * P:(i + 1) * P], CI(C_IDENT))
                finish(mm)


_INS = ["x", "ffn1_norm", "ffn1_w_gate", "ffn1_w_up", "ffn1_w_down", "mix_norm", "w_in", "q_norm", "k_norm", "rel_bias",
        "pool_w", "pool_scale", "w_out", "ffn2_norm", "ffn2_w_gate", "ffn2_w_up", "ffn2_w_down", "final_norm",
        "norm_mix_pre_2", "w_in_2", "conv_w_2", "conv_b_2", "b_igate_2", "b_fgate_2", "lambda_q1_2", "lambda_k1_2",
        "lambda_q2_2", "lambda_k2_2", "diff_norm_2", "mlstm_norm_2", "w_out_2", "norm_mix_post_2", "norm_mlp_pre_2",
        "w_up_2", "w_down_2", "norm_mlp_post_2"]


def kernel(**inputs):
    import concourse.bacc as _bacc
    from concourse.bass_utils import run_bass_kernel_spmd as _run

    nc = _bacc.Bacc("TRN2", target_bir_lowering=False, num_devices=1)
    arrays, t = {}, {}
    for name in _INS + ["const"]:
        a = shape_constants() if name == "const" else np.ascontiguousarray(inputs[name])
        arrays[f"in_{name}"] = a
        t[name] = nc.dram_tensor(f"in_{name}", a.shape, mybir.dt.from_np(a.dtype), kind="ExternalInput").ap()
    t["out"] = nc.dram_tensor("out_0", (1, S, D), F32, kind="ExternalOutput").ap()
    build(nc, t)
    r = _run(nc, [arrays], core_ids=[0])
    return r.results[0]["out_0"]
```

```python
from contextlib import ExitStack

import numpy as np
import concourse.bass as bass
from concourse import mybir

ALU = mybir.AluOpType
ACT = mybir.ActivationFunctionType
F32 = mybir.dt.float32
F32R = mybir.dt.float32r

P = 128
S = 512
TT = S // P
D = 1024
DT = D // P
EPS = 1e-6
BIG = 1e30
FF = 2816
FF2 = 4096
HALF = 16
HEADS = 8
DH = 4
MH = 4
LAM_INIT = 0.2
PAD = 16
CONV = 4
RING = 4
BANKS = 4
AHEAD = 2

C_IDENT, C_FLIP, C_SWAP, C_HSUM, C_ONES, C_MASKT, C_CAUSAL = (128 * i for i in range(7))
C_HROW = 7 * 128
C_COS, C_SIN = C_HROW, C_HROW + 512
C_SEL4 = C_HROW + 1024
C_POOL = C_SEL4 + 512
C_ALL = C_POOL + 64


def shape_constants():
    c = np.zeros((P, C_ALL + 2 * S), np.float32)
    p = np.arange(P)
    c[:, C_IDENT:C_IDENT + P] = np.eye(P)
    c[p, C_FLIP + P - 1 - p] = -1.0
    partner = np.where(p % 64 < 32, p + 32, p - 32)
    c[partner, C_SWAP + p] = 1.0
    for t in range(8):
        c[2 * t + p // 64, C_HROW + P * t + p] = 1.0
        c[32 + 2 * t + p // 64, C_HROW + P * t + p] = 1.0
    c[p, C_HSUM + p // 64] = 1.0
    c[:, C_ONES:C_ONES + P] = 1.0
    c[:, C_MASKT:C_MASKT + P] = np.where(p[:, None] > p[None, :], -BIG, 0.0)
    c[:, C_CAUSAL:C_CAUSAL + P] = np.where(p[None, :] > p[:, None], BIG, 0.0)
    for h in range(4):
        c[h, C_SEL4 + P * h:C_SEL4 + P * (h + 1)] = 1.0
        c[32 + h, C_SEL4 + P * h:C_SEL4 + P * (h + 1)] = 1.0
    inv = np.float32(10000.0) ** (-np.arange(0, 64, 2, dtype=np.float32) / np.float32(64))
    ang = np.arange(S, dtype=np.float32)[None, :] * inv[p % 32][:, None]
    c[:, C_ALL:C_ALL + S] = np.cos(ang)
    c[:, C_ALL + S:] = np.sin(ang) * np.where(p % 64 < 32, -1.0, 1.0)[:, None]
    for g in range(4):
        w = 2 ** (g + 1)
        c[:, C_POOL + 16 * g:C_POOL + 16 * (g + 1)] = w / np.minimum(np.arange(16) + 1, w)
    return c


def numbered(sizes):
    first, n = {}, 0
    for name, size in sizes:
        first[name] = n
        n += size
    return first, n


FT = FF // P
FT2 = FF2 // P
BLK, NBLK = numbered([
    ("f1_up0", 2 * HALF), ("f1_dn0", 2 * DT), ("f1_up1", 2 * (FT - HALF)), ("f1_dn1", DT),
    ("qk", 8), ("v", 4), ("u", 4), ("poolw", 1), ("out1", 8),
    ("f2_up0", 2 * HALF), ("f2_dn0", 2 * DT), ("f2_up1", 2 * (FT - HALF)), ("f2_dn1", DT),
    ("gate", 1), ("dqk", 8), ("dv", 4), ("mqk", 4), ("mo", 4), ("mv", 4), ("out2", 8),
    ("f3_up0", HALF), ("f3_dn0", 2 * DT), ("f3_up1", HALF), ("f3_dn1", 2 * DT)])
RES, NRES = numbered([
    ("input", 8),
    ("f1_up0", 2 * HALF), ("f1_dn0", DT), ("f1_up1", 2 * (FT - HALF)), ("f1_dn1", DT),
    ("qk", 8), ("v", 4), ("u", 4), ("poolw", 4), ("out1", 8),
    ("f2_up0", 2 * HALF), ("f2_dn0", DT), ("f2_up1", 2 * (FT - HALF)), ("f2_dn1", DT),
    ("gate", 1), ("dqk", 8), ("dv", 4), ("mqk", 4), ("mo", 4), ("mv", 4), ("out2", 8),
    ("f3_up0", HALF), ("f3_dn0", DT), ("f3_up1", HALF), ("f3_dn1", DT), ("final", 8)])
HID, NHID = numbered([("f1_up0", HALF), ("f1_up1", FT - HALF), ("f2_up0", HALF), ("f2_up1", FT - HALF),
                      ("f3_up0", HALF), ("f3_up1", HALF)])
GEN, _ = numbered([("f1", 8), ("m1", 8), ("f2", 8), ("m2", 8), ("f3", 8)])
SQ, _ = numbered([("f1", 8), ("m1", 8), ("f2", 8), ("m2", 16), ("post1", 8), ("f3", 8), ("post2", 8)])
SPREAD, _ = numbered([("f1", 1), ("m1", 1), ("f2", 1), ("m2", 2), ("post1", 1), ("f3", 1), ("post2", 1)])
NORM = {n: i for i, n in enumerate(["f1", "m1", "f2", "m2", "post1", "f3", "post2"])}
GAINS = ["ffn1_norm", "mix_norm", "ffn2_norm", "final_norm", "norm_mix_pre_2", "norm_mix_post_2",
         "norm_mlp_pre_2", "norm_mlp_post_2"]


def build(nc, t):
    with ExitStack() as ctx:
        def sb(name, shape, dt=F32, stack=ctx):
            return stack.enter_context(nc.sbuf_tensor(name, shape, dt))

        def sem(name):
            return ctx.enter_context(nc.semaphore(name))

        x = sb("x", [P, DT, S])
        part = []
        over = []
        for r in range(3):
            with ExitStack() as s:
                over.append(sb(f"region{r}_f32", [P, 16, S], F32, s))
            part.append(sb(f"region{r}", [P, 16 if r < 2 else 18, S], F32R))
        w_raw, w_low = [], []
        for r in range(RING):
            with ExitStack() as s:
                w_raw.append(sb(f"w_raw{r}", [P, 1024], F32, s))
            w_low.append(sb(f"w_low{r}", [P, 1024], F32R))
        w_high = [sb(f"w_high{r}", [P, 1024], F32R) for r in range(RING)]
        const = sb("const", [P, C_ALL])
        gains = sb("gains", [P, len(GAINS), DT])
        ones_r = sb("ones_r", [P, P], F32R)
        rstd = sb("rstd", [P, S])
        rstd_fin = sb("rstd_fin", [P, S])
        diag = sb("diag", [P, TT, P])
        sq = sb("sq", [P, 2, S])
        sq_sum = sb("sq_sum", [P, 2, S])
        std_col = sb("std_col", [P, 2 * TT])
        r_col = sb("r_col", [P, 4 * TT])
        eps_col = sb("eps_col", [P, 1])
        head_std = sb("head_std", [P, TT * 2 * HEADS])
        head_rstd = sb("head_rstd", [P, TT * 2 * HEADS])
        qk_gain = sb("qk_gain", [P, 2])
        pool_gain = sb("pool_gain", [P, 4])
        far = sb("far", [P, HEADS])
        conv_w = sb("conv_w", [P, CONV, 4])
        conv_b = sb("conv_b", [P, 4])
        gate_b = sb("gate_b", [P, 2])
        lam_in = sb("lam_in", [P, 4])
        lam_pr = sb("lam_pr", [P, 2])
        lam_ex = sb("lam_ex", [P, 2])
        neg_lam = sb("neg_lam", [P, 1])
        diff_gain = sb("diff_gain", [P, 1])
        mlstm_gain = sb("mlstm_gain", [P, MH])
        rel_rows = sb("rel_rows", [HEADS, 384])

        with ExitStack() as s:
            ff_z = sb("ff_z", [P, 2, S], F32, s)
            ff_u = sb("ff_u", [P, 2, S], F32, s)
            ff_s = sb("ff_s", [P, 2, S], F32, s)
            ff_t = sb("ff_t", [P, 2, S], F32, s)
            y_tmp = sb("y_tmp", [P, 2, S], F32, s)
        with ExitStack() as s:
            u_pad = sb("u_pad", [P, 4, PAD + S], F32, s)
            win = sb("win", [P, 2, PAD + S], F32, s)
            with ExitStack() as s2:
                head_sq = sb("head_sq", [P, 2, S], F32, s2)
                qk_full = sb("qk_full", [P, 2, S], F32, s2)
                head_rows = sb("head_rows", [48, S], F32R, s2)
                head_select = sb("head_select", [48, 2 * S], F32R, s2)
            with ExitStack() as s2:
                a_s = sb("a_s", [P, 2, S], F32, s2)
                a_p = sb("a_p", [P, 3, S], F32, s2)
                toep = sb("toep", [P, 2, 2, P], F32, s2)
                bias = sb("bias", [P, 2, S], F32, s2)
                a_min = sb("a_min", [P, 4 * HEADS], F32, s2)
                a_sum = sb("a_sum", [P, 4 * HEADS], F32, s2)
                a_rec = sb("a_rec", [P, 4 * HEADS], F32, s2)
        with ExitStack() as s:
            max_rows = sb("max_rows", [36, S], F32R, s)
            sum_rows = sb("sum_rows", [36, S], F32R, s)
            rstd_rows = sb("rstd_rows", [36, S], F32R, s)
            select4 = sb("select4", [36, TT * P], F32R, s)
            a_col = sb("a_col", [P, TT, MH], F32, s)
            with ExitStack() as s2:
                scan = sb("scan", [MH, 4, S], F32, s2)
                rope_y = sb("rope_y", [P, 4, S], F32, s2)
                rope_c = sb("rope_c", [P, 2, S], F32, s2)
                rope_s = sb("rope_s", [P, 2, S], F32, s2)
            with ExitStack() as s2:
                d_s = sb("d_s", [P, 2, S], F32, s2)
                d_p = sb("d_p", [P, 6, S], F32, s2)
                d_mask = sq_sum[:, 0, :]
                d_min = sb("d_min", [P, 32], F32, s2)
                d_sum = sb("d_sum", [P, 32], F32, s2)
                d_rec = sb("d_rec", [P, 32], F32, s2)
                d_lam = sb("d_lam", [P, 16], F32, s2)
                d_full = d_s
                c_acc = sb("c_acc", [P, 4, S], F32, s2)
            with ExitStack() as s2:
                m_num = sb("m_num", [P, MH, S], F32, s2)
                m_e = sb("m_e", [P, 3, S], F32, s2)
                m_dm = sb("m_dm", [P, TT, P], F32, s2)
                m_eg = sq_sum[:, 1, :]
                m_den = sq_sum[:, 0, :]
                m_sq = sq[:, 0, :]
                m_full = m_e

        x_tok = over[2][:, 0:8, :].rearrange("p a b -> p (a b)").rearrange("p (t d) -> p t d", t=TT)
        qk_raw = over[2][:, 8:16, :]
        mixed = over[2][:, 0:8, :]
        x_back = over[1][:, 0:8, :]
        out_tok = over[0][:, 0:8, :].rearrange("p a b -> p (a b)").rearrange("p (t d) -> p t d", t=TT)
        o_diff = over[1][:, 0:4, :]
        mqk_raw = x[:, 0:4, :]
        sig = x[:, 4:8, :]

        turned = part[2][:, 8:18, :].rearrange("p a b -> p (a b)").rearrange("p (s b n) -> p s b n", s=2, n=P)

        def turned_unit(h, q, low):
            first, step = (q + 1, 5) if h % 2 == 0 else (15 - 5 * q, 6)
            return turned[:, low, first:first + step * q + 1:step, :]

        def turned_keys(h, k, low):
            first = 6 * k + 1 if h % 2 == 0 else 5 * (3 - k)
            return turned[:, low, first:first + TT - k, :].rearrange("p b n -> p (b n)")

        bank = [ctx.enter_context(nc.psum_tensor(f"bank{i}", [P, S], F32)) for i in range(8)]

        landed = [sem(f"landed{r}") for r in range(RING)]
        x_in = [sem(f"x_in{c}") for c in range(4)]
        ident_in, const_in = sem("ident_in"), sem("const_in")
        small_in, rel_in, toep_in = sem("small_in"), sem("rel_in"), [sem("toep_in0"), sem("toep_in1")]
        rel_padded, rel_stored = sem("rel_padded"), sem("rel_stored")
        consts_made, small_made = sem("consts_made"), sem("small_made")
        w_hi, w_lo, w_used = sem("w_hi"), sem("w_lo"), sem("w_used")
        acc_ready, acc_free = sem("acc_ready"), sem("acc_free")
        x_new, xt_hi, xt_lo = sem("x_new"), sem("xt_hi"), sem("xt_lo")
        sq_ready, sq_added = sem("sq_ready"), sem("sq_added")
        stat_ready, std_ready, rcol_ready, diag_ready = sem("stat_ready"), sem("std_ready"), sem("rcol_ready"), sem("diag_ready")
        bc_ready, rstd_ready = sem("bc_ready"), sem("rstd_ready")
        z_ready, s_ready, t_ready, hid_hi, hid_done = sem("z_ready"), sem("s_ready"), sem("t_ready"), sem("hid_hi"), sem("hid_done")
        ev_hi = sem("ev_hi")
        v1 = sem("dve_step")
        pool_step = sem("pool_step")
        gate_in, gain_in, lam_made, lam_summed = sem("gate_in"), sem("gain_in"), sem("lam_products_ready"), sem("lam_summed")
        x_unit, pads_zero = sem("x_unit_ready"), sem("pads_zero")

        w_dram = {n: t[n][0] for n in ("ffn1_w_gate", "ffn1_w_up", "ffn1_w_down", "w_in", "w_out",
                                       "ffn2_w_gate", "ffn2_w_up", "ffn2_w_down", "w_in_2", "w_out_2",
                                       "w_up_2", "w_down_2")}
        w_dram = {n: a.rearrange("(k p) n -> p k n", p=P) for n, a in w_dram.items()}

        CI = lambda c, n=P, rows=P: const[0:rows, c:c + n]

        def split3(pe, out, a_hi, a_lo, b_hi, b_lo, start, stop, new_block=False):
            mm = pe.matmul(out, a_hi, b_hi, start=start, stop=False)
            if new_block:
                mm.then_inc(w_used, 1)
            pe.matmul(out, a_hi, b_lo, start=False, stop=False)
            return pe.matmul(out, a_lo, b_hi, start=False, stop=stop)

        def free_bank(pe, r, it=None, step=0):
            n = r - BANKS + 1
            if it is not None:
                pe.wait_ge(acc_free, it * step + n)
            elif n > 0:
                pe.wait_ge(acc_free, n)

        def block_ready(pe, b, it=None, step=0):
            pe.wait_ge(w_lo, b + 1 if it is None else it * step + (b + 1))

        def block_parts(b, it):
            if it is None and b == BLK["poolw"]:
                return [lambda a: a[:, 0:4 * P]]
            if it is None and b == BLK["gate"]:
                return [lambda a, c=c: a[:].rearrange("p (k n) -> p k n", n=P)[:, :, c:c + MH] for c in (0, 32)]
            return [lambda a: a[:]]

        def w_tiles(b, width=P):
            hi, lo = w_high[b % RING], w_low[b % RING]
            return (hi[:].rearrange("p (k n) -> p k n", n=width), lo[:].rearrange("p (k n) -> p k n", n=width))

        def fetch(sp, b, src, it=None, step=0, width=P):
            if it is not None:
                sp.wait_ge(w_used, it * step + (b - RING + 1))
            elif b >= RING:
                sp.wait_ge(w_used, b - RING + 1)
            dst = w_raw[b % RING][:].rearrange("p (k n) -> p k n", n=width)
            nk = src.shape[1]
            sp.dma_start(dst[:, 0:nk, :], src).then_inc(landed[b % RING], 16)

        def first_blocks(sp):
            for q, m in enumerate(("ffn1_w_gate", "ffn1_w_up")):
                fetch(sp, q, w_dram[m][:, :, 0:P])

        def sp_up(sp, name, mats, ht0, tiles):
            per = RING // len(mats)
            def turn(it):
                q = 0
                for j in range(per):
                    for m in mats:
                        b = BLK[name] + q
                        if it is None and q < 2:
                            q += 1
                            continue
                        if it is None:
                            src = w_dram[m][:, :, (ht0 + j) * P:(ht0 + j + 1) * P]
                        else:
                            src = w_dram[m][:, :, bass.ds(it * (per * P) + (ht0 + j) * P, P)]
                        fetch(sp, b, src, it, RING)
                        q += 1
            first = 1 if BLK[name] == 0 else 0
            if first:
                turn(None)
            with sp.Fori(first, tiles // per) as it:
                turn(it)

        def sp_down(sp, name, m, k0, nk):
            pieces = [(min(k, k0 + nk - 8), 8) for k in range(k0, k0 + nk, 8)]
            per = RING // len(pieces)
            with sp.Fori(0, DT // per) as it:
                q = 0
                for j in range(per):
                    for k, n in pieces:
                        fetch(sp, BLK[name] + q, w_dram[m][:, k:k + n, bass.ds(it * (per * P) + j * P, P)], it, RING)
                        q += 1

        def sp_cols(sp, name, m, tiles, col0):
            for j in range(tiles):
                fetch(sp, BLK[name] + j, w_dram[m][:, :, col0 + j * P:col0 + (j + 1) * P])

        def sp_rows(sp, name, m, col0):
            for j in range(4):
                fetch(sp, BLK[name] + j, w_dram[m][:, 2 * j:2 * j + 2, col0:col0 + S], width=S)

        out_stored, x_spilled, x_returned, y_final = sem("out_stored"), sem("x_spilled"), sem("x_returned"), sem("out_tile_ready")
        x_spill = [nc.dram_tensor(f"x_spill{i}", [P, DT, S], F32).ap() for i in range(2)]
        rel_pad_dram = nc.dram_tensor("rel_padded_rows", [HEADS, 384], F32).ap()

        y_sq, h_stat, h_std, h_rec, h_bc, qk_full_ready, qk_hi, qk_lo = (sem(n) for n in (
            "head_sq_ready", "head_stat_added", "head_std_ready", "head_rstd_ready", "head_bc_ready",
            "qk_full_ready", "qk_hi_ready", "qk_lo_ready"))
        h_turned, h_rows_hi, h_rows_lo = sem("head_rstd_turned"), sem("head_rows_hi"), sem("head_rows_lo")
        e_rturned, e_rows_hi, e_rows_lo = sem("d_rstd_turned"), sem("d_rows_hi"), sem("d_rows_lo")
        m_rturned, m_rows_hi, m_rows_lo = sem("m_rstd_turned"), sem("m_rows_hi"), sem("m_rows_lo")
        select_made, select4_made = sem("head_select_made"), sem("select4_made")
        b_mm, b_done = sem("bias_product"), sem("bias_ready")
        a_score, a_biased, a_exp, a_prob, a_turned, a_thi, a_tlo, a_out, a_ohi, a_olo = (sem(n) for n in (
            "scores_ready", "scores_biased", "exp_ready", "probs_ready", "probs_turned", "turned_hi",
            "turned_lo", "head_out_ready", "head_out_hi", "head_out_lo"))
        pool_done, pd_hi, pd_lo = sem("pooled"), sem("pooled_hi"), sem("pooled_lo")
        g_abs, g_exp, g_ln, g_rows, g_turn, g_cols = (sem(n) for n in (
            "gate_abs", "gate_exp", "gate_ln", "gate_rows_ready", "gate_turned", "gate_cols_ready"))
        rope_in_sem = sem("rope_tables_in")
        rows_filled = sem("rows_filled")
        r_perm, r_cos = sem("rope_swapped"), sem("rope_cos_ready")
        r_full, r_hi, r_lo = sem("rope_ready"), sem("rope_hi"), sem("rope_lo")
        e_score, e_biased, e_exp, e_prob, e_turned, e_thi, e_tlo, e_out, e_sq, e_copied, e_stat, e_std, e_rec, e_bc, e_full, e_hi, e_lo = (
            sem("d_" + n) for n in ("scores_ready", "scores_masked", "exp_ready", "probs_ready", "probs_turned",
                                    "turned_hi", "turned_lo", "out_ready", "sq_ready", "out_copied", "stat_added",
                                    "std_ready", "rstd_ready", "bc_ready", "normed", "normed_hi", "normed_lo"))
        c_sum, c_act, c_hi, c_lo, mo_sig = (sem(n) for n in (
            "conv_ready", "conv_silu", "conv_hi", "conv_lo", "gate_o_sigmoid"))
        m_bc, m_score, m_diag, m_exp, m_prod, m_phi, m_plo, m_pv, m_egr, m_nsq, m_ncp, m_dn, m_dsq, m_sqs, m_stat, m_std, m_rec, m_bcr, m_norm, m_hi, m_lo = (
            sem("m_" + n) for n in ("rows_spread", "scores_ready", "diag_ready", "exp_ready", "weights_ready",
                                    "weights_hi", "weights_lo", "values_added", "exp_g_ready", "num_sq_ready",
                                    "num_copied", "den_ready", "den_sq_ready", "sq_sum_ready", "stat_added",
                                    "std_ready", "rstd_ready", "bc_ready", "normed", "normed_hi", "normed_lo"))

        block = ctx.enter_context(nc.Block())

        @block.sync
        def _(sp):
            sp.dma_start(const[:, 0:P], t["const"][:, 0:P]).then_inc(ident_in, 16)
            for c in range(4):
                cols = slice(2 * P * c, 2 * P * (c + 1))
                sp.dma_start(x_tok[:, :, cols], t["x"][0].rearrange("(t p) d -> p t d", p=P)[:, :, cols]).then_inc(x_in[c], 16)
            first_blocks(sp)
            sp.dma_start(const[:, P:C_ALL], t["const"][:, P:C_ALL]).then_inc(const_in, 16)
            sp_up(sp, "f1_up0", ("ffn1_w_gate", "ffn1_w_up"), 0, HALF)
            sp_down(sp, "f1_dn0", "ffn1_w_down", 0, HALF)
            sp_up(sp, "f1_up1", ("ffn1_w_gate", "ffn1_w_up"), HALF, FT - HALF)
            sp_down(sp, "f1_dn1", "ffn1_w_down", HALF, FT - HALF)
            sp_cols(sp, "qk", "w_in", 8, 0)
            sp_rows(sp, "v", "w_in", S * 2)
            sp_cols(sp, "u", "w_in", 4, S * 3)
            fetch(sp, BLK["poolw"], t["pool_w"][0].rearrange("g c d -> c g d"))
            sp_cols(sp, "out1", "w_out", 8, 0)
            sp.wait_ge(qk_full_ready, 8)
            sp.dma_start(const[:, C_COS:C_COS + 2 * S], t["const"][:, C_ALL:]).then_inc(rope_in_sem, 16)
            sp_up(sp, "f2_up0", ("ffn2_w_gate", "ffn2_w_up"), 0, HALF)
            sp_down(sp, "f2_dn0", "ffn2_w_down", 0, HALF)
            sp_up(sp, "f2_up1", ("ffn2_w_gate", "ffn2_w_up"), HALF, FT - HALF)
            sp_down(sp, "f2_dn1", "ffn2_w_down", HALF, FT - HALF)
            b = BLK["gate"]
            sp.wait_ge(w_used, b - RING + 1)
            gw = w_raw[b % RING][:].rearrange("p (k n) -> p k n", n=P)
            with nc.allow_non_contiguous_dma("eight columns of w_in_2"):
                sp.dma_start(gw[:, :, 0:MH], w_dram["w_in_2"][:, :, 3072:3076]).then_inc(landed[b % RING], 16)
                sp.dma_start(gw[:, :, 32:32 + MH], w_dram["w_in_2"][:, :, 3076:3080]).then_inc(gate_in, 16)
            sp_cols(sp, "dqk", "w_in_2", 8, 0)
            sp_rows(sp, "dv", "w_in_2", 1024)
            sp_cols(sp, "mqk", "w_in_2", 4, 1536)
            sp_cols(sp, "mo", "w_in_2", 4, 2560)
            sp_rows(sp, "mv", "w_in_2", 2048)
            sp_cols(sp, "out2", "w_out_2", 8, 0)
            sp_up(sp, "f3_up0", ("w_up_2",), 0, HALF)
            sp_down(sp, "f3_dn0", "w_down_2", 0, HALF)
            sp_up(sp, "f3_up1", ("w_up_2",), HALF, HALF)
            sp_down(sp, "f3_dn1", "w_down_2", HALF, HALF)
            for n in range(DT):
                sp.wait_ge(y_final, n + 1)
                sp.dma_start(t["out"][0].rearrange("(t p) d -> p t d", p=P)[:, :, n * P:(n + 1) * P],
                             out_tok[:, :, n * P:(n + 1) * P]).then_inc(out_stored, 16)
            sp.wait_ge(out_stored, 16 * DT)

        SMALL = []

        @block.scalar
        def _(act):
            def load(dst, src):
                SMALL.append(1)
                with nc.allow_non_contiguous_dma("small vectors, once"):
                    act.dma_start(dst, src).then_inc(small_in, 16)

            def column(v):
                return v.rearrange("(n p) -> p n", p=P)

            act.dma_start(rel_rows[:, 0:257], t["rel_bias"][0]).then_inc(rel_in, 16)
            with nc.allow_non_contiguous_dma("small vectors, once"):
                act.dma_start(gains[:, 0, :], column(t[GAINS[0]][0])).then_inc(gain_in, 16)
            smalls = [(gains[:, i + 1, :], column(t[n][0])) for i, n in enumerate(GAINS[1:])]
            smalls += [(qk_gain[64 * half:64 * half + 64, i:i + 1], t[n].rearrange("a d -> d a"))
                       for i, n in enumerate(("q_norm", "k_norm")) for half in range(2)]
            smalls += [(pool_gain[:], column(t["pool_scale"][0])),
                       (far[:], t["rel_bias"][0][:, 256:257].rearrange("h a -> a h").broadcast_to([P, HEADS]))]
            smalls += [(conv_w[:, j, :], column(t["conv_w_2"][0, j])) for j in range(CONV)]
            smalls += [(conv_b[:], column(t["conv_b_2"][0])),
                       (gate_b[0:MH, 0:1], t["b_igate_2"].rearrange("a d -> d a")),
                       (gate_b[0:MH, 1:2], t["b_fgate_2"].rearrange("a d -> d a"))]
            smalls += [(lam_in[0:64, i:i + 1], t[n].rearrange("a d -> d a"))
                       for i, n in enumerate(("lambda_q1_2", "lambda_k1_2", "lambda_q2_2", "lambda_k2_2"))]
            smalls += [(diff_gain[:], t["diff_norm_2"].rearrange("a d -> d a")),
                       (mlstm_gain[:], t["mlstm_norm_2"][0].rearrange("h d -> d h"))]

            def load_smalls(n):
                for dst, src in smalls[4 * n:4 * n + 4]:
                    load(dst, src)
                if n == 0:
                    act.wait_ge(rel_padded, 1)
                    act.dma_start(rel_pad_dram, rel_rows[:]).then_inc(rel_stored, 16)

            def split_hi(b, it=None, step=0):
                if it is None:
                    if b >= NBLK:
                        return
                    act.wait_ge(landed[b % RING], 16 * (b // RING + 1))
                    if b >= RING:
                        act.wait_ge(w_used, b - RING + 1)
                    if b == BLK["gate"]:
                        act.wait_ge(gate_in, 16)
                else:
                    act.wait_ge(landed[b % RING], it * (16 * step // RING) + 16 * (b // RING + 1))
                    act.wait_ge(w_used, it * step + (b - RING + 1))
                for piece in block_parts(b, it):
                    last = act.copy(piece(w_high[b % RING]), piece(w_raw[b % RING]))
                last.then_inc(w_hi, 1)

            def residual(sqk, n, g, dst):
                act.activation(dst[:, n, :], x[:, n, :], ACT.Identity, scale=gains[:, g, n:n + 1]).then_inc(xt_hi, 1)
                if sqk is not None:
                    square(sqk + n, x[:, n, :])

            def square(i, src, scale=1.0):
                if i >= 2:
                    act.wait_ge(sq_added, i - 1)
                act.activation(sq[:, i % 2, :], src, ACT.Square, scale=scale).then_inc(sq_ready, 1)

            def norm_std(name):
                act.wait_ge(stat_ready, NORM[name] + 1)
                act.activation(std_col[:, 0:TT], bank[4][:, 0:TT], ACT.Sqrt, scale=1.0 / D, bias=eps_col[:]).then_inc(std_ready, 1)

            def norm_copy(name, dst, extra=0):
                act.wait_ge(bc_ready, SPREAD[name] + 1 + extra)
                act.copy(dst[:], bank[5][:]).then_inc(rstd_ready, 1)

            def up(name, dst, gated, head=None):
                per = 2 if gated else 4
                tiles = FT - HALF if (gated and name.endswith("1")) else HALF
                def turn(it):
                    for j in range(per):
                        c = HID[name] + j
                        val = lambda n: n if it is None else it * per + n
                        def nxt(q):
                            b = BLK[name] + q + AHEAD
                            split_hi(b) if it is None else split_hi(b, it, RING)
                        idx = j if it is None else it * per + j
                        if gated:
                            nxt(2 * j)
                            act.wait_ge(z_ready, val(c + 1))
                            act.activation(ff_s[:, j % 2, :], ff_z[:, j % 2, :], ACT.Silu).then_inc(s_ready, 1)
                            nxt(2 * j + 1)
                            act.wait_ge(t_ready, val(c + 1))
                        else:
                            if it is not None or j > 1:
                                nxt(j)
                            act.wait_ge(acc_free, val(RES[name] + j + 1))
                            if c >= 2:
                                act.wait_ge(hid_done, val(c - 1))
                            act.activation(ff_t[:, j % 2, :], ff_z[:, j % 2, :], ACT.Square).then_inc(t_ready, 1)
                            act.wait_ge(t_ready, val(c + 1))
                        act.copy(dst[:, bass.ds(idx, 1), :] if it is not None else dst[:, idx, :],
                                 ff_t[:, j % 2, :]).then_inc(hid_hi, 1)
                if head is not None:
                    head()
                    turn(None)
                with act.Fori(0 if head is None else 1, tiles // per) as it:
                    turn(it)

            def down(name, blocks, each=None):
                for n in range(DT):
                    for q in range(blocks):
                        split_hi(BLK[name] + n * blocks + q + AHEAD)
                    if each is not None:
                        each(n)

            def head(name):
                def run():
                    norm_std(name)
                    norm_copy(name, rstd)
                return run

            act.wait_ge(consts_made, 2)
            act.wait_ge(gain_in, 16)
            for n in range(DT):
                act.wait_ge(acc_free, RES["input"] + n + 1)
                residual(SQ["f1"], n, 0, part[0])
                if n in (2, 4):
                    split_hi(n // 2 - 1)
            act.wait_ge(const_in, 16)
            act.copy(ones_r[:], CI(C_ONES)).then_inc(ev_hi, 1)

            def ffn(f, hid):
                up(f"f{f}_up0", hid, True, head(f"f{f}"))
                down(f"f{f}_dn0", 2, load_smalls if f == 1 else None)
                up(f"f{f}_up1", hid, True)
                def each(n):
                    if f == 1 and n == 0:
                        act.wait_ge(small_in, 16 * len(SMALL))
                    act.wait_ge(acc_free, RES[f"f{f}_dn1"] + n + 1)
                    if f == 1:
                        residual(SQ["m1"], n, 1, part[0])
                    else:
                        square(SQ["m2"] + 2 * n, y_tmp[:, n % 2, :])
                        act.wait_ge(x_new, n + 1)
                        residual(None, n, 4, part[0])
                        square(SQ["m2"] + 2 * n + 1, x[:, n, :])
                down(f"f{f}_dn1", 1, each)

            ffn(1, part[1])

            act.wait_ge(lam_summed, 1)
            act.activation(lam_ex[:], bank[5][:, 0:2], ACT.Exp).then_inc(ev_hi, 1)
            act.copy(head_select[:], const[0:48, C_HROW:C_HROW + 2 * S]).then_inc(select_made, 1)
            for i in range(8):
                split_hi(BLK["qk"] + i + AHEAD)
                if i == 0:
                    head("m1")()
                act.wait_ge(acc_free, RES["qk"] + i + 1)
                if i >= 2:
                    act.wait_ge(h_stat, i - 1)
                act.activation(head_sq[:, i % 2, :], qk_raw[:, i, :], ACT.Square).then_inc(y_sq, 1)
            for i in range(3):
                split_hi(BLK["v"] + i + AHEAD)
            act.wait_ge(h_stat, 8)
            act.activation(head_std[:], bank[4][:, 0:TT * 2 * HEADS], ACT.Sqrt, scale=1.0 / 64, bias=eps_col[:]).then_inc(h_std, 1)
            act.wait_ge(h_turned, 1)
            act.wait_ge(select_made, 2)
            act.copy(head_rows[0:2 * HEADS, :], bank[5][0:2 * HEADS, :]).then_inc(h_rows_hi, 1)
            for i in range(8):
                if i == 2:
                    split_hi(BLK["v"] + 3 + AHEAD)
                act.wait_ge(qk_full_ready, i + 1)
                act.copy(part[1][:, i, :], qk_full[:, i % 2, :]).then_inc(qk_hi, 1)
            for i in range(TT):
                act.wait_ge(acc_ready, RES["v"] + i + 1)
                act.activation(part[2][:, i, :], bank[(RES["v"] + i) % BANKS][:], ACT.Identity,
                               scale=r_col[:, i:i + 1]).then_inc(ev_hi, 1)
            def toeplitz(h):
                if h >= 2:
                    act.wait_ge(b_mm, h - 1)
                src = rel_pad_dram[h:h + 1, 1:2].copy()
                src = bass.AP(src.tensor, src.offset, [[1, P], [128, 2], [1, P]])
                act.dma_start(toep[:, h % 2, :, :], src).then_inc(toep_in[h % 2], 16)
            act.wait_ge(rel_stored, 16)
            act.wait_ge(qk_lo, 8)
            for h in range(2):
                toeplitz(h)

            def a_expo(u):
                h, q = divmod(u, TT)
                n = (q + 1) * P
                act.wait_ge(a_biased, u + 1)
                if u >= 3:
                    act.wait_ge(a_turned, u - 2)
                act.activation(a_p[:, u % 3, 0:n], a_s[:, u % 2, 0:n], ACT.Exp, scale=-1.0,
                               bias=a_min[:, u:u + 1], accum_out=a_sum[:, u:u + 1]).then_inc(a_exp, 1)

            def turned_hi(u, ready, done, out_sem):
                h, q = divmod(u, TT)
                act.wait_ge(ready, u + 1)
                if h >= 2:
                    act.wait_ge(out_sem, h - 1)
                act.copy(turned_unit(h, q, 0),
                         bank[6 + u % 2][:, 0:(q + 1) * P].rearrange("p (k n) -> p k n", n=P)).then_inc(done, 1)

            def pooled_hi(g):
                act.wait_ge(pool_done, g + 1)
                act.copy(part[1][:, 4 + g, :], u_pad[:, g, PAD:]).then_inc(pd_hi, 1)

            def a_head_out(h):
                r = 64 * (h % 2)
                act.wait_ge(a_out, h + 1)
                act.copy(part[1][r:r + 64, h // 2, :], bank[h % 2][r:r + 64, :]).then_inc(a_ohi, 1)

            for u in range(4 * HEADS + 8):
                if u < 4 * HEADS and u % 8 == 4:
                    split_hi(BLK["u"] + u // 8 + AHEAD)
                if u < 4 * HEADS:
                    a_expo(u)
                    if u % TT == 3 and u // TT + 2 < HEADS:
                        toeplitz(u // TT + 2)
                if 2 <= u < 4 * HEADS + 2:
                    turned_hi(u - 2, a_turned, a_thi, a_out)
                if u >= 11 and (u - 11) % TT == 0:
                    a_head_out((u - 11) // TT)
                if u in (14, 22, 30):
                    pooled_hi((u - 14) // 8)
            pooled_hi(3)
            split_hi(BLK["poolw"] + AHEAD)
            for g in range(4):
                act.wait_ge(acc_ready, RES["poolw"] + g + 1)
                act.activation(part[1][:, 4 + g, :], bank[(RES["poolw"] + g) % BANKS][:], ACT.Identity,
                               scale=pool_gain[:, g:g + 1]).then_inc(ev_hi, 1)
            for n in range(DT):
                split_hi(BLK["out1"] + n + AHEAD)
                act.wait_ge(acc_free, RES["out1"] + n + 1)
                residual(SQ["f2"], n, 2, part[0])

            ffn(2, part[1])

            def rope_hi(act, i):
                act.wait_ge(r_full, i + 1)
                act.copy(part[1][:, i, :], rope_c[:, i % 2, :]).then_inc(r_hi, 1)

            act.wait_ge(x_new, DT)
            act.dma_start(x_spill[0], x[:]).then_inc(x_spilled, 16)
            split_hi(BLK["gate"] + AHEAD)
            split_hi(BLK["dqk"] + AHEAD)
            act.copy(select4[:], const[0:36, C_SEL4:C_SEL4 + TT * P]).then_inc(select4_made, 1)
            norm_std("m2")
            act.wait_ge(rcol_ready, 1)
            act.activation(std_col[:, TT:2 * TT], r_col[:, 3 * TT:4 * TT], ACT.Sqrt, scale=1.0 / D, bias=eps_col[:]).then_inc(std_ready, 1)
            norm_copy("m2", rstd)
            norm_copy("m2", rstd_fin, 1)
            act.wait_ge(acc_free, RES["gate"] + 1)
            act.activation(scan[:, 2, :], scan[:, 1, :], ACT.Abs, bias=gate_b[0:MH, 1:2]).then_inc(g_abs, 1)
            act.wait_ge(g_abs, 1)
            act.activation(scan[:, 2, 0:S], scan[:, 2, 0:S], ACT.Exp, scale=-1.0).then_inc(g_exp, 1)
            act.wait_ge(g_exp, 1)
            act.activation(scan[:, 2, 0:S], scan[:, 2, 0:S], ACT.Ln, bias=1.0).then_inc(g_ln, 1)
            for i in range(8):
                if i > 0:
                    split_hi(BLK["dqk"] + i + AHEAD)
                if i >= 2:
                    rope_hi(act, i - 2)
            for i in range(6, 8):
                rope_hi(act, i)
                split_hi(BLK["dv"] + i - 6 + AHEAD)
            for i in range(2, 4):
                split_hi(BLK["dv"] + i + AHEAD)
            for i in range(TT):
                act.wait_ge(acc_ready, RES["dv"] + i + 1)
                act.activation(part[2][:, i, :], bank[(RES["dv"] + i) % BANKS][:], ACT.Identity,
                               scale=r_col[:, TT + i:TT + i + 1]).then_inc(ev_hi, 1)

            def d_expo(u):
                n = (u // 2 % TT + 1) * P
                act.wait_ge(e_biased, u + 1)
                if u >= 6:
                    act.wait_ge(e_turned, u // 2 - 2)
                act.activation(d_p[:, u % 6, 0:n], d_s[:, u % 2, 0:n], ACT.Exp, scale=-1.0,
                               bias=d_min[:, u:u + 1], accum_out=d_sum[:, u:u + 1]).then_inc(e_exp, 1)

            def d_square(h):
                act.wait_ge(e_out, h + 1)
                if h >= 2:
                    act.wait_ge(e_stat, h - 1)
                act.activation(sq[:, h % 2, :], bank[h % 2][:], ACT.Square).then_inc(e_sq, 1)

            for w in range(4 * DH + 8):
                if w < 4 * DH:
                    if w % 2 == 0:
                        split_hi(BLK["mqk"] + w // 2 + AHEAD)
                    d_expo(2 * w)
                    d_expo(2 * w + 1)
                if 2 <= w < 4 * DH + 2:
                    turned_hi(w - 2, e_turned, e_thi, e_out)
                if w >= 11 and (w - 11) % TT == 0:
                    d_square((w - 11) // TT)
            act.wait_ge(e_stat, DH)
            act.activation(head_std[:, 0:TT * DH], bank[2][:, 0:TT * DH], ACT.Sqrt, scale=1.0 / P, bias=eps_col[:]).then_inc(e_std, 1)
            for i in range(2):
                split_hi(BLK["mv"] + i + AHEAD)
            for i in range(4):
                act.wait_ge(c_sum, i + 1)
                act.activation(c_acc[:, i, :], c_acc[:, i, :], ACT.Silu).then_inc(c_act, 1)
            act.wait_ge(e_rturned, 1)
            act.copy(rstd_rows[0:DH, :], bank[6][0:DH, :]).then_inc(e_rows_hi, 1)
            for i in range(4):
                act.wait_ge(c_act, i + 1)
                act.activation(part[1][:, 8 + i, :], c_acc[:, i, :], ACT.Copy, scale=0.125 if i < 2 else 1.0).then_inc(c_hi, 1)
            act.wait_ge(acc_free, RES["mo"] + 4)
            for i in range(4):
                act.activation(sig[:, i, :], sig[:, i, :], ACT.Sigmoid).then_inc(mo_sig, 1)
            for h in range(DH):
                act.wait_ge(e_full, h + 1)
                act.copy(part[1][:, 4 + h, :], d_full[:, h % 2, :]).then_inc(e_hi, 1)
            for i in range(TT):
                act.wait_ge(acc_ready, RES["mv"] + i + 1)
                act.activation(part[2][:, i, :], bank[(RES["mv"] + i) % BANKS][:], ACT.Identity,
                               scale=r_col[:, TT + i:TT + i + 1]).then_inc(ev_hi, 1)

            def m_expo(u):
                h, k = divmod(u, TT)
                act.wait_ge(m_diag, h + 1)
                if u >= 3:
                    act.wait_ge(m_plo, u - 2)
                last = act.activation(m_e[:, u % 3, 0:P], m_dm[:, k, :], ACT.Exp, bias=a_col[:, k, h:h + 1])
                if k < TT - 1:
                    last = act.activation(m_e[:, u % 3, P:S - k * P], bank[2][:, (k + 1) * P:], ACT.Exp, bias=a_col[:, k, h:h + 1])
                last.then_inc(m_exp, 1)

            def m_high(u):
                h, k = divmod(u, TT)
                act.wait_ge(m_prod, u + 1)
                if h >= 1:
                    act.wait_ge(m_pv, u - 3)
                act.copy(part[2][:, 8 + k, k * P:], m_e[:, u % 3, 0:S - k * P]).then_inc(m_phi, 1)

            def m_head(h):
                act.wait_ge(m_bc, 2 * h + 2)
                if h >= 1:
                    act.wait_ge(m_dn, h)
                act.activation(m_eg, bank[3][:], ACT.Exp).then_inc(m_egr, 1)
                act.wait_ge(m_pv, TT * (h + 1))
                if h >= 1:
                    act.wait_ge(m_stat, h)
                act.activation(m_sq, bank[h % 2][:], ACT.Square, scale=float(P) ** -0.5).then_inc(m_nsq, 1)

            def m_den_square(h):
                act.wait_ge(m_dn, h + 1)
                act.activation(m_den, m_den, ACT.Square, scale=(EPS / P) ** 0.5).then_inc(m_dsq, 1)

            m_expo(0)
            for u in range(MH * TT + 3):
                if u + 1 < MH * TT:
                    m_expo(u + 1)
                if u < MH * TT:
                    m_high(u)
                if u in (3, 6, 9):
                    split_hi(BLK["out2"] + u // 3 - 1)
                if u >= 5 and (u - 5) % TT == 0:
                    m_head((u - 5) // TT)
                if u >= 6 and (u - 6) % TT == 0:
                    m_den_square((u - 6) // TT)
            act.wait_ge(m_stat, MH)
            act.activation(head_std[:, 0:TT * MH], bank[7][:, 0:TT * MH], ACT.Sqrt).then_inc(m_std, 1)
            act.wait_ge(m_rturned, 1)
            act.copy(rstd_rows[0:MH, :], bank[7][0:MH, :]).then_inc(m_rows_hi, 1)
            for h in range(MH):
                act.wait_ge(m_norm, h + 1)
                act.copy(part[0][:, h, :], m_full[:, h % 2, :]).then_inc(m_hi, 1)
            act.wait_ge(x_spilled, 16)
            act.dma_start(x[:], x_spill[0]).then_inc(x_returned, 16)

            for n in range(DT):
                if n > 0:
                    split_hi(BLK["out2"] + n + AHEAD)
                act.wait_ge(acc_free, RES["out2"] + n + 1)
                square(SQ["post1"] + n, mixed[:, n, :])
            split_hi(BLK["f3_up0"] + 2)
            head("post1")()
            for n in range(DT):
                act.wait_ge(x_new, DT + n + 1)
                residual(SQ["f3"], n, 6, part[1])
            act.dma_start(x_spill[1], x[:]).then_inc(x_spilled, 16)

            split_hi(BLK["f3_up0"] + 3)
            up("f3_up0", part[0], False, head("f3"))
            down("f3_dn0", 2)
            up("f3_up1", part[0], False)
            def last(n):
                if n == 0:
                    act.wait_ge(acc_ready, RES["f3_dn1"] + 1)
                    act.wait_ge(x_spilled, 32)
                    act.dma_start(x_back, x_spill[1]).then_inc(x_returned, 16)
                act.wait_ge(acc_free, RES["f3_dn1"] + n + 1)
                square(SQ["post2"] + n, x[:, n, :])
            down("f3_dn1", 2, last)
            head("post2")()
            for n in range(DT):
                act.wait_ge(acc_ready, RES["final"] + n + 1)
                act.copy(out_tok[:, :, n * P:(n + 1) * P],
                         bank[(RES["final"] + n) % BANKS][:].rearrange("p (t d) -> p t d", t=TT)).then_inc(y_final, 1)

        @block.vector
        def _(dve):
            chained = [0]

            def link(ins):
                chained[0] += 1
                ins.then_inc(v1, 1)
                dve.wait_ge(v1, chained[0])

            def split_lo(b, it=None, step=0):
                if it is None:
                    if b >= NBLK:
                        return
                    dve.wait_ge(w_hi, b + 1)
                else:
                    dve.wait_ge(w_hi, it * step + (b + 1))
                for piece in block_parts(b, it):
                    last = dve.tensor_tensor(piece(w_low[b % RING]), piece(w_raw[b % RING]), piece(w_high[b % RING]).bitcast(F32),
                                             ALU.subtract)
                last.then_inc(w_lo, 1)

            def result(r):
                dve.wait_ge(acc_ready, r + 1)
                return bank[r % BANKS]

            def residual_lo(gen, n, g, dst):
                dve.wait_ge(xt_hi, GEN[gen] + n + 1)
                dve.scalar_tensor_tensor(dst[:, 8 + n, :], x[:, n, :], gains[:, g, n:n + 1], dst[:, n, :].bitcast(F32),
                                         ALU.mult, ALU.subtract).then_inc(xt_lo, 1)

            def norm_spread(col, n_diag):
                if n_diag > 0:
                    dve.wait_ge(bc_ready, n_diag)
                for i in range(TT):
                    last = dve.tensor_scalar(diag[:, i, :], CI(C_IDENT), r_col[:, col + i:col + i + 1], None, ALU.mult)
                last.then_inc(diag_ready, 1)

            def norm(name):
                dve.wait_ge(std_ready, SPREAD[name] + 1)
                link(dve.reciprocal(r_col[:, 0:TT], std_col[:, 0:TT]))
                norm_spread(0, SPREAD[name])
                dve.wait_ge(rstd_ready, SPREAD[name] + 1)

            def up(name, dst, gated, head=None):
                per = 2 if gated else 4
                tiles = FT - HALF if (gated and name.endswith("1")) else HALF
                def turn(it):
                    for j in range(per):
                        c = HID[name] + j
                        val = lambda n: n if it is None else it * per + n
                        rval = lambda n: n if it is None else it * BANKS + n
                        def nxt(q):
                            b = BLK[name] + q + AHEAD
                            split_lo(b) if it is None else split_lo(b, it, RING)
                        idx = j if it is None else it * per + j
                        place = dst[:, idx, :] if it is None else dst[:, bass.ds(idx, 1), :]
                        if gated:
                            r = RES[name] + 2 * j
                            dve.wait_ge(acc_ready, rval(r + 1))
                            dve.tensor_tensor(ff_z[:, j % 2, :], bank[r % BANKS][:], rstd[:], ALU.mult).then_inc(z_ready, 1)
                            nxt(2 * j)
                            dve.wait_ge(acc_ready, rval(r + 2))
                            dve.tensor_tensor(ff_u[:, j % 2, :], bank[(r + 1) % BANKS][:], rstd[:], ALU.mult).then_inc(acc_free, 2)
                            dve.wait_ge(acc_free, rval(r + 2))
                            dve.wait_ge(s_ready, val(c + 1))
                            dve.tensor_tensor(ff_t[:, j % 2, :], ff_s[:, j % 2, :], ff_u[:, j % 2, :], ALU.mult).then_inc(t_ready, 1)
                            nxt(2 * j + 1)
                        else:
                            r = RES[name] + j
                            if it is not None or j > 1:
                                nxt(j)
                            dve.wait_ge(acc_ready, rval(r + 1))
                            dve.scalar_tensor_tensor(ff_z[:, j % 2, :], bank[r % BANKS][:], 0.0, rstd[:],
                                                     ALU.max, ALU.mult).then_inc(acc_free, 1)
                        dve.wait_ge(hid_hi, val(c + 1))
                        dve.tensor_tensor(low_of(dst, place, idx, it), ff_t[:, j % 2, :], place.bitcast(F32), ALU.subtract).then_inc(hid_done, 1)
                low_of = lambda d, place, idx, it: part[2][:, idx, :] if it is None else part[2][:, bass.ds(idx, 1), :]
                if head is not None:
                    head()
                    turn(None)
                with dve.Fori(0 if head is None else 1, tiles // per) as it:
                    turn(it)

            def down(name, blocks, each):
                for n in range(DT):
                    r = RES[name] + n
                    b = BLK[name] + n * blocks + AHEAD
                    if blocks == 2:
                        split_lo(b)
                    acc = result(r)
                    each(n, acc)
                    split_lo(b + blocks - 1)

            def add_half(n, acc):
                dve.scalar_tensor_tensor(x[:, n, :], acc[:], 0.5, x[:, n, :], ALU.mult, ALU.add).then_inc(acc_free, 1)

            dve.memset(eps_col[:], EPS).then_inc(consts_made, 1)
            dve.memset(r_col[:], 0.0).then_inc(consts_made, 1)
            for n in range(DT):
                acc = result(RES["input"] + n)
                dve.tensor_copy(x[:, n, :], acc[:]).then_inc(acc_free, 1)
                if n >= 1:
                    residual_lo("f1", n - 1, 0, part[0])
                if n in (4, 6):
                    split_lo(n // 2 - 2)
            residual_lo("f1", DT - 1, 0, part[0])
            dve.wait_ge(rel_in, 16)
            dve.wait_ge(const_in, 16)
            dve.tensor_scalar(rel_rows[:, 257:384], CI(C_ONES, 127, HEADS), rel_rows[:, 256:257], None, ALU.mult).then_inc(rel_padded, 1)

            def small_products():
                dve.wait_ge(small_in, 16 * len(SMALL))
                for i in range(2):
                    last = dve.tensor_tensor(lam_pr[0:64, i:i + 1], lam_in[0:64, 2 * i:2 * i + 1],
                                             lam_in[0:64, 2 * i + 1:2 * i + 2], ALU.mult)
                last.then_inc(lam_made, 1)
                link(dve.tensor_scalar(qk_gain[:, 0:1], qk_gain[:, 0:1], -0.125, None, ALU.mult))
                link(dve.tensor_scalar(far[:], far[:], -1.0, None, ALU.mult))
                link(dve.tensor_scalar(diff_gain[:], diff_gain[:], 1.0 - LAM_INIT, None, ALU.mult))

            def lam_finish():
                dve.wait_ge(ev_hi, 2)
                link(dve.tensor_tensor(neg_lam[:], lam_ex[:, 1:2], lam_ex[:, 0:1], ALU.subtract))
                link(dve.tensor_scalar(neg_lam[:], neg_lam[:], -LAM_INIT, None, ALU.add))

            def ffn(f, hid):
                up(f"f{f}_up0", hid, True, lambda: norm(f"f{f}"))
                down(f"f{f}_dn0", 2, add_half)
                up(f"f{f}_up1", hid, True)
                if f == 1:
                    small_products()
                def one(n, acc):
                    add_half(n, acc)
                    residual_lo("m1", n, 1, part[0])
                def two(n, acc):
                    dve.scalar_tensor_tensor(y_tmp[:, n % 2, :], acc[:], 0.5, x[:, n, :], ALU.mult, ALU.add).then_inc(acc_free, 1)
                    dve.wait_ge(acc_free, RES["f2_dn1"] + n + 1)
                    dve.tensor_scalar(x[:, n, :], y_tmp[:, n % 2, :], gains[:, 3, n:n + 1], None, ALU.mult).then_inc(x_new, 1)
                    residual_lo("m2", n, 4, part[0])
                down(f"f{f}_dn1", 1, one if f == 1 else two)

            ffn(1, part[1])

            split_lo(BLK["qk"] + AHEAD)
            norm("m1")
            for g in range(4):
                dve.memset(u_pad[:, g, 0:PAD], 0.0)
            dve.memset(win[:, 0, 0:PAD], 0.0)
            dve.memset(win[:, 1, 0:PAD], 0.0).then_inc(pads_zero, 1)
            for i in range(8):
                acc = result(RES["qk"] + i)
                dve.tensor_tensor(qk_raw[:, i, :], acc[:], rstd[:], ALU.mult).then_inc(acc_free, 1)
                if i > 0:
                    split_lo(BLK["qk"] + i + AHEAD)
            def values_lo(name, col, seen):
                for i in range(TT):
                    acc = result(RES[name] + i)
                    dve.wait_ge(ev_hi, seen + i + 1)
                    dve.scalar_tensor_tensor(part[2][:, 4 + i, :], acc[:], r_col[:, col + i:col + i + 1],
                                             part[2][:, i, :].bitcast(F32), ALU.mult, ALU.subtract).then_inc(acc_free, 1)
            lam_finish()
            dve.tensor_copy(head_rows[:], const[0:48, C_HROW:C_HROW + S]).then_inc(select_made, 1)
            for i in range(3):
                split_lo(BLK["v"] + i + AHEAD)
            dve.wait_ge(h_std, 1)
            dve.reciprocal(head_rstd[:], head_std[:]).then_inc(h_rec, 1)
            dve.wait_ge(h_rows_hi, 1)
            dve.tensor_tensor(head_rows[32:32 + 2 * HEADS, :], bank[5][0:2 * HEADS, :], head_rows[0:2 * HEADS, :].bitcast(F32),
                              ALU.subtract).then_inc(h_rows_lo, 1)
            def qk_norm_lo(i):
                dve.wait_ge(qk_hi, i + 1)
                dve.tensor_tensor(part[1][:, 8 + i, :], qk_full[:, i % 2, :], part[1][:, i, :].bitcast(F32),
                                  ALU.subtract).then_inc(qk_lo, 1)
            for i in range(8):
                if i == 2:
                    split_lo(BLK["v"] + 3 + AHEAD)
                dve.wait_ge(h_bc, i + 1)
                if i >= 2:
                    dve.wait_ge(qk_lo, i - 1)
                dve.scalar_tensor_tensor(qk_full[:, i % 2, :], qk_raw[:, i, :], qk_gain[:, i // 4:i // 4 + 1],
                                         bank[6 + i % 2][:], ALU.mult, ALU.mult).then_inc(qk_full_ready, 1)
                if i > 0:
                    qk_norm_lo(i - 1)
            qk_norm_lo(7)
            values_lo("v", 0, 2)

            def a_bias(h):
                dve.wait_ge(b_mm, h + 1)
                o = bias[:, h % 2, :]
                dve.tensor_scalar(o[:, 0:256], const[:, C_ONES:C_ONES + 1].broadcast_to([P, 256]), far[:, h:h + 1], None, ALU.mult)
                dve.tensor_copy(o[0:64, 256:448], bank[2][0:64, 0:192])
                dve.tensor_copy(o[64:128, 256:512], bank[2][64:128, 0:256]).then_inc(b_done, 1)

            def a_min_of(u):
                h, q = divmod(u, TT)
                n = (q + 1) * P
                dve.wait_ge(a_score, u + 1)
                if q == 0:
                    dve.wait_ge(b_done, h + 1)
                if u >= 2:
                    dve.wait_ge(a_exp, u - 1)
                dve.tensor_tensor_reduce(out=a_s[:, u % 2, 0:n], in0=bank[4 + u % 2][:, 0:n],
                                         in1=bias[:, h % 2, S - n:S], scale=1.0, scalar=3e38, op0=ALU.add,
                                         op1=ALU.min, accum_out=a_min[:, u:u + 1]).then_inc(a_biased, 1)

            def a_normal(u):
                n = (u % TT + 1) * P
                dve.wait_ge(a_exp, u + 1)
                link(dve.reciprocal(a_rec[:, u:u + 1], a_sum[:, u:u + 1]))
                dve.tensor_scalar(a_p[:, u % 3, 0:n], a_p[:, u % 3, 0:n], a_rec[:, u:u + 1], None, ALU.mult).then_inc(a_prob, 1)

            def turned_lo(u, hi_sem, lo_sem):
                h, q = divmod(u, TT)
                dve.wait_ge(hi_sem, u + 1)
                dve.tensor_tensor(turned_unit(h, q, 1),
                                  bank[6 + u % 2][:, 0:(q + 1) * P].rearrange("p (k n) -> p k n", n=P),
                                  turned_unit(h, q, 0).bitcast(F32), ALU.subtract).then_inc(lo_sem, 1)

            def a_head_lo(h):
                r = 64 * (h % 2)
                dve.wait_ge(a_ohi, h + 1)
                dve.tensor_tensor(part[1][r:r + 64, 8 + h // 2, :], bank[h % 2][r:r + 64, :],
                                  part[1][r:r + 64, h // 2, :].bitcast(F32), ALU.subtract).then_inc(a_olo, 1)

            def pooled_lo(g):
                dve.wait_ge(pd_hi, g + 1)
                dve.tensor_tensor(part[1][:, 12 + g, :], u_pad[:, g, PAD:], part[1][:, 4 + g, :].bitcast(F32),
                                  ALU.subtract).then_inc(pd_lo, 1)

            for s_ in range(2):
                link(dve.memset(bias[0:64, s_, 448:512], BIG))
            for h in range(2):
                a_bias(h)
            for u in range(4 * HEADS + 8):
                if u < 4 * HEADS:
                    a_min_of(u)
                    if u % TT == 3 and 2 <= u // TT + 1 < HEADS:
                        a_bias(u // TT + 1)
                if 1 <= u < 4 * HEADS + 1:
                    a_normal(u - 1)
                if 3 <= u < 4 * HEADS + 3:
                    turned_lo(u - 3, a_thi, a_tlo)
                if u >= 11 and (u - 11) % TT == 0:
                    a_head_lo((u - 11) // TT)
                if u in (15, 23, 31):
                    pooled_lo((u - 15) // 8)
                if u < 4 * HEADS and u % 8 == 4:
                    split_lo(BLK["u"] + u // 8 + AHEAD)
                if u < 4 * HEADS and u % 8 == 6:
                    i = u // 8
                    dve.wait_ge(acc_ready, RES["u"] + i + 1)
                    dve.tensor_tensor(u_pad[:, i, PAD:], bank[3][:], rstd[:], ALU.mult).then_inc(acc_free, 1)
            pooled_lo(3)
            split_lo(BLK["poolw"] + AHEAD)
            for g in range(4):
                acc = result(RES["poolw"] + g)
                dve.wait_ge(ev_hi, 2 + TT + g + 1)
                dve.scalar_tensor_tensor(part[1][:, 12 + g, :], acc[:], pool_gain[:, g:g + 1], part[1][:, 4 + g, :].bitcast(F32),
                                         ALU.mult, ALU.subtract).then_inc(acc_free, 1)
            for n in range(DT):
                acc = result(RES["out1"] + n)
                dve.tensor_tensor(x[:, n, :], acc[:], x[:, n, :], ALU.add).then_inc(acc_free, 1)
                residual_lo("f2", n, 2, part[0])
                split_lo(BLK["out1"] + n + AHEAD)

            ffn(2, part[1])

            split_lo(BLK["gate"] + AHEAD)
            split_lo(BLK["dqk"] + AHEAD)
            for rows in (max_rows, sum_rows, rstd_rows):
                ins = dve.tensor_copy(rows[:], const[0:36, C_SEL4:C_SEL4 + S])
            ins.then_inc(rows_filled, 1)
            dve.wait_ge(std_ready, SPREAD["m2"] + 1)
            link(dve.reciprocal(r_col[:, 0:TT], std_col[:, 0:TT]))
            link(dve.tensor_tensor(r_col[:, 2 * TT:3 * TT], r_col[:, 0:TT], r_col[:, 0:TT], ALU.mult))
            dve.tensor_tensor(r_col[:, 3 * TT:4 * TT], bank[4][:, TT:2 * TT], r_col[:, 2 * TT:3 * TT], ALU.mult).then_inc(rcol_ready, 1)
            dve.wait_ge(std_ready, SPREAD["m2"] + 2)
            link(dve.reciprocal(r_col[:, 2 * TT:3 * TT], std_col[:, TT:2 * TT]))
            link(dve.tensor_tensor(r_col[:, TT:2 * TT], r_col[:, 0:TT], r_col[:, 2 * TT:3 * TT], ALU.mult))
            norm_spread(TT, SPREAD["m2"])
            norm_spread(0, SPREAD["m2"] + 1)
            dve.wait_ge(rstd_ready, SPREAD["m2"] + 1)

            acc = result(RES["gate"])
            i_raw, f_raw = scan[:, 3, :], scan[:, 1, :]
            dve.tensor_tensor(i_raw, acc[0:MH, :], rstd[0:MH, :], ALU.mult)
            dve.tensor_tensor(f_raw, acc[32:32 + MH, :], rstd[32:32 + MH, :], ALU.mult).then_inc(acc_free, 1)
            dve.wait_ge(acc_free, RES["gate"] + 1)
            link(dve.tensor_scalar(scan[:, 0, :], f_raw, gate_b[0:MH, 1:2], 0.0, ALU.add, ALU.min))

            logf, f_sum, a_row, m_row = scan[:, 0, :], scan[:, 1, :], scan[:, 2, :], scan[:, 0, :]

            def gate_rows(part_):
                if part_ == 0:
                    dve.wait_ge(g_ln, 1)
                    dve.wait_ge(rows_filled, 1)
                    link(dve.tensor_tensor(logf, logf, scan[:, 2, :], ALU.subtract))
                    link(dve.tensor_tensor_scan(f_sum, logf, const[0:MH, C_SEL4:C_SEL4 + S], 0.0, ALU.add, ALU.min))
                if part_ == 1:
                    link(dve.scalar_tensor_tensor(a_row, i_raw, gate_b[0:MH, 0:1], f_sum, ALU.add, ALU.subtract))
                    link(dve.tensor_tensor_scan(m_row, a_row, a_row, 0.0, ALU.max, ALU.max))
                if part_ == 2:
                    link(dve.tensor_scalar(max_rows[0:MH, :], m_row, -1.0, None, ALU.mult))
                    link(dve.scalar_tensor_tensor(max_rows[32:32 + MH, :], m_row, -1.0, max_rows[0:MH, :].bitcast(F32), ALU.mult, ALU.subtract))
                if part_ == 3:
                    link(dve.tensor_tensor(f_sum, f_sum, m_row, ALU.add))
                    link(dve.tensor_scalar(sum_rows[0:MH, :], f_sum, -1.0, None, ALU.mult))
                if part_ == 4:
                    dve.scalar_tensor_tensor(sum_rows[32:32 + MH, :], f_sum, -1.0, sum_rows[0:MH, :].bitcast(F32), ALU.mult,
                                             ALU.subtract).then_inc(g_rows, 1)

            dve.wait_ge(rope_in_sem, 16)

            def rope_in(i):
                acc = result(RES["dqk"] + i)
                dve.scalar_tensor_tensor(rope_y[:, i % 4, :], acc[:], -0.125 if i < 4 else 1.0, rstd[:], ALU.mult, ALU.mult).then_inc(acc_free, 1)

            def rope_sum(i):
                dve.wait_ge(r_perm, i + 1)
                link(dve.tensor_tensor(rope_s[:, i % 2, :], bank[6 + i % 2][:], const[:, C_SIN:C_SIN + S], ALU.mult))
                dve.wait_ge(r_cos, i + 1)
                dve.tensor_tensor(rope_c[:, i % 2, :], rope_c[:, i % 2, :], rope_s[:, i % 2, :], ALU.add).then_inc(r_full, 1)
                dve.wait_ge(r_hi, i + 1)
                dve.tensor_tensor(part[1][:, 8 + i, :], rope_c[:, i % 2, :], part[1][:, i, :].bitcast(F32), ALU.subtract).then_inc(r_lo, 1)

            for i in range(8):
                if i > 0:
                    split_lo(BLK["dqk"] + i + AHEAD)
                rope_in(i)
                if i >= 2:
                    rope_sum(i - 2)
                if i >= 2:
                    gate_rows(i - 2)
            for i in range(6, 8):
                rope_sum(i)
                split_lo(BLK["dv"] + i - 6 + AHEAD)
            split_lo(BLK["dv"] + 2 + AHEAD)
            dve.wait_ge(g_turn, 1)
            dve.tensor_copy(a_col[:].rearrange("p t h -> p (t h)"), bank[5][:, 0:TT * MH]).then_inc(g_cols, 1)
            split_lo(BLK["dv"] + 3 + AHEAD)
            link(dve.memset(d_mask[:, 0:S - P], 0.0))
            link(dve.tensor_copy(d_mask[:, S - P:], CI(C_CAUSAL)))
            values_lo("dv", TT, 2 + TT + 4)

            def d_min_of(u):
                n = (u // 2 % TT + 1) * P
                dve.wait_ge(e_score, u + 1)
                if u >= 2:
                    dve.wait_ge(e_exp, u - 1)
                dve.tensor_tensor_reduce(out=d_s[:, u % 2, 0:n], in0=bank[4 + u % 2][:, 0:n],
                                         in1=d_mask[:, S - n:S], scale=1.0, scalar=3e38, op0=ALU.add,
                                         op1=ALU.min, accum_out=d_min[:, u:u + 1]).then_inc(e_biased, 1)

            def d_combine(w):
                n = (w % TT + 1) * P
                p0, p1 = d_p[:, 2 * w % 6, 0:n], d_p[:, 2 * w % 6 + 1, 0:n]
                dve.wait_ge(e_exp, 2 * w + 2)
                link(dve.reciprocal(d_rec[:, 2 * w:2 * w + 2], d_sum[:, 2 * w:2 * w + 2]))
                link(dve.tensor_scalar(d_lam[:, w % 16:w % 16 + 1], d_rec[:, 2 * w + 1:2 * w + 2], neg_lam[:], None, ALU.mult))
                link(dve.tensor_scalar(p0, p0, d_rec[:, 2 * w:2 * w + 1], None, ALU.mult))
                dve.scalar_tensor_tensor(p0, p1, d_lam[:, w % 16:w % 16 + 1], p0, ALU.mult, ALU.add).then_inc(e_prob, 1)

            def d_copy(h):
                dve.wait_ge(e_sq, h + 1)
                dve.tensor_copy(o_diff[:, h, :], bank[h % 2][:]).then_inc(e_copied, 1)

            def convolve(i):
                o, y = c_acc[:, i, :], mqk_raw[:, i, :]
                link(dve.tensor_scalar(o, y, conv_w[:, CONV - 1, i:i + 1], conv_b[:, i:i + 1], ALU.mult, ALU.add))
                for back in range(1, CONV):
                    ins = dve.scalar_tensor_tensor(o[:, back:], y[:, 0:S - back], conv_w[:, CONV - 1 - back, i:i + 1], o[:, back:], ALU.mult, ALU.add)
                    if back < CONV - 1:
                        link(ins)
                ins.then_inc(c_sum, 1)

            dve.wait_ge(x_spilled, 16)
            for w in range(4 * DH + 8):
                if w < 4 * DH:
                    d_min_of(2 * w)
                    d_min_of(2 * w + 1)
                    if w % 2 == 0:
                        split_lo(BLK["mqk"] + w // 2 + AHEAD)
                if 1 <= w <= 4 * DH:
                    d_combine(w - 1)
                if 3 <= w < 4 * DH + 3:
                    turned_lo(w - 3, e_thi, e_tlo)
                if w >= 11 and (w - 11) % TT == 0:
                    d_copy((w - 11) // TT)
                if (w < 4 * DH - 2 and w % 2 == 1) or w == 4 * DH + 2:
                    i = min(w // 2, 7)
                    dve.wait_ge(acc_ready, RES["mqk"] + i + 1)
                    dve.tensor_tensor(x[:, i, :], bank[3][:], rstd[:], ALU.mult).then_inc(acc_free, 1)
                if w in (2, 4, 6, 8):
                    dve.wait_ge(acc_free, RES["mqk"] + w // 2)
                    convolve(w // 2 - 1)
            dve.wait_ge(e_std, 1)
            dve.reciprocal(head_rstd[:, 0:TT * DH], head_std[:, 0:TT * DH]).then_inc(e_rec, 1)
            for i in range(2):
                split_lo(BLK["mv"] + i + AHEAD)
            def rstd_rows_lo(src, hi_sem, lo_sem):
                dve.wait_ge(hi_sem, 1)
                dve.tensor_tensor(rstd_rows[32:32 + MH, :], src[0:MH, :], rstd_rows[0:MH, :].bitcast(F32), ALU.subtract).then_inc(lo_sem, 1)
            rstd_rows_lo(bank[6], e_rows_hi, e_rows_lo)
            for h in range(DH):
                dve.wait_ge(e_bc, h + 1)
                if h >= 2:
                    dve.wait_ge(e_lo, h - 1)
                dve.scalar_tensor_tensor(d_full[:, h % 2, :], o_diff[:, h, :], diff_gain[:], bank[4 + h % 2][:],
                                         ALU.mult, ALU.mult).then_inc(e_full, 1)
                dve.wait_ge(e_hi, h + 1)
                dve.tensor_tensor(part[1][:, 12 + h, :], d_full[:, h % 2, :], part[1][:, 4 + h, :].bitcast(F32),
                                  ALU.subtract).then_inc(e_lo, 1)
            for i in range(4):
                dve.wait_ge(c_hi, i + 1)
                dve.scalar_tensor_tensor(part[1][:, i, :], c_acc[:, i, :], 0.125 if i < 2 else 1.0,
                                         part[1][:, 8 + i, :].bitcast(F32), ALU.mult, ALU.subtract).then_inc(c_lo, 1)
            values_lo("mv", TT, 2 + TT + 4 + TT)

            def m_diag_of(h):
                dve.wait_ge(m_bc, 2 * h + 1)
                dve.tensor_tensor(m_dm[:], bank[2][:].rearrange("p (k n) -> p k n", n=P),
                                  const[:, C_MASKT:C_MASKT + P].rearrange("p (a n) -> p a n", a=1).broadcast_to([P, TT, P]),
                                  ALU.add).then_inc(m_diag, 1)

            def m_weigh(u):
                n = S - u % TT * P
                dve.wait_ge(m_exp, u + 1)
                dve.wait_ge(m_score, u + 1)
                dve.tensor_tensor(m_e[:, u % 3, 0:n], m_e[:, u % 3, 0:n], bank[4 + u % 2][:, 0:n], ALU.mult).then_inc(m_prod, 1)

            def m_low(u):
                k = u % TT
                dve.wait_ge(m_phi, u + 1)
                dve.tensor_tensor(part[2][:, 12 + k, k * P:], m_e[:, u % 3, 0:S - k * P], part[2][:, 8 + k, k * P:].bitcast(F32),
                                  ALU.subtract).then_inc(m_plo, 1)

            def m_head(h):
                dve.wait_ge(m_pv, TT * (h + 1))
                dve.wait_ge(m_egr, h + 1)
                if h >= 1:
                    dve.wait_ge(m_sqs, h)
                link(dve.scalar_tensor_tensor(m_den, bank[6][:], -1.0, m_eg, ALU.mult, ALU.max))
                dve.tensor_tensor(m_den, bank[6][:], m_den, ALU.max).then_inc(m_dn, 1)
                dve.wait_ge(m_nsq, h + 1)
                dve.tensor_copy(m_num[:, h, :], bank[h % 2][:]).then_inc(m_ncp, 1)

            def m_sum(h):
                dve.wait_ge(m_nsq, h + 1)
                dve.wait_ge(m_dsq, h + 1)
                dve.tensor_tensor(m_sq, m_sq, m_den, ALU.add).then_inc(m_sqs, 1)

            m_diag_of(0)
            for u in range(MH * TT + 4):
                if u + 1 < MH * TT and u % TT == TT - 1:
                    m_diag_of(u // TT + 1)
                if u < MH * TT:
                    m_weigh(u)
                if 1 <= u <= MH * TT:
                    m_low(u - 1)
                if u in (3, 6, 9):
                    split_lo(BLK["out2"] + u // 3 - 1)
                if u >= 5 and (u - 5) % TT == 0:
                    m_head((u - 5) // TT)
                if u >= 7 and (u - 7) % TT == 0:
                    m_sum((u - 7) // TT)
            dve.wait_ge(m_std, 1)
            dve.reciprocal(head_rstd[:, 0:TT * MH], head_std[:, 0:TT * MH]).then_inc(m_rec, 1)
            rstd_rows_lo(bank[7], m_rows_hi, m_rows_lo)
            for h in range(MH):
                dve.wait_ge(m_bcr, h + 1)
                if h >= 2:
                    dve.wait_ge(m_lo, h - 1)
                link(dve.scalar_tensor_tensor(m_full[:, h % 2, :], m_num[:, h, :], mlstm_gain[:, h:h + 1],
                                              bank[4 + h % 2][:], ALU.mult, ALU.mult))
                dve.wait_ge(mo_sig, h + 1)
                dve.tensor_tensor(m_full[:, h % 2, :], m_full[:, h % 2, :], sig[:, h, :], ALU.mult).then_inc(m_norm, 1)
                dve.wait_ge(m_hi, h + 1)
                dve.tensor_tensor(part[0][:, 8 + h, :], m_full[:, h % 2, :], part[0][:, h, :].bitcast(F32), ALU.subtract).then_inc(m_lo, 1)

            for n in range(DT):
                if n > 0:
                    split_lo(BLK["out2"] + n + AHEAD)
                acc = result(RES["out2"] + n)
                dve.tensor_copy(mixed[:, n, :], acc[:]).then_inc(acc_free, 1)
            split_lo(BLK["f3_up0"] + 2)
            norm("post1")
            for n in range(DT):
                link(dve.scalar_tensor_tensor(mixed[:, n, :], mixed[:, n, :], gains[:, 5, n:n + 1], rstd[:], ALU.mult, ALU.mult))
                if n == 0:
                    dve.wait_ge(x_unit, DT)
                dve.tensor_tensor(x[:, n, :], x[:, n, :], mixed[:, n, :], ALU.add).then_inc(x_new, 1)
                if n >= 1:
                    residual_lo("f3", n - 1, 6, part[1])
            residual_lo("f3", DT - 1, 6, part[1])

            split_lo(BLK["f3_up0"] + 3)
            up("f3_up0", part[0], False, lambda: norm("f3"))
            def first(n, acc):
                if n == 0:
                    dve.wait_ge(x_spilled, 32)
                dve.tensor_copy(x[:, n, :], acc[:]).then_inc(acc_free, 1)
            down("f3_dn0", 2, first)
            up("f3_up1", part[0], False)
            down("f3_dn1", 2, lambda n, acc: dve.tensor_tensor(x[:, n, :], acc[:], x[:, n, :], ALU.add).then_inc(acc_free, 1))
            norm("post2")
            dve.wait_ge(x_returned, 32)
            for n in range(DT):
                link(dve.scalar_tensor_tensor(x[:, n, :], x[:, n, :], gains[:, 7, n:n + 1], rstd[:], ALU.mult, ALU.mult))
                dve.tensor_tensor(x[:, n, :], x[:, n, :], x_back[:, n, :], ALU.add).then_inc(x_new, 1)

        @block.gpsimd
        def _(pool):
            stepped = [0]

            def link(ins):
                stepped[0] += 1
                ins.then_inc(pool_step, 1)
                pool.wait_ge(pool_step, stepped[0])

            def add_square(i, which, first):
                pool.wait_ge(sq_ready, i + 1)
                if first:
                    pool.tensor_copy(sq_sum[:, which, :], sq[:, i % 2, :]).then_inc(sq_added, 1)
                else:
                    pool.wait_ge(sq_added, i)
                    pool.tensor_tensor(sq_sum[:, which, :], sq_sum[:, which, :], sq[:, i % 2, :], ALU.add).then_inc(sq_added, 1)

            def sum_squares(name):
                if NORM[name]:
                    pool.wait_ge(stat_ready, NORM[name])
                for n in range(DT):
                    add_square(SQ[name] + n, 0, n == 0)

            sum_squares("f1")
            sum_squares("m1")
            for g in range(4):
                pool.wait_ge(acc_free, RES["u"] + g + 1)
                pool.wait_ge(pads_zero, 1)
                src = u_pad[:, g, :]
                for k in range(g + 1):
                    dst = win[:, k % 2, :]
                    link(pool.tensor_tensor(dst[:, PAD:], src[:, PAD:], src[:, PAD - 2 ** k:PAD - 2 ** k + S], ALU.add))
                    src = dst
                link(pool.tensor_tensor(src[:, PAD:2 * PAD], src[:, PAD:2 * PAD], const[:, C_POOL + 16 * g:C_POOL + 16 * (g + 1)], ALU.mult))
                link(pool.tensor_scalar(src[:, PAD:], src[:, PAD:], 0.5 ** (g + 1), None, ALU.mult))
                pool.tensor_tensor(u_pad[:, g, PAD:], src[:, PAD:], u_pad[:, g, PAD:], ALU.subtract).then_inc(pool_done, 1)
                pool.wait_ge(pool_done, g + 1)
            sum_squares("f2")
            pool.wait_ge(stat_ready, NORM["m2"])
            for n in range(DT):
                for which in range(2):
                    add_square(SQ["m2"] + 2 * n + which, which, n == 0)
            pool.wait_ge(rope_in_sem, 16)
            for i in range(8):
                pool.wait_ge(acc_free, RES["dqk"] + i + 1)
                if i >= 2:
                    pool.wait_ge(r_lo, i - 1)
                pool.tensor_tensor(rope_c[:, i % 2, :], rope_y[:, i % 4, :], const[:, C_COS:C_COS + S], ALU.mult).then_inc(r_cos, 1)
            pool.wait_ge(rstd_ready, SPREAD["m2"] + 2)
            pool.wait_ge(x_returned, 16)
            pool.wait_ge(stat_ready, NORM["post1"])
            for n in range(DT):
                pool.tensor_tensor(x[:, n, :], x[:, n, :], rstd_fin[:], ALU.mult).then_inc(x_unit, 1)
                add_square(SQ["post1"] + n, 0, n == 0)
            sum_squares("f3")
            sum_squares("post2")

        @block.tensor
        def _(pe):
            def parts(region, k):
                return part[region][:, k, :], part[region][:, 8 + k, :]

            def finish(mm):
                mm.then_inc(acc_ready, 1)

            def norm_stat(name, sums=1):
                pe.wait_ge(sq_added, SQ[name] + DT * sums)
                if name == "f1":
                    pe.wait_ge(const_in, 16)
                for s_ in range(sums):
                    for i in range(TT):
                        mm = pe.matmul(bank[4][:, s_ * TT + i:s_ * TT + i + 1], sq_sum[:, s_, i * P:(i + 1) * P],
                                       const[:, C_ONES:C_ONES + 1], start=True, stop=True)
                mm.then_inc(stat_ready, 1)

            def norm_spread(name, extra=0):
                n = SPREAD[name] + extra
                pe.wait_ge(diag_ready, n + 1)
                if n > 0:
                    pe.wait_ge(rstd_ready, n)
                for i in range(TT):
                    mm = pe.matmul(bank[5][:, i * P:(i + 1) * P], CI(C_ONES), diag[:, i, :], start=True, stop=True)
                mm.then_inc(bc_ready, 1)

            def tile(b, r, src, k0=0, nk=8, skip=0, start=True, stop=True, need=None, m=P):
                hi, lo = w_tiles(b)
                for k in range(nk):
                    if need is not None:
                        need(k0 + k)
                    x_hi, x_lo = src(k0 + k)
                    mm = split3(pe, bank[r % BANKS][0:m, :], hi[:, skip + k, 0:m], lo[:, skip + k, 0:m], x_hi, x_lo,
                                start and k == 0, stop and k == nk - 1, k == 0)
                return mm

            def side_by_side(name, tiles, k, src, need=None, very_first=False):
                if need is not None:
                    need(k)
                x_hi, x_lo = src(k)
                for j in range(tiles):
                    b, r = BLK[name] + j, RES[name] + j
                    if k == 0:
                        block_ready(pe, b)
                        free_bank(pe, r)
                    hi, lo = w_tiles(b)
                    new = (j == 0 and not very_first) if k == 0 else (k == DT - 1 and j > 0)
                    mm = split3(pe, bank[r % BANKS][:], hi[:, k, :], lo[:, k, :], x_hi, x_lo, k == 0, k == DT - 1, new)
                    if k == DT - 1:
                        finish(mm)

            def up(name, src, gated, gen=None, after=()):
                tiles = 2 * (FT - HALF if name.endswith("1") else HALF) if gated else HALF
                def turn(it):
                    side = 0
                    if it is None:
                        side = 1 if gated else 3
                        for k in range(DT):
                            side_by_side(name, side, k, src, lambda k: pe.wait_ge(xt_lo, GEN[gen] + k + 1), BLK[name] == 0)
                        after[0]()
                    for q in range(side, RING):
                        b, r = BLK[name] + q, RES[name] + q
                        block_ready(pe, b, it, RING)
                        free_bank(pe, r, it, RING)
                        finish(tile(b, r, src, need=(lambda k: after[1]() if k == 4 else None) if it is None and q == side else None))
                if gen is not None:
                    turn(None)
                with pe.Fori(0 if gen is None else 1, tiles // RING) as it:
                    turn(it)

            def down(name, blocks, hid, h0, tiles):
                def turn(it):
                    for j in range(BANKS):
                        r = RES[name] + j
                        free_bank(pe, r, it, BANKS)
                        for c in range(blocks):
                            b = BLK[name] + j * blocks + c
                            block_ready(pe, b, it, BANKS * blocks)
                            def need(k):
                                if k == 0:
                                    pe.wait_ge(hid_done, h0 + tiles - 2)
                                if k == tiles - 2:
                                    pe.wait_ge(hid_done, h0 + tiles)
                            nk = min(8, tiles - 8 * c)
                            mm = tile(b, r, lambda k: (part[hid][:, k, :], part[2][:, k, :]), 8 * c, nk, 8 - nk, c == 0, c == blocks - 1, need=need)
                        finish(mm)
                with pe.Fori(0, DT // BANKS) as it:
                    turn(it)

            def columns(name, n, src, after=None, need=None, first=0, within=None):
                for i in range(first, n):
                    block_ready(pe, BLK[name] + i)
                    free_bank(pe, RES[name] + i)
                    finish(tile(BLK[name] + i, RES[name] + i, src, need=need if i == 0 else within if i == 1 else None))
                    if after is not None:
                        after(i)

            def values(name, region, after=None):
                for j in range(4):
                    b = BLK[name] + j
                    block_ready(pe, b)
                    hi, lo = w_tiles(b, S)
                    for kk in range(2):
                        k = 2 * j + kk
                        x_hi, x_lo = parts(region, k)
                        for i in range(TT):
                            if k == 0:
                                free_bank(pe, RES[name] + i)
                            mm = split3(pe, bank[(RES[name] + i) % BANKS][:], x_hi[:, i * P:(i + 1) * P], x_lo[:, i * P:(i + 1) * P],
                                        hi[:, kk, :], lo[:, kk, :], k == 0, k == DT - 1, kk == 0 and i == 0)
                            if k == DT - 1:
                                finish(mm)
                        if after is not None:
                            after(k)

            pe.wait_ge(ident_in, 16)
            for n in range(DT):
                if n % 2 == 0:
                    pe.wait_ge(x_in[n // 2], 16)
                free_bank(pe, RES["input"] + n)
                for i in range(TT):
                    mm = pe.transpose(bank[(RES["input"] + n) % BANKS][:, i * P:(i + 1) * P],
                                      x_tok[:, i, n * P:(n + 1) * P], CI(C_IDENT))
                finish(mm)
            def lam_sum():
                pe.wait_ge(lam_made, 1)
                pe.matmul(bank[5][:, 0:2], const[0:64, C_ONES:C_ONES + P], lam_pr[0:64, :], start=True, stop=True).then_inc(lam_summed, 1)

            def norm_steps(name):
                return (lambda: norm_stat(name), lambda: norm_spread(name))

            def ffn(f, region, hid):
                src = lambda k: parts(region, k)
                up(f"f{f}_up0", src, True, f"f{f}", norm_steps(f"f{f}"))
                down(f"f{f}_dn0", 2, hid, HID[f"f{f}_up0"], HALF)
                up(f"f{f}_up1", src, True)
                down(f"f{f}_dn1", 1, hid, HID[f"f{f}_up1"], FT - HALF)

            ffn(1, 0, 1)

            def head_stat(i):
                pe.wait_ge(y_sq, i + 1)
                for t_ in range(TT):
                    c = 2 * HEADS * t_ + 2 * i
                    mm = pe.matmul(bank[4][:, c:c + 2], head_sq[:, i % 2, t_ * P:(t_ + 1) * P], const[:, C_HSUM:C_HSUM + 2],
                                   start=True, stop=True)
                mm.then_inc(h_stat, 1)

            def turn_rstd(dst, n, ready, done):
                pe.wait_ge(ready, 1)
                for t_ in range(TT):
                    mm = pe.transpose(dst[0:n, t_ * P:(t_ + 1) * P], head_rstd[:, n * t_:n * (t_ + 1)], CI(C_IDENT))
                mm.then_inc(done, 1)

            def after_qk(i):
                if i == 0:
                    norm_stat("m1")
                if i >= 3:
                    head_stat(i - 3)
            lam_sum()
            x_in1 = lambda k: parts(0, k)
            columns("qk", 8, x_in1, after_qk, need=lambda k: pe.wait_ge(xt_lo, GEN["m1"] + k + 1),
                    within=lambda k: norm_spread("m1") if k == 4 else None)
            def after_v(k):
                if k == 1:
                    for i in range(5, 8):
                        head_stat(i)
                if k == 3:
                    turn_rstd(bank[5], 2 * HEADS, h_rec, h_turned)
                    pe.wait_ge(h_rows_lo, 1)
                for i in ((), (), (), (0, 1), (2, 3), (4,), (5, 6), (7,))[k]:
                    head_spread(i)
            def head_spread(i):
                if i >= 2:
                    pe.wait_ge(qk_full_ready, i - 1)
                pe.matmul(bank[6 + i % 2][:], head_select[:, P * i:P * (i + 1)], head_rows[:], start=True, stop=True).then_inc(h_bc, 1)
            values("v", 0, after_v)

            def side_steps(name, first, last, src):
                for step in range(first, last):
                    i, k = divmod(step, DT)
                    b = BLK[name] + i
                    hi, lo = w_tiles(b)
                    if k == 0:
                        block_ready(pe, b)
                        pe.wait_ge(acc_free, RES[name] + i)
                    x_hi, x_lo = src(k)
                    mm = split3(pe, bank[3][:], hi[:, k, :], lo[:, k, :], x_hi, x_lo, k == 0, k == DT - 1, k == 0)
                    if k == DT - 1:
                        finish(mm)

            def a_bias(h):
                pe.wait_ge(toep_in[h % 2], 16 * (h // 2 + 1))
                if h >= 1:
                    pe.wait_ge(b_done, h)
                pe.matmul(bank[2][:, 0:P], toep[:, h % 2, 1, :], CI(C_FLIP), start=True, stop=True)
                pe.matmul(bank[2][:, P:2 * P], toep[:, h % 2, 0, :], CI(C_FLIP), start=True, stop=True).then_inc(b_mm, 1)

            def a_scores(u):
                h, q = divmod(u, TT)
                n, r = (q + 1) * P, 64 * (h % 2)
                if u >= 2:
                    pe.wait_ge(a_biased, u - 1)
                rows_ = slice(r, r + 64)
                qt, kt = h // 2, 4 + h // 2
                split3(pe, bank[4 + u % 2][:, 0:n], part[1][rows_, qt, q * P:(q + 1) * P], part[1][rows_, 8 + qt, q * P:(q + 1) * P],
                       part[1][rows_, kt, 0:n], part[1][rows_, 8 + kt, 0:n], True, True).then_inc(a_score, 1)

            def turn_probs(u, probs, ready, lo_sem, done):
                h, q = divmod(u, TT)
                pe.wait_ge(ready, u + 1)
                if u >= 2:
                    pe.wait_ge(lo_sem, u - 1)
                for k in range(q + 1):
                    place = k if h % 2 == 0 else q - k
                    mm = pe.transpose(bank[6 + u % 2][:, place * P:(place + 1) * P], probs[:, k * P:(k + 1) * P], CI(C_IDENT))
                mm.then_inc(done, 1)

            def weigh_values(h, k, col, lo_sem, done, copied):
                if k == 0:
                    pe.wait_ge(lo_sem, TT * (h + 1))
                    if h >= 2:
                        pe.wait_ge(copied, h - 1)
                mm = split3(pe, bank[h % 2][:, k * P:], part[2][:, k, col:col + P], part[2][:, 4 + k, col:col + P],
                            turned_keys(h, k, 0), turned_keys(h, k, 1), k == 0, k == TT - 1)
                if k == TT - 1:
                    mm.then_inc(done, 1)

            pe.wait_ge(acc_free, RES["v"] + TT)
            for h in range(2):
                a_bias(h)
            pe.wait_ge(qk_lo, 8)
            for u in range(4 * HEADS + 8):
                if u < 4 * HEADS:
                    a_scores(u)
                    first = u // 8 * 8 + (0, 2, 4, 5, 6, 7, 8, 8, 8)[u % 8]
                    last = u // 8 * 8 + (2, 4, 5, 6, 7, 8, 8, 8)[u % 8]
                    side_steps("u", first, last, x_in1)
                    if u % TT == 1 and 2 <= u // TT + 1 < HEADS:
                        a_bias(u // TT + 1)
                if 7 <= u < 4 * HEADS + 7:
                    h, k = divmod(u - 7, TT)
                    weigh_values(h, k, P * (h // 2), a_tlo, a_out, a_olo)
                if 2 <= u < 4 * HEADS + 2:
                    turn_probs(u - 2, a_p[:, (u - 2) % 3, :], a_prob, a_tlo, a_turned)
            pe.wait_ge(a_olo, HEADS)
            block_ready(pe, BLK["poolw"])
            hi, lo = w_tiles(BLK["poolw"])
            for g in range(4):
                free_bank(pe, RES["poolw"] + g)
                pe.wait_ge(pd_lo, g + 1)
                finish(split3(pe, bank[(RES["poolw"] + g) % BANKS][:], hi[:, g, :], lo[:, g, :], part[1][:, 4 + g, :],
                              part[1][:, 12 + g, :], True, True, g == 0))
            def mixed_in(k):
                if k >= 4:
                    pe.wait_ge(acc_free, RES["poolw"] + k - 3)
            columns("out1", 8, lambda k: parts(1, k), need=mixed_in)

            ffn(2, 0, 1)

            x_in2 = lambda k: parts(0, k)
            block_ready(pe, BLK["gate"])
            free_bank(pe, RES["gate"])
            finish(tile(BLK["gate"], RES["gate"], x_in2, need=lambda k: pe.wait_ge(xt_lo, GEN["m2"] + k + 1), m=36))
            norm_stat("m2", 2)

            def swap_halves(i):
                pe.wait_ge(acc_free, RES["dqk"] + i + 1)
                if i >= 2:
                    pe.wait_ge(r_full, i - 1)
                pe.matmul(bank[6 + i % 2][:], CI(C_SWAP), rope_y[:, i % 4, :], start=True, stop=True).then_inc(r_perm, 1)

            def after_dqk(i):
                if i >= 3:
                    swap_halves(i - 3)
            columns("dqk", 8, x_in2, after_dqk, need=lambda k: norm_spread("m2") if k == 6 else None,
                    within=lambda k: norm_spread("m2", 1) if k == 3 else None)
            def after_dv(j):
                for i in ((5, ), (6,), (7,), (), (), (), (), ())[j]:
                    swap_halves(i)
                if j == 2:
                    pe.wait_ge(g_rows, 1)
                    pe.wait_ge(rstd_ready, SPREAD["m2"] + 2)
                    for i in range(TT):
                        mm = pe.transpose(bank[5][:, i * MH:(i + 1) * MH], scan[:, 2, i * P:(i + 1) * P], const[0:MH, C_IDENT:C_IDENT + MH])
                    mm.then_inc(g_turn, 1)
            values("dv", 0, after_dv)

            def d_scores(u):
                w, c = divmod(u, 2)
                h, q = divmod(w, TT)
                n, rows_ = (q + 1) * P, slice(64 * c, 64 * c + 64)
                if u >= 2:
                    pe.wait_ge(e_biased, u - 1)
                split3(pe, bank[4 + u % 2][:, 0:n], part[1][rows_, h, q * P:(q + 1) * P], part[1][rows_, 8 + h, q * P:(q + 1) * P],
                       part[1][rows_, 4 + h, 0:n], part[1][rows_, 12 + h, 0:n], True, True).then_inc(e_score, 1)

            def head_sums(dst, h, squares):
                for t_ in range(TT):
                    mm = pe.matmul(dst[:, MH * t_ + h:MH * t_ + h + 1], squares[:, t_ * P:(t_ + 1) * P], const[:, C_ONES:C_ONES + 1],
                                   start=True, stop=True)
                return mm

            def spread4(dst, h, rows):
                return pe.matmul(dst[:], select4[:, P * h:P * (h + 1)], rows[:], start=True, stop=True)

            def d_stat(h):
                pe.wait_ge(e_sq, h + 1)
                head_sums(bank[2], h, sq[:, h % 2, :]).then_inc(e_stat, 1)

            pe.wait_ge(r_lo, 8)
            pe.wait_ge(g_cols, 1)
            for w in range(4 * DH + 8):
                if w < 4 * DH:
                    d_scores(2 * w)
                    d_scores(2 * w + 1)
                    if w == 0:
                        pe.wait_ge(acc_free, RES["dv"] + TT)
                    if w % 2 == 1 and w < 4 * DH - 2:
                        side_steps("mqk", 4 * w, 4 * w + 4, x_in2)
                if 7 <= w < 4 * DH + 7:
                    h, k = divmod(w - 7, TT)
                    weigh_values(h, k, P * h, e_tlo, e_out, e_copied)
                if 2 <= w < 4 * DH + 2:
                    turn_probs(w - 2, d_p[:, 2 * (w - 2) % 6, :], e_prob, e_tlo, e_turned)
                if w < 4 * DH - 2 and w % 2 == 0:
                    side_steps("mqk", 4 * w, 4 * w + 4, x_in2)
                if w in (4 * DH, 4 * DH + 1):
                    side_steps("mqk", 4 * (w - 2), 4 * (w - 2) + 4, x_in2)
                if w >= 12 and (w - 12) % TT == 0:
                    d_stat((w - 12) // TT)
            d_stat(DH - 1)
            pe.wait_ge(e_copied, DH)
            pe.wait_ge(e_std, 1)

            def after_mv(k):
                if k == 1:
                    turn_rstd(bank[6], DH, e_rec, e_rturned)
                if k == 3:
                    pe.wait_ge(select4_made, 1)
                    pe.wait_ge(e_rows_lo, 1)
                for h in ((), (), (), (0, 1), (2,), (3,), (), ())[k]:
                    if h >= 2:
                        pe.wait_ge(e_full, h - 1)
                    spread4(bank[4 + h % 2], h, rstd_rows).then_inc(e_bc, 1)
            values("mv", 0, after_mv)

            def m_spread_max(h):
                if h >= 1:
                    pe.wait_ge(m_exp, TT * h)
                spread4(bank[2], h, max_rows).then_inc(m_bc, 1)

            def m_spread_sum(h):
                if h >= 1:
                    pe.wait_ge(m_egr, h)
                spread4(bank[3], h, sum_rows).then_inc(m_bc, 1)

            def m_scores(u):
                h, k = divmod(u, TT)
                rows_ = slice(64 * (h % 2), 64 * (h % 2) + 64)
                qt, kt = h // 2, 2 + h // 2
                if u >= 2:
                    pe.wait_ge(m_prod, u - 1)
                split3(pe, bank[4 + u % 2][:, 0:S - k * P], part[1][rows_, 8 + kt, k * P:(k + 1) * P], part[1][rows_, kt, k * P:(k + 1) * P],
                       part[1][rows_, 8 + qt, k * P:], part[1][rows_, qt, k * P:], True, True).then_inc(m_score, 1)

            def m_values(u):
                h, k = divmod(u, TT)
                pe.wait_ge(m_plo, u + 1)
                if k == 0 and h >= 2:
                    pe.wait_ge(m_ncp, h - 1)
                split3(pe, bank[h % 2][:, k * P:], part[2][:, k, P * h:P * (h + 1)], part[2][:, 4 + k, P * h:P * (h + 1)],
                       part[2][:, 8 + k, k * P:], part[2][:, 12 + k, k * P:], k == 0, k == TT - 1)
                if k == 0 and h >= 1:
                    pe.wait_ge(m_dn, h)
                pe.matmul(bank[6][:, k * P:], ones_r[:], part[2][:, 8 + k, k * P:], start=(k == 0), stop=False)
                pe.matmul(bank[6][:, k * P:], ones_r[:], part[2][:, 12 + k, k * P:], start=False, stop=(k == TT - 1)).then_inc(m_pv, 1)

            def m_stat_of(h):
                pe.wait_ge(m_sqs, h + 1)
                head_sums(bank[7], h, m_sq).then_inc(m_stat, 1)

            pe.wait_ge(acc_free, RES["mv"] + TT)
            pe.wait_ge(c_lo, 4)
            pe.wait_ge(e_full, DH)
            m_spread_max(0)
            for u in range(MH * TT + 2):
                if u < MH * TT:
                    m_scores(u)
                    if u % TT == 2:
                        m_spread_sum(u // TT)
                    if u % TT == 3 and u // TT + 1 < MH:
                        m_spread_max(u // TT + 1)
                if 2 <= u < MH * TT + 2:
                    m_values(u - 2)
                if u >= 8 and (u - 8) % TT == 0:
                    m_stat_of((u - 8) // TT)
            m_stat_of(MH - 1)
            def mix2(k):
                return (part[1][:, 4 + k, :], part[1][:, 12 + k, :]) if k < 4 else (part[0][:, k - 4, :], part[0][:, 4 + k, :])
            def mix2_in(k):
                if k < 4:
                    pe.wait_ge(e_lo, k + 1)
                else:
                    pe.wait_ge(m_lo, k - 3)
            def m_rstd_spread(h):
                if h >= 2:
                    pe.wait_ge(m_norm, h - 1)
                spread4(bank[4 + h % 2], h, rstd_rows).then_inc(m_bcr, 1)

            pe.wait_ge(m_ncp, MH)
            pe.wait_ge(m_egr, MH)
            side_by_side("out2", 3, 0, mix2, mix2_in)
            turn_rstd(bank[7], MH, m_rec, m_rturned)
            side_by_side("out2", 3, 1, mix2, mix2_in)
            pe.wait_ge(m_rows_lo, 1)
            for h in range(MH):
                m_rstd_spread(h)
                if h in (1, 2):
                    side_by_side("out2", 3, h + 1, mix2, mix2_in)
            for k in range(4, DT):
                side_by_side("out2", 3, k, mix2, mix2_in)
            columns("out2", 8, mix2, first=3)
            norm_stat("post1")
            norm_spread("post1")

            src = lambda k: parts(1, k)
            up("f3_up0", src, False, "f3", norm_steps("f3"))
            down("f3_dn0", 2, 0, HID["f3_up0"], HALF)
            up("f3_up1", src, False)
            down("f3_dn1", 2, 0, HID["f3_up1"], HALF)
            norm_stat("post2")
            norm_spread("post2")
            for n in range(DT):
                free_bank(pe, RES["final"] + n) if n < 4 else pe.wait_ge(y_final, n - 3)
                pe.wait_ge(x_new, 2 * DT + n + 1)
                for i in range(TT):
                    mm = pe.transpose(bank[(RES["final"] + n) % BANKS][:, i * P:(i + 1) * P], x[:, n, i * P:(i + 1) * P], CI(C_IDENT))
                finish(mm)


_INS = ["x", "ffn1_norm", "ffn1_w_gate", "ffn1_w_up", "ffn1_w_down", "mix_norm", "w_in", "q_norm", "k_norm", "rel_bias",
        "pool_w", "pool_scale", "w_out", "ffn2_norm", "ffn2_w_gate", "ffn2_w_up", "ffn2_w_down", "final_norm",
        "norm_mix_pre_2", "w_in_2", "conv_w_2", "conv_b_2", "b_igate_2", "b_fgate_2", "lambda_q1_2", "lambda_k1_2",
        "lambda_q2_2", "lambda_k2_2", "diff_norm_2", "mlstm_norm_2", "w_out_2", "norm_mix_post_2", "norm_mlp_pre_2",
        "w_up_2", "w_down_2", "norm_mlp_post_2"]


def kernel(**inputs):
    import concourse.bacc as _bacc
    from concourse.bass_utils import run_bass_kernel_spmd as _run

    nc = _bacc.Bacc("TRN2", target_bir_lowering=False, num_devices=1)
    arrays, t = {}, {}
    for name in _INS + ["const"]:
        a = shape_constants() if name == "const" else np.ascontiguousarray(inputs[name])
        arrays[f"in_{name}"] = a
        t[name] = nc.dram_tensor(f"in_{name}", a.shape, mybir.dt.from_np(a.dtype), kind="ExternalInput").ap()
    t["out"] = nc.dram_tensor("out_0", (1, S, D), F32, kind="ExternalOutput").ap()
    build(nc, t)
    r = _run(nc, [arrays], core_ids=[0])
    return r.results[0]["out_0"]
```
